# Optimizing a Trainium2 kernel written in Bass

```python
import jax
import jax.numpy as jnp
from jax import lax
import numpy as np
import math
import jax, jax.numpy as jnp

D_MODEL = 1024
BATCH = 1
SEQ = 512
DEPTH = 2

DN_HEADS = 4
DN_DK = 128
DN_DV = 128
DN_CONV = 4
DN_CHUNK = 64
DN_WIDTH = DN_HEADS * DN_DV
POOL_WINDOWS = (2, 4, 8, 16)
POOL_GROUP = 128
POOL_WIDTH = POOL_GROUP * len(POOL_WINDOWS)
SA_HEADS = 4
SA_HEAD_DIM = 128
SA_WIDTH = SA_HEADS * SA_HEAD_DIM
IDX_HEADS = 4
IDX_DIM = 64
TOPK_MAX = 256
Q_BLOCK = 128
ROPE_THETA = 10000.0
NORM_EPS = 1e-6
N_BRANCH = 3
BRANCH_WIDTH = 512
SPLIT_SIZES = (DN_WIDTH, DN_WIDTH, DN_WIDTH, DN_WIDTH, DN_HEADS, DN_HEADS,
               POOL_WIDTH, POOL_WIDTH,
               SA_WIDTH, SA_WIDTH, SA_WIDTH, SA_WIDTH, IDX_HEADS * IDX_DIM, IDX_DIM, IDX_HEADS,
               N_BRANCH * D_MODEL)
IN_WIDTH = sum(SPLIT_SIZES)


def rms_norm(x, g):
    x32 = x.astype(jnp.float32)
    y = x32 * lax.rsqrt(jnp.mean(x32 * x32, axis=-1, keepdims=True) + NORM_EPS)
    return y.astype(x.dtype) * g

def l2_normalize(x):
    x32 = x.astype(jnp.float32)
    return x32 * lax.rsqrt(jnp.sum(x32 * x32, axis=-1, keepdims=True) + NORM_EPS)

def rope_tables(seq_len, dim):
    inv_freq = ROPE_THETA ** (-jnp.arange(0, dim, 2, dtype=jnp.float32) / dim)
    ang = jnp.arange(seq_len, dtype=jnp.float32)[:, None] * inv_freq[None, :]
    return jnp.cos(ang), jnp.sin(ang)

def apply_rope(x, cos, sin):
    x32 = x.astype(jnp.float32)
    x1, x2 = jnp.split(x32, 2, axis=-1)
    c = cos[None, :, None, :]
    s = sin[None, :, None, :]
    return jnp.concatenate([x1 * c - x2 * s, x2 * c + x1 * s], axis=-1).astype(x.dtype)

def split_columns(proj):
    parts = []
    start = 0
    for size in SPLIT_SIZES:
        parts.append(proj[..., start:start + size])
        start += size
    return parts

def causal_depthwise_conv(x, w):
    k = w.shape[0]
    return lax.conv_general_dilated(x, w[:, None, :], window_strides=(1,), padding=((k - 1, 0),),
                                    dimension_numbers=('NWC', 'WIO', 'NWC'),
                                    feature_group_count=x.shape[-1])

def chunk_gated_delta_rule(q, k, v, beta, g):
    b, t, h, dk = q.shape
    dv = v.shape[-1]
    n = t // DN_CHUNK
    c = DN_CHUNK
    to_chunks4 = lambda a: a.reshape(b, n, c, h, a.shape[-1]).transpose(1, 0, 3, 2, 4)
    to_chunks3 = lambda a: a.reshape(b, n, c, h).transpose(1, 0, 3, 2)
    qc = to_chunks4(q * (dk ** -0.5))
    kc = to_chunks4(k)
    vc = to_chunks4(v)
    bc = to_chunks3(beta)
    gc = jnp.cumsum(to_chunks3(g), axis=-1)
    tril = jnp.tril(jnp.ones((c, c), dtype=bool))
    strict = jnp.tril(jnp.ones((c, c), dtype=bool), -1)
    decay = jnp.exp(jnp.where(tril, gc[..., :, None] - gc[..., None, :], -jnp.inf))
    k_beta = kc * bc[..., None]
    v_beta = vc * bc[..., None]
    lmat = jnp.where(strict, jnp.einsum('nbhid,nbhjd->nbhij', k_beta, kc) * decay, 0.0)
    eye = jnp.eye(c, dtype=jnp.float32)
    tmat = lax.linalg.triangular_solve(eye + lmat, jnp.broadcast_to(eye, lmat.shape),
                                       left_side=True, lower=True, unit_diagonal=True)
    u = jnp.einsum('nbhij,nbhjd->nbhid', tmat, v_beta)
    w = jnp.einsum('nbhij,nbhjd->nbhid', tmat, k_beta * jnp.exp(gc)[..., None])
    attn_intra = jnp.where(tril, jnp.einsum('nbhid,nbhjd->nbhij', qc, kc) * decay, 0.0)

    def step(state, xs):
        q_i, k_i, u_i, w_i, g_i, a_i = xs
        v_new = u_i - jnp.einsum('bhck,bhkv->bhcv', w_i, state)
        o = (jnp.einsum('bhck,bhkv->bhcv', q_i * jnp.exp(g_i)[..., None], state)
             + jnp.einsum('bhij,bhjv->bhiv', a_i, v_new))
        g_last = g_i[..., -1:]
        state = (state * jnp.exp(g_last)[..., None]
                 + jnp.einsum('bhck,bhcv->bhkv', k_i * jnp.exp(g_last - g_i)[..., None], v_new))
        return state, o

    state0 = jnp.zeros((b, h, dk, dv), dtype=jnp.float32)
    _, o = lax.scan(step, state0, (qc, kc, u, w, gc, attn_intra))
    return o.transpose(1, 0, 3, 2, 4).reshape(b, t, h, dv)

def deltanet_branch(qa, ka, va, za, ba, aa, conv_w, a_log, dt_bias, o_norm):
    b, t, _ = qa.shape
    qkv = jax.nn.silu(causal_depthwise_conv(jnp.concatenate([qa, ka, va], axis=-1), conv_w))
    q, k, v = jnp.split(qkv, 3, axis=-1)
    q = l2_normalize(q.reshape(b, t, DN_HEADS, DN_DK))
    k = l2_normalize(k.reshape(b, t, DN_HEADS, DN_DK))
    v = v.reshape(b, t, DN_HEADS, DN_DV).astype(jnp.float32)
    beta = jax.nn.sigmoid(ba.astype(jnp.float32))
    g = -jnp.exp(a_log.astype(jnp.float32)) * jax.nn.softplus(aa.astype(jnp.float32) + dt_bias.astype(jnp.float32))
    o = chunk_gated_delta_rule(q, k, v, beta, g)
    o = rms_norm(o, o_norm) * jax.nn.silu(za.reshape(b, t, DN_HEADS, DN_DV))
    return o.reshape(b, t, DN_WIDTH)

def pooling_branch(u, z, pool_w, pool_scale):
    b, t, _ = u.shape
    u32 = u.astype(jnp.float32)
    cs = jnp.cumsum(u32, axis=1)
    pos_count = jnp.arange(1, t + 1, dtype=jnp.int32)
    groups = []
    for gi, win in enumerate(POOL_WINDOWS):
        sl = slice(gi * POOL_GROUP, (gi + 1) * POOL_GROUP)
        cs_g = cs[..., sl]
        lagged = jnp.pad(cs_g, ((0, 0), (win, 0), (0, 0)))[:, :t]
        count = jnp.minimum(pos_count, win).astype(jnp.float32)[None, :, None]
        groups.append((cs_g - lagged) / count - u32[..., sl])
    pooled = jnp.stack(groups, axis=2)
    mixed = jnp.einsum('btgc,gcd->btgd', pooled.astype(pool_w.dtype), pool_w).reshape(b, t, POOL_WIDTH)
    return mixed * pool_scale * jax.nn.silu(z)

def sparse_attention_branch(qc, kc, vc, zc, iq, ik, iw, q_norm, k_norm, cos_a, sin_a, cos_i, sin_i):
    b, t, _ = qc.shape
    q = apply_rope(rms_norm(qc.reshape(b, t, SA_HEADS, SA_HEAD_DIM), q_norm), cos_a, sin_a)
    k = apply_rope(rms_norm(kc.reshape(b, t, SA_HEADS, SA_HEAD_DIM), k_norm), cos_a, sin_a)
    v = vc.reshape(b, t, SA_HEADS, SA_HEAD_DIM)
    qi = apply_rope(iq.reshape(b, t, IDX_HEADS, IDX_DIM), cos_i, sin_i)
    ki = apply_rope(ik.reshape(b, t, 1, IDX_DIM), cos_i, sin_i)[:, :, 0].astype(jnp.float32)
    wi = iw.astype(jnp.float32) * (IDX_HEADS ** -0.5 * IDX_DIM ** -0.5)
    topk = min(TOPK_MAX, t // 4)
    nb = t // Q_BLOCK
    to_blocks = lambda a: a.reshape((b, nb, Q_BLOCK) + a.shape[2:]).swapaxes(0, 1)
    key_pos = jnp.arange(t, dtype=jnp.int32)
    gather_rows = jax.vmap(lambda src, idx: src[idx])

    def attend(xs):
        q_b, qi_b, wi_b, start = xs
        q_pos = start + jnp.arange(Q_BLOCK, dtype=jnp.int32)
        causal = key_pos[None, :] <= q_pos[:, None]
        dots = jnp.einsum('bqhd,bsd->bqhs', qi_b.astype(jnp.float32), ki)
        score = jnp.einsum('bqh,bqhs->bqs', wi_b, jax.nn.relu(dots))
        score = jnp.where(causal[None], score, -jnp.inf)
        _, idx = lax.top_k(score, topk)
        k_sel = gather_rows(k, idx)
        v_sel = gather_rows(v, idx)
        logits = jnp.einsum('bqhd,bqkhd->bhqk', q_b.astype(jnp.float32), k_sel.astype(jnp.float32)) * (SA_HEAD_DIM ** -0.5)
        valid = idx <= q_pos[None, :, None]
        logits = jnp.where(valid[:, None], logits, -jnp.inf)
        p = jax.nn.softmax(logits, axis=-1)
        return jnp.einsum('bhqk,bqkhd->bqhd', p.astype(v_sel.dtype), v_sel)

    starts = jnp.arange(nb, dtype=jnp.int32) * Q_BLOCK
    o = lax.map(attend, (to_blocks(q), to_blocks(qi), to_blocks(wi), starts))
    o = o.swapaxes(0, 1).reshape(b, t, SA_WIDTH)
    return o * jax.nn.silu(zc)

def hybrid_layer(x, norm_g, w_in, gate_b, conv_w, a_log, dt_bias, dn_onorm, pool_w, pool_scale,
                 q_norm, k_norm, w_branch, w_out, cos_a, sin_a, cos_i, sin_i):
    b, t, _ = x.shape
    h = rms_norm(x, norm_g)
    proj = jnp.einsum('btd,de->bte', h, w_in)
    (qa, ka, va, za, ba, aa, ub, zb, qc, kc, vc, zc, iq, ik, iw, gates) = split_columns(proj)
    ya = deltanet_branch(qa, ka, va, za, ba, aa, conv_w, a_log, dt_bias, dn_onorm)
    yb = pooling_branch(ub, zb, pool_w, pool_scale)
    yc = sparse_attention_branch(qc, kc, vc, zc, iq, ik, iw, q_norm, k_norm, cos_a, sin_a, cos_i, sin_i)
    branches = jnp.stack([ya, yb, yc], axis=2).astype(w_branch.dtype)
    projected = jnp.einsum('btnc,ncd->btnd', branches, w_branch)
    gate = jax.nn.sigmoid(gates.reshape(b, t, N_BRANCH, D_MODEL).astype(jnp.float32) + gate_b.astype(jnp.float32))
    merged = jnp.sum(gate * projected, axis=2).astype(w_out.dtype)
    return x + jnp.einsum('btd,de->bte', merged, w_out).astype(x.dtype)

def first_inputs(seed: int = 0) -> dict:
    key = jax.random.key(seed)
    ks = jax.random.split(key, 16)
    f32 = jnp.float32
    x = jax.random.normal(ks[0], (BATCH, SEQ, D_MODEL), f32)
    norm_g = 1.0 + 0.02 * jax.random.normal(ks[1], (DEPTH, D_MODEL), f32)
    w_in = jax.random.normal(ks[2], (DEPTH, D_MODEL, IN_WIDTH), f32) * D_MODEL ** -0.5
    gate_b = 0.02 * jax.random.normal(ks[3], (DEPTH, N_BRANCH, D_MODEL), f32)
    conv_w = jax.random.normal(ks[4], (DEPTH, DN_CONV, 3 * DN_WIDTH), f32) * DN_CONV ** -0.5
    a_log = jnp.log(jax.random.uniform(ks[5], (DEPTH, DN_HEADS), f32, minval=1.0, maxval=16.0))
    dt = jnp.exp(jax.random.uniform(ks[6], (DEPTH, DN_HEADS), f32, minval=float(np.log(1e-3)), maxval=float(np.log(1e-1))))
    dt_bias = dt + jnp.log(-jnp.expm1(-dt))
    dn_onorm = 1.0 + 0.02 * jax.random.normal(ks[7], (DEPTH, DN_DV), f32)
    pool_w = jax.random.normal(ks[8], (DEPTH, len(POOL_WINDOWS), POOL_GROUP, POOL_GROUP), f32) * POOL_GROUP ** -0.5
    pool_scale = 1.0 + 0.1 * jax.random.normal(ks[9], (DEPTH, POOL_WIDTH), f32)
    q_norm = 1.0 + 0.02 * jax.random.normal(ks[10], (DEPTH, SA_HEAD_DIM), f32)
    k_norm = 1.0 + 0.02 * jax.random.normal(ks[11], (DEPTH, SA_HEAD_DIM), f32)
    w_branch = jax.random.normal(ks[12], (DEPTH, N_BRANCH, BRANCH_WIDTH, D_MODEL), f32) * BRANCH_WIDTH ** -0.5
    w_out = jax.random.normal(ks[13], (DEPTH, D_MODEL, D_MODEL), f32) * D_MODEL ** -0.5
    return {'x': x, 'norm_g': norm_g, 'w_in': w_in, 'gate_b': gate_b, 'conv_w': conv_w,
            'a_log': a_log, 'dt_bias': dt_bias, 'dn_onorm': dn_onorm, 'pool_w': pool_w,
            'pool_scale': pool_scale, 'q_norm': q_norm, 'k_norm': k_norm,
            'w_branch': w_branch, 'w_out': w_out}

def first_block(x, norm_g, w_in, gate_b, conv_w, a_log, dt_bias, dn_onorm, pool_w, pool_scale,
              q_norm, k_norm, w_branch, w_out):
    t = x.shape[1]
    cos_a, sin_a = rope_tables(t, SA_HEAD_DIM)
    cos_i, sin_i = rope_tables(t, IDX_DIM)
    for layer in range(DEPTH):
        x = hybrid_layer(x, norm_g[layer], w_in[layer], gate_b[layer], conv_w[layer], a_log[layer],
                         dt_bias[layer], dn_onorm[layer], pool_w[layer], pool_scale[layer],
                         q_norm[layer], k_norm[layer], w_branch[layer], w_out[layer],
                         cos_a, sin_a, cos_i, sin_i)
    return x


DEPTH_2 = 1

N_HEADS = 8
N_KV = 2
HEAD_DIM = 64
HPG = N_HEADS // N_KV
NSA_WIDTH = N_HEADS * HEAD_DIM
KV_WIDTH = N_KV * HEAD_DIM
ROPE_DIM = HEAD_DIM // 4
ROPE_THETA_2 = 500000.0
CMP_BLOCK = 32
CMP_STRIDE = 16
SLC_BLOCK = 64
N_SLC = 16
WINDOW = 512
PHI_HIDDEN = 256
LRU_WIDTH = D_MODEL
LRU_BLOCKS = 8
LRU_BD = LRU_WIDTH // LRU_BLOCKS
LRU_C = 8.0
CONV_W = 4
D_FF = 4 * D_MODEL
EPS = 1e-6
NEG = -1e30
FORCE_SCORE = 1e4
COL_WIDTHS = (NSA_WIDTH,) + (KV_WIDTH,) * 6 + (N_BRANCH * N_HEADS, LRU_WIDTH, LRU_WIDTH, 2 * D_MODEL)
IN_COLS = sum(COL_WIDTHS)


def rmsnorm(x, w):
    xf = x.astype(jnp.float32)
    y = xf * lax.rsqrt(jnp.mean(xf * xf, axis=-1, keepdims=True) + EPS)
    return (y * w.astype(jnp.float32)).astype(x.dtype)

def rope_partial(x, pos):
    half = ROPE_DIM // 2
    inv = ROPE_THETA_2 ** (-jnp.arange(half, dtype=jnp.float32) / half)
    ang = pos.astype(jnp.float32)[:, None] * inv[None, :]
    cos, sin = jnp.cos(ang), jnp.sin(ang)
    xr = x[..., :ROPE_DIM].astype(jnp.float32)
    x1, x2 = xr[..., :half], xr[..., half:]
    rot = jnp.concatenate([x1 * cos - x2 * sin, x2 * cos + x1 * sin], axis=-1).astype(x.dtype)
    return jnp.concatenate([rot, x[..., ROPE_DIM:]], axis=-1)

def kv_heads(t):
    b, s, _ = t.shape
    return t.reshape(b, s, N_KV, HEAD_DIM).transpose(0, 2, 1, 3)

def compress_mlp(blocks, pos_emb, w1, w2):
    z = (blocks + pos_emb).reshape(blocks.shape[:3] + (CMP_BLOCK * HEAD_DIM,))
    return jax.nn.gelu(z @ w1) @ w2

def nsa_mixer(q_raw, kc_raw, vc_raw, ks_raw, vs_raw, kw_raw, vw_raw, g_raw,
              q_norm_w, k_norm_w, phi_k_pos, phi_k_w1, phi_k_w2, phi_v_pos, phi_v_w1, phi_v_w2):
    B, S, _ = q_raw.shape
    dt = q_raw.dtype
    scale = HEAD_DIM ** -0.5
    t = jnp.arange(S, dtype=jnp.int32)
    nqb = S // Q_BLOCK

    q = q_raw.reshape(B, S, N_KV, HPG, HEAD_DIM).transpose(0, 2, 3, 1, 4)
    q = rope_partial(rmsnorm(q, q_norm_w), t)

    n_cmp = (S - CMP_BLOCK) // CMP_STRIDE + 1
    cmp_idx = jnp.arange(n_cmp)[:, None] * CMP_STRIDE + jnp.arange(CMP_BLOCK)[None, :]
    cmp_end = cmp_idx[:, -1]
    kc = compress_mlp(kv_heads(kc_raw)[:, :, cmp_idx], phi_k_pos, phi_k_w1, phi_k_w2)
    vc = compress_mlp(kv_heads(vc_raw)[:, :, cmp_idx], phi_v_pos, phi_v_w1, phi_v_w2)
    kc = rope_partial(rmsnorm(kc, k_norm_w[0]), cmp_end)
    s_c = jnp.einsum('bghsd,bgnd->bghsn', q, kc).astype(jnp.float32) * scale
    mask_c = cmp_end[None, :] <= t[:, None]
    p_c = jax.nn.softmax(jnp.where(mask_c, s_c, NEG), axis=-1)
    p_c = jnp.where((t >= CMP_BLOCK - 1)[:, None], p_c, 0.0)
    o_cmp = jnp.einsum('bghsn,bgnd->bghsd', p_c.astype(dt), vc)

    n_slc = S // SLC_BLOCK
    n_sel = min(N_SLC, n_slc)
    blk = jnp.arange(n_slc)
    slc_lo = blk * SLC_BLOCK
    overlap = ((cmp_idx[:, 0][:, None] <= (slc_lo + SLC_BLOCK - 1)[None, :]) &
               (cmp_end[:, None] >= slc_lo[None, :])).astype(jnp.float32)
    imp = jnp.einsum('bghsn,nj->bgsj', p_c, overlap)
    cur = t // SLC_BLOCK
    forced = (blk[None, :] == 0) | (blk[None, :] == cur[:, None]) | (blk[None, :] == cur[:, None] - 1)
    causal_ok = blk[None, :] <= cur[:, None]
    score = jnp.where(causal_ok, jnp.where(forced, FORCE_SCORE, imp), NEG)
    _, sel = lax.top_k(score, n_sel)

    k_s = rope_partial(rmsnorm(kv_heads(ks_raw), k_norm_w[1]), t)
    v_s = kv_heads(vs_raw)
    b_ix = jnp.arange(B)[:, None, None]
    g_ix = jnp.arange(N_KV)[None, :, None]
    q_blk = q.reshape(B, N_KV, HPG, nqb, Q_BLOCK, HEAD_DIM).transpose(3, 0, 1, 2, 4, 5)
    sel_blk = sel.reshape(B, N_KV, nqb, Q_BLOCK, n_sel).transpose(2, 0, 1, 3, 4)
    t_blk = t.reshape(nqb, Q_BLOCK)

    def attend_selected(args):
        qb, sb, tb = args
        tok = sb[..., None] * SLC_BLOCK + jnp.arange(SLC_BLOCK)
        tok = tok.reshape(B, N_KV, Q_BLOCK * n_sel * SLC_BLOCK)
        kg = k_s[b_ix, g_ix, tok].reshape(B, N_KV, Q_BLOCK, n_sel * SLC_BLOCK, HEAD_DIM)
        vg = v_s[b_ix, g_ix, tok].reshape(B, N_KV, Q_BLOCK, n_sel * SLC_BLOCK, HEAD_DIM)
        s = jnp.einsum('bghqd,bgqkd->bghqk', qb, kg).astype(jnp.float32) * scale
        m = tok.reshape(B, N_KV, Q_BLOCK, n_sel * SLC_BLOCK) <= tb[None, None, :, None]
        p = jax.nn.softmax(jnp.where(m[:, :, None], s, NEG), axis=-1)
        return jnp.einsum('bghqk,bgqkd->bghqd', p.astype(dt), vg)

    o_slc = lax.map(attend_selected, (q_blk, sel_blk, t_blk))
    o_slc = o_slc.transpose(1, 2, 3, 0, 4, 5).reshape(B, N_KV, HPG, S, HEAD_DIM)

    k_w = rope_partial(rmsnorm(kv_heads(kw_raw), k_norm_w[2]), t)
    v_w = kv_heads(vw_raw)
    win_pos = jnp.arange(nqb)[:, None] * Q_BLOCK + jnp.arange(WINDOW + Q_BLOCK)[None, :] - WINDOW
    safe = jnp.clip(win_pos, 0, S - 1)
    kb = k_w[:, :, safe]
    vb = v_w[:, :, safe]
    qw = q.reshape(B, N_KV, HPG, nqb, Q_BLOCK, HEAD_DIM)
    s_w = jnp.einsum('bghnqd,bgnkd->bghnqk', qw, kb).astype(jnp.float32) * scale
    kp = win_pos[:, None, :]
    tq = t_blk[:, :, None]
    mask_w = (kp <= tq) & (kp > tq - WINDOW) & (kp >= 0)
    p_w = jax.nn.softmax(jnp.where(mask_w, s_w, NEG), axis=-1)
    o_win = jnp.einsum('bghnqk,bgnkd->bghnqd', p_w.astype(dt), vb).reshape(B, N_KV, HPG, S, HEAD_DIM)

    g = jax.nn.sigmoid(g_raw).reshape(B, S, N_BRANCH, N_KV, HPG).transpose(2, 0, 3, 4, 1)[..., None]
    o = g[0] * o_cmp + g[1] * o_slc + g[2] * o_win
    return o.transpose(0, 3, 1, 2, 4).reshape(B, S, NSA_WIDTH)

def rglru_mixer(xr, yr, conv_w, conv_b, lru_wa, lru_ba, lru_wx, lru_bx, lru_lambda):
    B, S, W = xr.shape
    xp = jnp.pad(xr, ((0, 0), (CONV_W - 1, 0), (0, 0)))
    xc = conv_b + sum(xp[:, j:j + S] * conv_w[j] for j in range(CONV_W))
    xb = xc.reshape(B, S, LRU_BLOCKS, LRU_BD)
    r = jax.nn.sigmoid(jnp.einsum('bsnd,nde->bsne', xb, lru_wa) + lru_ba).reshape(B, S, W)
    i_g = jax.nn.sigmoid(jnp.einsum('bsnd,nde->bsne', xb, lru_wx) + lru_bx).reshape(B, S, W)
    log_a = -LRU_C * jax.nn.softplus(-lru_lambda.astype(jnp.float32)) * r.astype(jnp.float32)
    a = jnp.exp(log_a)
    bterm = jnp.sqrt(-jnp.expm1(2.0 * log_a)) * (i_g.astype(jnp.float32) * xc.astype(jnp.float32))

    def combine(left, right):
        a1, b1 = left
        a2, b2 = right
        return a1 * a2, a2 * b1 + b2

    _, h = lax.associative_scan(combine, (a, bterm), axis=1)
    return h.astype(xr.dtype) * jax.nn.gelu(yr)

def second_inputs(seed: int = 0) -> dict:
    key = jax.random.key(seed)
    ks = jax.random.split(key, 24)
    L = DEPTH_2

    def nrm(k, shape, scale):
        return jax.random.normal(k, shape, jnp.float32) * scale

    u = jax.random.uniform(ks[17], (L, LRU_WIDTH), jnp.float32, 0.9, 0.999)
    a0 = u ** (1.0 / LRU_C)
    return {
        "x": nrm(ks[0], (BATCH, SEQ, D_MODEL), 1.0),
        "norm1_w": 1.0 + nrm(ks[1], (L, D_MODEL), 0.02),
        "w_in": nrm(ks[2], (L, D_MODEL, IN_COLS), D_MODEL ** -0.5),
        "q_norm_w": 1.0 + nrm(ks[3], (L, HEAD_DIM), 0.02),
        "k_norm_w": 1.0 + nrm(ks[4], (L, N_BRANCH, HEAD_DIM), 0.02),
        "phi_k_pos": nrm(ks[5], (L, CMP_BLOCK, HEAD_DIM), 0.02),
        "phi_k_w1": nrm(ks[6], (L, CMP_BLOCK * HEAD_DIM, PHI_HIDDEN), (CMP_BLOCK * HEAD_DIM) ** -0.5),
        "phi_k_w2": nrm(ks[7], (L, PHI_HIDDEN, HEAD_DIM), PHI_HIDDEN ** -0.5),
        "phi_v_pos": nrm(ks[8], (L, CMP_BLOCK, HEAD_DIM), 0.02),
        "phi_v_w1": nrm(ks[9], (L, CMP_BLOCK * HEAD_DIM, PHI_HIDDEN), (CMP_BLOCK * HEAD_DIM) ** -0.5),
        "phi_v_w2": nrm(ks[10], (L, PHI_HIDDEN, HEAD_DIM), PHI_HIDDEN ** -0.5),
        "conv_w": nrm(ks[11], (L, CONV_W, LRU_WIDTH), CONV_W ** -0.5),
        "conv_b": nrm(ks[12], (L, LRU_WIDTH), 0.01),
        "lru_wa": nrm(ks[13], (L, LRU_BLOCKS, LRU_BD, LRU_BD), LRU_BD ** -0.5),
        "lru_ba": nrm(ks[14], (L, LRU_BLOCKS, LRU_BD), 0.01),
        "lru_wx": nrm(ks[15], (L, LRU_BLOCKS, LRU_BD, LRU_BD), LRU_BD ** -0.5),
        "lru_bx": nrm(ks[16], (L, LRU_BLOCKS, LRU_BD), 0.01),
        "lru_lambda": jnp.log(a0) - jnp.log1p(-a0),
        "w_nsa_up": nrm(ks[18], (L, NSA_WIDTH, D_MODEL), NSA_WIDTH ** -0.5),
        "w_lru_up": nrm(ks[19], (L, LRU_WIDTH, D_MODEL), LRU_WIDTH ** -0.5),
        "w_o": nrm(ks[20], (L, D_MODEL, D_MODEL), D_MODEL ** -0.5),
        "norm2_w": 1.0 + nrm(ks[21], (L, D_MODEL), 0.02),
        "w_ff1": nrm(ks[22], (L, D_MODEL, D_FF), D_MODEL ** -0.5),
        "w_ff2": nrm(ks[23], (L, D_FF, D_MODEL), D_FF ** -0.5),
    }

def second_block(x, norm1_w, w_in, q_norm_w, k_norm_w, phi_k_pos, phi_k_w1, phi_k_w2,
              phi_v_pos, phi_v_w1, phi_v_w2, conv_w, conv_b, lru_wa, lru_ba, lru_wx, lru_bx,
              lru_lambda, w_nsa_up, w_lru_up, w_o, norm2_w, w_ff1, w_ff2):
    h = x
    for l in range(DEPTH_2):
        xn = rmsnorm(h, norm1_w[l])
        proj = xn @ w_in[l]
        parts = []
        off = 0
        for wdt in COL_WIDTHS:
            parts.append(proj[..., off:off + wdt])
            off += wdt
        q_raw, kc_raw, vc_raw, ks_raw, vs_raw, kw_raw, vw_raw, g_nsa, xr, yr, g_merge = parts

        o_nsa = nsa_mixer(q_raw, kc_raw, vc_raw, ks_raw, vs_raw, kw_raw, vw_raw, g_nsa,
                          q_norm_w[l], k_norm_w[l], phi_k_pos[l], phi_k_w1[l], phi_k_w2[l],
                          phi_v_pos[l], phi_v_w1[l], phi_v_w2[l])
        o_lru = rglru_mixer(xr, yr, conv_w[l], conv_b[l], lru_wa[l], lru_ba[l], lru_wx[l],
                            lru_bx[l], lru_lambda[l])
        gate = jax.nn.sigmoid(g_merge)
        merged = gate[..., :D_MODEL] * (o_nsa @ w_nsa_up[l]) + gate[..., D_MODEL:] * (o_lru @ w_lru_up[l])
        h = h + merged @ w_o[l]

        hn = rmsnorm(h, norm2_w[l])
        h = h + jnp.square(jax.nn.relu(hn @ w_ff1[l])) @ w_ff2[l]
    return h


def setup_inputs(seed=0):
    out = dict(first_inputs(seed))
    for name, value in second_inputs(seed + 1).items():
        if name != "x":
            out[name + "_2"] = value
    return out


def reference(
    x, norm_g, w_in, gate_b, conv_w, a_log, dt_bias, dn_onorm, pool_w, pool_scale, q_norm,
    k_norm, w_branch, w_out, norm1_w_2, w_in_2, q_norm_w_2, k_norm_w_2, phi_k_pos_2, phi_k_w1_2,
    phi_k_w2_2, phi_v_pos_2, phi_v_w1_2, phi_v_w2_2, conv_w_2, conv_b_2, lru_wa_2, lru_ba_2,
    lru_wx_2, lru_bx_2, lru_lambda_2, w_nsa_up_2, w_lru_up_2, w_o_2, norm2_w_2, w_ff1_2,
    w_ff2_2,
):
    x = first_block(
        x, norm_g, w_in, gate_b, conv_w, a_log, dt_bias, dn_onorm, pool_w, pool_scale, q_norm,
        k_norm, w_branch, w_out,
    )
    return second_block(
        x, norm1_w_2, w_in_2, q_norm_w_2, k_norm_w_2, phi_k_pos_2, phi_k_w1_2, phi_k_w2_2,
        phi_v_pos_2, phi_v_w1_2, phi_v_w2_2, conv_w_2, conv_b_2, lru_wa_2, lru_ba_2, lru_wx_2,
        lru_bx_2, lru_lambda_2, w_nsa_up_2, w_lru_up_2, w_o_2, norm2_w_2, w_ff1_2, w_ff2_2,
    )


_drawn_inputs = setup_inputs


def setup_inputs(seed=0):
    import zlib

    import numpy as np

    out = dict(_drawn_inputs(seed))
    spreads = {}
    factors = {'gate_b': 8.0,
     'dn_onorm': 5.524,
     'q_norm': 8.0,
     'k_norm': 8.0,
     'norm1_w_2': 8.0,
     'q_norm_w_2': 8.0,
     'k_norm_w_2': 21.816,
     'phi_k_pos_2': 64.0,
     'phi_v_pos_2': 194.68,
     'conv_b_2': 11.097,
     'lru_ba_2': 64.0,
     'lru_bx_2': 47.536,
     'norm2_w_2': 19.763}
    for name, (base, spread) in spreads.items():
        noise = np.random.default_rng([zlib.crc32(name.encode()), seed]).standard_normal(out[name].shape)
        drawn = base * np.exp(spread * noise) if base else spread * noise
        out[name] = jnp.asarray(drawn.astype(out[name].dtype))
    for name, factor in factors.items():
        out[name] = (out[name] * factor).astype(out[name].dtype)
    return out
```

```python
import math
from contextlib import ExitStack

import numpy as np

import concourse.bass as bass
from concourse import mybir

F32 = mybir.dt.float32
F32R = mybir.dt.float32r
ACT = mybir.ActivationFunctionType
ALU = mybir.AluOpType
AXX = mybir.AxisListType.X

T = 512
D = 1024
NK = 8
NEG = -1.0e30
MARK = -3.0e38
EPS = 1e-6
U = 1024



def plan():
    out = []
    for l in range(2):
        out += [("small", l)]
        out += [("p", l, 128 * c) for c in range(12)]
        out += [("p", l, 1536 + 128 * c) for c in range(4)]
        out += [("p", l, 5128), ("p", l, 5256), ("ik", l)]
        out += [("p", l, 3080 + 128 * c) for c in range(4)]
        out += [("p", l, 3592 + 128 * c) for c in range(4)]
        out += [("v", l, j) for j in range(4)]
        for g in range(4):
            out += [("p", l, 2568 + 128 * g), ("p", l, 2056 + 128 * g)]
        out += [("p", l, 4616 + 128 * c) for c in range(4)]
        for n in (1, 0, 2):
            for m in range(8):
                if m % 2 == 0:
                    out.append(("br", l, n, m // 2))
                out.append(("p", l, 5452 + 1024 * n + 128 * m))
        out += [("o", l, m) for m in range(8)]
    out += [("q2", c) for c in range(4)]
    out += [("c2", 512), ("c2", 640), ("c2", 768), ("c2", 1024)]
    out += [("v2", j) for j in range(3)]
    for c in range(8):
        out += [("c2", 1304 + 128 * c), ("c2", 2328 + 128 * c)]
    for m in range(8):
        out += [("c2", 4376 + 128 * m), ("lup", m)]
    for m in range(8):
        if m % 2 == 0:
            out.append(("nup", m // 2))
        out += [("c2", 3352 + 128 * m)]
    out += [("o2", m) for m in range(8)]
    for h in range(2):
        out += [("f1", 16 * h + j) for j in range(16)]
        out += [("f2", 2 * h + jj, m) for m in range(8) for jj in range(2)]
    return out


def q2_columns(c):
    return np.concatenate([np.arange(64 * c, 64 * c + 64), np.arange(64 * (4 + c), 64 * (4 + c) + 64)])


def pack_units(I):
    keys = plan()
    units = np.zeros((len(keys), 128, U), np.float32)

    def kmajor(w):
        k, n = w.shape[0] // 128, w.shape[1]
        return w.reshape(k, 128, n).transpose(1, 0, 2).reshape(128, k * n)

    w2 = I["w_in_2"][0]
    vg = np.concatenate([w2[:, 896:1024], w2[:, 1152:1280], w2[:, 1280:1304]], axis=1)
    for n, key in enumerate(keys):
        kind = key[0]
        if kind == "small":
            u = units[n].reshape(128, 8, 128)
            w = I["w_in"][key[1]]
            for c0, at in ((2048, 0), (2052, 32), (5448, 64)):
                u[:, :, at:at + 4] = kmajor(w[:, c0:c0 + 4]).reshape(128, 8, 4)
        elif kind == "p":
            units[n] = kmajor(I["w_in"][key[1]][:, key[2]:key[2] + 128])
        elif kind == "ik":
            w = I["w_in"][key[1]][:, 5384:5448]
            units[n].reshape(128, 8, 128)[:, :, 0:64] = kmajor(w).reshape(128, 8, 64)
            units[n].reshape(128, 8, 128)[:, :, 64:128] = kmajor(w).reshape(128, 8, 64)
        elif kind == "v":
            j = key[2]
            units[n] = kmajor(I["w_in"][key[1]][256 * j:256 * j + 256, 4104:4616])
        elif kind == "br":
            w = I["w_branch"][key[1], key[2]][:, 256 * key[3]:256 * key[3] + 256]
            units[n] = w.reshape(4, 128, 2, 128).transpose(1, 2, 0, 3).reshape(128, U)
        elif kind == "o":
            units[n] = kmajor(I["w_out"][key[1]][:, 128 * key[2]:128 * key[2] + 128])
        elif kind == "q2":
            units[n] = kmajor(w2[:, q2_columns(key[1])])
        elif kind == "c2":
            units[n] = kmajor(w2[:, key[1]:key[1] + 128])
        elif kind == "v2":
            k0, k1 = 3 * key[1], min(8, 3 * key[1] + 3)
            units[n, :, 0:280 * (k1 - k0)] = kmajor(vg[128 * k0:128 * k1])
        elif kind == "lup":
            units[n] = kmajor(I["w_lru_up_2"][0][:, 128 * key[1]:128 * key[1] + 128])
        elif kind == "nup":
            w = I["w_nsa_up_2"][0][:, 256 * key[1]:256 * key[1] + 256]
            units[n] = w.reshape(4, 128, 2, 128).transpose(1, 2, 0, 3).reshape(128, U)
        elif kind == "o2":
            units[n] = kmajor(I["w_o_2"][0][:, 128 * key[1]:128 * key[1] + 128])
        elif kind == "f1":
            units[n] = kmajor(I["w_ff1_2"][0][:, 128 * key[1]:128 * key[1] + 128])
        elif kind == "f2":
            j, m = key[1], key[2]
            units[n] = kmajor(I["w_ff2_2"][0][1024 * j:1024 * j + 1024, 128 * m:128 * m + 128])
    return units



class Packed:

    def __init__(self):
        self.at, self.parts, self.n = {}, [], 0

    def add(self, name, a):
        a = np.asarray(a, np.float32)
        a = a.reshape(128, -1)
        self.at[name] = (self.n, self.n + a.shape[1])
        self.parts.append(a)
        self.n += a.shape[1]

    def array(self):
        return np.ascontiguousarray(np.concatenate(self.parts, axis=1))


def rope_np(seq, dim, theta):
    inv = theta ** (-np.arange(0, dim, 2, dtype=np.float32) / np.float32(dim))
    ang = np.arange(seq, dtype=np.float32)[:, None] * inv[None, :].astype(np.float32)
    return np.cos(ang).astype(np.float32), np.sin(ang).astype(np.float32)


def constants():
    c = Packed()
    i = np.arange(128)
    c.add("ident", np.eye(128))
    c.add("ones", np.ones((128, 128)))
    c.add("blk", (i[:, None] // 64 == i[None, :] // 64))
    same = i[:, None] // 64 == i[None, :] // 64
    c.add("decay", np.where(same & (i[:, None] <= i[None, :]), 0.0, NEG))
    c.add("last", i[:, None] == 64 * (i[None, :] // 64) + 63)
    levels = []
    for n in range(6):
        s = 2 ** n
        j, k = i[:, None], i[None, :]
        levels.append((j // (2 * s) == k // (2 * s)) & (j // s % 2 == 0) & (k // s % 2 == 1))
    c.add("levels", np.stack(levels, 1))
    r128 = np.zeros((128, 128))
    for k in range(64):
        r128[k + 64, k] = -1.0
        r128[k, k + 64] = 1.0
    c.add("r128", r128)
    r64 = np.zeros((128, 128))
    for b in (0, 64):
        for k in range(32):
            r64[b + k + 32, b + k] = -1.0
            r64[b + k, b + k + 32] = 1.0
    c.add("r64", r64)
    c.add("causal", np.where((np.arange(512)[None, :] - 384) <= i[:, None], 0.0, NEG))
    reset = np.ones((128, T))
    reset[:, ::64] = 0.0
    c.add("reset", reset)
    cnt = np.zeros((4, 16), np.float32)
    for g, w in enumerate((2, 4, 8, 16)):
        cnt[g] = np.float32(1.0) / np.minimum(np.arange(1, 17), w).astype(np.float32)
    c.add("count", np.broadcast_to(cnt[None], (128, 4, 16)))
    c.add("eps", np.full((128, 1), EPS))
    return c


def tables_a():
    c = Packed()
    co, si = rope_np(T, 128, 10000.0)
    c.add("cosA", np.concatenate([co.T, co.T]))
    c.add("sinA", np.concatenate([si.T, si.T]))
    co, si = rope_np(T, 64, 10000.0)
    c.add("cosI", np.concatenate([co.T] * 4))
    c.add("sinI", np.concatenate([si.T] * 4))
    return c


def tables_b():
    c = Packed()
    inv = np.float32(500000.0) ** (-np.arange(8, dtype=np.float32) / np.float32(8))
    ang = np.arange(T, dtype=np.float32)[:, None] * inv[None, :]
    co, si = np.ones((128, T), np.float32), np.zeros((128, T), np.float32)
    r = np.zeros((128, 128))
    for b in (0, 64):
        for h in (0, 8):
            co[b + h:b + h + 8] = np.cos(ang).T
            si[b + h:b + h + 8] = np.sin(ang).T
        for k in range(8):
            r[b + k + 8, b + k] = -1.0
            r[b + k, b + k + 8] = 1.0
    c.add("cos", co)
    c.add("sin", si)
    end = 16 * np.arange(31) + 31
    c.add("cosC", co[:, end])
    c.add("sinC", si[:, end])
    c.add("r16", r)
    t = np.arange(128)[:, None, None] + 128 * np.arange(4)[None, :, None]
    c.add("maskC", np.where(end[None, None, :] <= t, 0.0, NEG))
    c.add("validC", (t[:, :, 0] >= 31))
    return c


def column_names():
    at, n = {}, 0
    sizes = []
    for l in range(2):
        sizes += [(f"norm{l}", 8), (f"gateb{l}", 24), (f"conv{l}", 48), (f"alog{l}", 1), (f"dt{l}", 1),
                  (f"onorm{l}", 1), (f"pscale{l}", 4), (f"qn{l}", 1), (f"kn{l}", 1)]
    sizes += [("nrmA", 8), ("nrmB", 8), ("qn2", 1), ("kn2", 3), ("conv2", 32), ("convb", 8), ("ba", 8),
              ("bx", 8), ("lam", 8), ("posk", 16), ("posv", 16)]
    for name, k in sizes:
        at[name] = (n, n + k)
        n += k
    return at, n


def pack_columns(I):
    at, n = column_names()
    c = np.zeros((128, n), np.float32)

    def put(name, a):
        c[:, at[name][0]:at[name][1]] = a

    def chunks(v):
        return v.reshape(-1, 128).T

    for l in range(2):
        put(f"norm{l}", chunks(I["norm_g"][l]))
        put(f"gateb{l}", chunks(I["gate_b"][l].reshape(-1)))
        put(f"conv{l}", I["conv_w"][l].reshape(4, 12, 128).transpose(2, 1, 0).reshape(128, 48))
        c[32:36, at[f"alog{l}"][0]] = I["a_log"][l]
        c[32:36, at[f"dt{l}"][0]] = I["dt_bias"][l]
        put(f"onorm{l}", I["dn_onorm"][l][:, None])
        put(f"pscale{l}", chunks(I["pool_scale"][l]))
        put(f"qn{l}", I["q_norm"][l][:, None])
        put(f"kn{l}", I["k_norm"][l][:, None])
    put("nrmA", chunks(I["norm1_w_2"][0]))
    put("nrmB", chunks(I["norm2_w_2"][0]))
    put("qn2", np.concatenate([I["q_norm_w_2"][0]] * 2)[:, None])
    put("kn2", np.concatenate([I["k_norm_w_2"][0].T] * 2))
    put("conv2", I["conv_w_2"][0].reshape(4, 8, 128).transpose(2, 1, 0).reshape(128, 32))
    put("convb", chunks(I["conv_b_2"][0]))
    put("ba", I["lru_ba_2"][0].T)
    put("bx", I["lru_bx_2"][0].T)
    put("lam", chunks(I["lru_lambda_2"][0]))
    put("posk", I["phi_k_pos_2"][0].reshape(16, 128).T)
    put("posv", I["phi_v_pos_2"][0].reshape(16, 128).T)
    return c



class Queue:

    def __init__(self, sem):
        self.sem, self.n, self.items, self.waited = sem, 0, [], {}

    def wait(self, *tokens):
        for t in tokens:
            if t is None:
                continue
            sem, value = t
            if self.waited.get(sem.name, 0) < value:
                self.waited[sem.name] = value
                self.items.append(lambda e, s=sem, v=value: e.wait_ge(s, v))

    def do(self, f, after=(), signal=True):
        self.wait(*after)
        if not signal:
            self.items.append(f)
            return None
        self.n += 1
        self.items.append(lambda e, s=self.sem: f(e).then_inc(s, 1))
        return (self.sem, self.n)

    def last(self):
        return (self.sem, self.n) if self.n else None

    def dma(self, out, in_, sem, *after):
        self.do(lambda e: e.dma_start(out, in_).then_inc(sem, 16), after, signal=False)

    def play(self, e):
        for f in self.items:
            f(e)


class Vec(Queue):
    def tt(self, out, a, b, op, *after):
        return self.do(lambda e: e.tensor_tensor(out, a, b, op), after)

    def ts(self, out, a, s1, op0, s2, op1, *after):
        if s2 is None:
            return self.do(lambda e: e.tensor_scalar(out, a, s1, None, op0), after)
        return self.do(lambda e: e.tensor_scalar(out, a, s1, s2, op0, op1), after)

    def stt(self, out, a, s, b, op0, op1, *after):
        return self.do(lambda e: e.scalar_tensor_tensor(out=out, in0=a, scalar=s, in1=b, op0=op0, op1=op1), after)

    def cp(self, out, a, *after):
        return self.do(lambda e: e.tensor_copy(out, a), after)

    def set(self, out, v, *after):
        return self.do(lambda e: e.memset(out, v), after)

    def scan(self, out, a, b, initial, *after):
        return self.do(lambda e: e.tensor_tensor_scan(out, a, b, initial, ALU.mult, ALU.add), after)

    def max8(self, out, a, *after):
        return self.do(lambda e: e.max(out, a), after)

    def replace(self, out, vals, a, v, *after):
        return self.do(lambda e: e.match_replace(out, vals, a, v), after)

    def addred(self, out, a, b, scale, init, red, acc, *after):
        return self.do(lambda e: e.tensor_tensor_reduce(out, a, b, scale, init, ALU.add, red, acc), after)

    def rec(self, out, a, *after):
        return self.do(lambda e: e.reciprocal(out, a), after)


class Act(Queue):
    def act(self, out, a, func, scale, bias, *after, acc=None):
        def f(e):
            kw = {}
            if bias is not None:
                kw["bias"] = bias
            if acc is not None:
                kw["accum_out"] = acc
            return e.activation(out, a, func, scale=scale, **kw)
        return self.do(f, after)

    def cp(self, out, a, *after):
        return self.do(lambda e: e.activation(out, a, ACT.Copy), after)


class Ten(Queue):
    def mm(self, out, lhsT, rhs, start, stop, *after, signal=False, share=False):
        return self.do(lambda e: e.matmul(out, lhsT, rhs, start=start, stop=stop, skip_group_check=share),
                       after, signal)

    def tr(self, out, a, ident, *after, signal=False):
        return self.do(lambda e: e.transpose(out, a, ident), after, signal)


class Slot:

    def __init__(self, ap):
        self.ap, self.free = ap, ()


def weave(main, side, every=1, steps=1):
    n = 0
    alive = True
    for _ in main:
        n += 1
        if alive and n % every == 0:
            for _ in range(steps):
                if next(side, "end") == "end":
                    alive = False
                    break
    if alive:
        for _ in side:
            pass



def build(nc, units, consts, tabA, tabB, cols, poolw, lruw, phi1, phi2, x_in, x_out, cpack, apack, bpack, debug=None):
    keys = plan()
    with ExitStack() as ctx:
        def sb(name, shape, dt=F32, stack=ctx):
            return stack.enter_context(nc.sbuf_tensor(name, shape, dt))

        def sem(name):
            return ctx.enter_context(nc.semaphore(name))

        PE, V, A, G = Ten(sem("s_pe")), Vec(sem("s_dve")), Act(sem("s_act")), Vec(sem("s_pool"))
        S = Queue(sem("s_sp"))

        def barrier():
            last = [q.last() for q in (PE, V, A, G)]
            for q in (PE, V, A, G):
                q.wait(*last)
            return last

        bank = [Slot(ctx.enter_context(nc.psum_tensor(f"bank{i}", [128, 512], F32))) for i in range(8)]
        cst = sb("cst", [128, cpack.n])
        col = sb("col", [128, cols.shape[1]])
        colx = sb("colx", [128, 96])
        hh = sb("hh", [128, 8, T], F32R)
        hl = sb("hl", [128, 8, T], F32R)
        tmp = [Slot(sb(f"tmp{i}", [128, T])) for i in range(4)]
        tno = [0]

        def tmps(k):
            out = [tmp[(tno[0] + i) % len(tmp)] for i in range(k)]
            tno[0] = (tno[0] + k) % len(tmp)
            return out

        def C(name):
            a, b = cpack.at[name]
            return cst[:, a:b]

        names, _ = column_names()

        def K(name, i=0, rows=slice(0, 128)):
            return col[rows, names[name][0] + i:names[name][0] + i + 1]

        ident, ones, blk, eps = C("ident"), C("ones"), C("blk"), C("eps")

        s_c = sem("s_consts")
        S.dma(cst[:], consts, s_c)
        S.dma(col[:], cols, s_c)
        t_const = (s_c, 32)
        for q in (PE, V, A, G):
            q.wait(t_const)

        NS, NH, AHEAD = 3, 3, 2
        stage = [Slot(sb(f"st{i}", [128, U])) for i in range(NS)]
        wh = [sb(f"wh{i}", [128, U], F32R) for i in range(NH)]
        wl = [sb(f"wl{i}", [128, U], F32R) for i in range(NH)]
        s_st = [sem(f"s_st{i}") for i in range(NS)]
        wfree = [None] * NH
        st = {"loaded": 0, "split": 0, "used": 0}
        split_tok = {}

        def load(n):
            s = stage[n % NS]
            S.wait(*s.free)
            S.dma(s.ap[:], units[n], s_st[n % NS])

        def split(n):
            src, i = stage[n % NS], n % NH
            landed = (s_st[n % NS], 16 * (n // NS + 1))
            thi = A.cp(wh[i][:], src.ap[:], landed, wfree[i])
            tlo = G.tt(wl[i][:], src.ap[:], wh[i][:].bitcast(F32), ALU.subtract, thi, landed)
            src.free = (thi, tlo)
            split_tok[n] = (thi, tlo)

        def take(key):
            n = st["used"]
            assert keys[n] == key, (keys[n], key)
            st["used"] += 1
            while st["split"] < min(n + AHEAD, len(keys)):
                m = st["split"]
                load(m)
                split(m)
                st["split"] += 1
            PE.wait(*split_tok.pop(n))
            return n % NH

        def done(i, tok):
            wfree[i] = tok

        def prod3(out, i, wsl, xh, xl, first, last, signal=None):
            PE.mm(out, wh[i][:, wsl], xh, first, False)
            PE.mm(out, wh[i][:, wsl], xl, False, False)
            return PE.mm(out, wl[i][:, wsl], xh, False, last, signal=last if signal is None else signal)

        def project(key, b, xh=None, xl=None, nk=8):
            xh, xl = hh if xh is None else xh, hl if xl is None else xl
            i = take(key)
            PE.wait(*bank[b].free)
            for k in range(nk):
                t = prod3(bank[b].ap[:], i, slice(128 * k, 128 * k + 128), xh[:, k, :], xl[:, k, :], k == 0, k == nk - 1)
                if k == 3:
                    yield
            done(i, t)
            return t

        def pair(dst_h, dst_l, src, tok, lo=None):
            th = A.cp(dst_h, src, tok)
            tl = (lo or V).tt(dst_l, src, dst_h.bitcast(F32), ALU.subtract, tok, th)
            return th, tl

        def rnorm(dst, src, scale, *after):
            t1 = A.act(dst, src, ACT.Ln, scale, eps, *after)
            return A.act(dst, dst, ACT.Exp, -0.5, None, t1)

        def norm_into_h(xt, toks, gname):
            acc, sq = tmps(2)
            V.wait(*acc.free)
            t_acc = None
            for k in range(8):
                t_sq = A.act(sq.ap[:], xt[:, k, :], ACT.Square, 1.0, None, toks[k], *sq.free, *(acc.free if k == 0 else ()))
                if k == 0:
                    t_acc = V.cp(acc.ap[:], sq.ap[:], t_sq)
                else:
                    t_acc = V.tt(acc.ap[:], acc.ap[:], sq.ap[:], ALU.add, t_sq, t_acc)
                sq.free = (t_acc,)
            b = bank[7]
            t = PE.mm(b.ap[:], ones, acc.ap[:], True, True, t_acc, *b.free, signal=True)
            acc.free = (t,)
            rr, h0 = tmps(2)
            h1, = tmps(1)
            t_r = rnorm(rr.ap[:], b.ap[:], 1.0 / D, t, *rr.free)
            b.free = (t_r,)
            last = (PE.last(),)
            for k in range(8):
                hb = (h0, h1)[k % 2]
                th = V.stt(hb.ap[:], xt[:, k, :], K(gname, k), rr.ap[:], ALU.mult, ALU.mult, t_r, *hb.free)
                rr.free = (th,)
                t_hi = A.cp(hh[:, k, :], hb.ap[:], th, *last)
                t_lo = V.tt(hl[:, k, :], hb.ap[:], hh[:, k, :].bitcast(F32), ALU.subtract, th, t_hi)
                hb.free = (t_hi, t_lo)
                PE.wait(t_hi, t_lo)

        dbg = {}

        def tap(name, ap, *toks):
            if debug is not None and name in debug:
                if "sem" not in dbg:
                    dbg["sem"] = sem("s_dbg")
                dbg["n"] = dbg.get("n", 0) + 16
                A.wait(*toks)
                A.dma(debug[name], ap, dbg["sem"])
                A.wait((dbg["sem"], dbg["n"]))

        s_x = sem("s_x")
        xn = [0]
        scratch = nc.dram_tensor("x_scratch", [128, 8, T], F32).ap()
        s_sc = sem("s_scratch")
        scn = [0]

        def conv(ps, tok, wname, c, dst, bias=None):
            xp, = pads(1)
            t0 = A.cp(xp.ap[:, 3:3 + T], ps.ap[:], tok, *xp.free)
            w = lambda j: K(wname, 4 * c + j)
            t1 = A.act(dst, ps.ap[:], ACT.Identity, w(3), bias if bias is not None else 0.0)
            ps.free = (t1,)
            t = V.stt(dst, xp.ap[:, 2:2 + T], w(2), dst, ALU.mult, ALU.add, t0, t1)
            t = V.stt(dst, xp.ap[:, 1:1 + T], w(1), dst, ALU.mult, ALU.add, t)
            t = V.stt(dst, xp.ap[:, 0:T], w(0), dst, ALU.mult, ALU.add, t)
            xp.free = (t,)
            return t

        pad = [Slot(sb(f"pad{i}", [128, 16 + T])) for i in range(2)]
        pno = [0]
        for p in pad:
            p.free = (V.set(p.ap[:, 0:3], 0.0),)

        def pads(k):
            out = [pad[(pno[0] + i) % 2] for i in range(k)]
            pno[0] += k
            return out

        def silu2(dst, src, tok, *after):
            th, = tmps(1)
            t1 = A.act(th.ap[:], src, ACT.Tanh, 0.5, None, tok, *th.free)
            t2 = V.stt(dst, th.ap[:], 1.0, src, ALU.add, ALU.mult, t1, tok, *after)
            th.free = (t2,)
            return t2

        def rope(dst, src, rot, cos, sin, b, tok, width=T):
            t_p = PE.mm(bank[b].ap[:, 0:width], rot, src, True, True, tok, *bank[b].free, signal=True)
            s1, = tmps(1)
            t1 = V.tt(s1.ap[:, 0:width], bank[b].ap[:, 0:width], sin, ALU.mult, t_p, *s1.free)
            bank[b].free = (t1,)
            t2 = V.tt(dst, src, cos, ALU.mult, tok, t_p)
            t3 = V.tt(dst, dst, s1.ap[:, 0:width], ALU.add, t1, t2)
            s1.free = (t3,)
            return t3

        tabs = sb("tabs", [128, max(apack.n, bpack.n)])
        xstack = ExitStack()
        xt = sb("xt_in", [128, 8, T], stack=xstack)
        S.dma(xt[:], x_in, s_x)
        xn[0] = 16
        x_toks = [(s_x, 16)] * 8
        x_src = x_in
        s_tab = sem("s_tab")
        S.dma(tabs[:, 0:apack.n], tabA, s_tab)
        for q in (PE, V, A):
            q.wait((s_tab, 16))
        t_lam = V.set(colx[:], 0.0)

        for l in range(2):
            def TA(name):
                a, b = apack.at[name]
                return tabs[:, a:b]

            norm_into_h(xt, x_toks, f"norm{l}")
            barrier()
            xstack.close()

            lay, dn = ExitStack(), ExitStack()
            za = sb(f"za{l}", [128, 4, T], stack=lay)
            qs, ks = [sb(f"{n}s{l}", [128, 4, T], stack=lay) for n in "qk"]
            qi, ki = [sb(f"{n}i{l}", [128, 2, T], stack=lay) for n in "qk"]
            wi = sb(f"wi{l}", [128, 4, 4], stack=lay)
            rw = sb(f"rw{l}", [128, T], stack=dn)
            tpc = sb(f"tpc{l}", [128, 4, 128], stack=dn)
            gcol = sb(f"gcol{l}", [128, 4, 16], stack=dn)
            egl = sb(f"egl{l}", [128, 2, 4, 4], stack=dn)
            qf, kf, vf = [sb(f"{n}f{l}", [128, 4, T], stack=dn) for n in "qkv"]
            t_z = V.set(rw[:], 0.0)

            small = {}

            def phase1():
                t = yield from project(("small", l), 0)
                b = bank[0]
                e1, z1 = tmps(2)
                z2, z3 = tmps(2)
                R0, R1, R2 = slice(0, 4), slice(32, 36), slice(64, 68)
                ta = A.act(e1.ap[R0, :], b.ap[R0, :], ACT.Exp, -1.0, None, t, *e1.free)
                tb = V.ts(e1.ap[R0, :], e1.ap[R0, :], 1.0, ALU.add, None, None, ta)
                tb = V.rec(rw[R0, :], e1.ap[R0, :], tb, t_z)
                e1.free = (tb,)
                tc = V.ts(z1.ap[R1, :], b.ap[R1, :], K(f"dt{l}", 0, R1), ALU.add, None, None, ta, *z1.free)
                td = A.act(z2.ap[R1, :], z1.ap[R1, :], ACT.Abs, 1.0, None, tc, *z2.free)
                te = A.act(z2.ap[R1, :], z2.ap[R1, :], ACT.Exp, -1.0, None, td)
                te = A.act(z2.ap[R1, :], z2.ap[R1, :], ACT.Ln, 1.0, 1.0, te)
                tf = V.stt(z1.ap[R1, :], z1.ap[R1, :], 0.0, z2.ap[R1, :], ALU.max, ALU.add, te, tc)
                z2.free = (tf,)
                tg = A.act(colx[R1, 0:1], K(f"alog{l}", 0, R1), ACT.Exp, 1.0, None, t_lam)
                tf = V.ts(z1.ap[R1, :], z1.ap[R1, :], colx[R1, 0:1], ALU.mult, -1.0, ALU.mult, tf, tg)
                th = V.scan(rw[R1, :], C("reset")[R1, :], z1.ap[R1, :], 0.0, tf, t_z)
                z1.free = (th,)
                ti = V.ts(rw[R2, :], b.ap[R2, :], 1.0 / 16.0, ALU.mult, None, None, ta, t_z)
                b.free = (ta, tc, ti)
                small["rw"] = (tb, th, ti)
                for c in range(12):
                    b = c % 3
                    t = yield from project(("p", l, 128 * c), b)
                    dst = (qf, kf, vf)[c // 4][:, c % 4, :]
                    cv, = tmps(1)
                    V.wait(*cv.free)
                    A.wait(*cv.free)
                    tcv = conv(bank[b], t, f"conv{l}", c, cv.ap[:])
                    small[("qkv", c)] = silu2(dst, cv.ap[:], tcv)
                    cv.free = (small[("qkv", c)],)
                    yield
                for c in range(4):
                    b = c % 3
                    t = yield from project(("p", l, 1536 + 128 * c), b)
                    small[("za", c)] = silu2(za[:, c, :], bank[b].ap[:], t)
                    bank[b].free = (small[("za", c)],)
                    yield

            sa = {}

            def phase2():
                for c in range(2):
                    t = yield from project(("p", l, 5128 + 128 * c), c)
                    r, = tmps(1)
                    ta = A.cp(r.ap[:], bank[c].ap[:], t, *r.free)
                    bank[c].free = (ta,)
                    yield
                    sa[("qi", c)] = rope(qi[:, c, :], r.ap[:], C("r64"), TA("cosI"), TA("sinI"), 3, ta)
                    r.free = (sa[("qi", c)],)
                t = yield from project(("ik", l), 2)
                r, r2 = tmps(2)
                ta = A.cp(r.ap[:], bank[2].ap[:], t, *r.free)
                bank[2].free = (ta,)
                yield
                tk = rope(r2.ap[:], r.ap[:], C("r64"), TA("cosI"), TA("sinI"), 3, ta, *())
                r.free = (tk,)
                sa["ki"] = [V.cp(ki[0:64, 0, :], r2.ap[0:64, :], tk), V.cp(ki[64:128, 1, :], r2.ap[64:128, :], tk),
                            V.set(ki[64:128, 0, :], 0.0), V.set(ki[0:64, 1, :], 0.0)]
                r2.free = tuple(sa["ki"])
                for c in range(8):
                    b = c % 3
                    t = yield from project(("p", l, 3080 + 128 * c), b)
                    x1, x2 = tmps(2)
                    tx = A.cp(x1.ap[:], bank[b].ap[:], t, *x1.free)
                    bank[b].free = (tx,)
                    ts_ = A.act(x2.ap[:], x1.ap[:], ACT.Square, 1.0, None, tx, *x2.free)
                    yield
                    tm = PE.mm(bank[3].ap[:], ones, x2.ap[:], True, True, ts_, *bank[3].free, signal=True)
                    tr = rnorm(x2.ap[:], bank[3].ap[:], 1.0 / 128.0, tm)
                    bank[3].free = (tr,)
                    name = f"qn{l}" if c < 4 else f"kn{l}"
                    tq = V.stt(x1.ap[:], x1.ap[:], K(name), x2.ap[:], ALU.mult, ALU.mult, tr, tx)
                    x2.free = (tq,)
                    yield
                    dst = (qs if c < 4 else ks)[:, c % 4, :]
                    sa[("qk", c)] = rope(dst, x1.ap[:], C("r128"), TA("cosA"), TA("sinA"), 3, tq)
                    x1.free = (sa[("qk", c)],)

            def delta():
                for c in range(8):
                    dst = (qf, kf)[c // 4][:, c % 4, :]
                    a, = sts(1)
                    t = A.act(a.ap[:], dst, ACT.Square, 1.0, None, small[("qkv", c)], *a.free)
                    b = bank[4 + c % 4]
                    t = PE.mm(b.ap[:], ones, a.ap[:], True, True, t, *b.free, signal=True)
                    t = rnorm(a.ap[:], b.ap[:], 0.25, t)
                    b.free = (t,)
                    t = V.stt(dst, dst, 0.5 * (128.0 ** -0.5 if c < 4 else 1.0), a.ap[:], ALU.mult, ALU.mult, t)
                    a.free = (t,)
                    small[("n", c)] = t
                    yield
                b = bank[4]
                PE.wait(*small["rw"])
                for i in range(4):
                    t = PE.tr(b.ap[:, 128 * i:128 * i + 128], rw[:, 128 * i:128 * i + 128], ident, *(b.free if i == 0 else ()), signal=i == 3)
                t_c = V.cp(tpc[:].rearrange("p a b -> p (a b)"), b.ap[:], t)
                b.free = (t_c,)
                gc = tpc[:, :, 32:36]
                beta = tpc[:, :, 0:4]
                t_wi = V.cp(wi[:], tpc[:, :, 64:68], t_c)
                sa["wi"] = t_wi
                yield
                b = bank[5]
                last = C("last")
                PE.mm(b.ap[:, 0:16], last, gc, True, True, t_c, *b.free, share=True)
                for p in range(2):
                    sel = ident[:, 63 + 64 * p:64 + 64 * p].broadcast_to([128, 128])
                    t = PE.mm(b.ap[:, 16 + 16 * p:32 + 16 * p], sel, gc, True, True, share=True, signal=p == 1)
                t_gl = A.act(egl[:].rearrange("p a b c -> p (a b c)"), b.ap[:, 16:48], ACT.Exp, 1.0, None, t)
                t1 = V.tt(gcol[:, :, 4:8], b.ap[:, 0:16].rearrange("p (a b) -> p a b", a=4), gc, ALU.subtract, t_gl, t_c)
                b.free = (t_gl, t1)
                t2 = A.act(gcol[:, :, 4:8], gcol[:, :, 4:8], ACT.Exp, 1.0, None, t1)
                t3 = A.act(gcol[:, :, 0:4], gc, ACT.Exp, 1.0, None, t_c)
                t4 = V.tt(gcol[:, :, 0:4], gcol[:, :, 0:4], beta, ALU.mult, t3)
                t5 = V.ts(gcol[:, :, 8:12], beta, 0.5, ALU.mult, None, None, t_c)
                t_col = (t2, t4, t5)
                yield
                f4 = lambda ap: ap.rearrange("p (a b) -> p a b", a=4)
                rec = {}
                for h in range(4):
                    kT, qT = kf[:, h, :], qf[:, h, :]
                    t_k, t_q = small[("n", 4 + h)], small[("n", h)]
                    b4, b5, b6, b7 = bank[4], bank[5], bank[6], bank[7]
                    sel = ident[:, 32 + h:33 + h].broadcast_to([128, 128])
                    tG = PE.mm(b4.ap[:], sel, rw[:], True, True, *b4.free, signal=True)
                    t_eg = A.act(eg[:], b4.ap[:], ACT.Exp, 1.0, None, tG, *rec.get("eg", ()))
                    t_d = V.tt(f4(dT[:]), f4(b4.ap[:]), gc[:, :, h:h + 1].broadcast_to([128, 4, 128]), ALU.subtract, t_eg, *rec.get("dT", ()))
                    b4.free = (t_d, t_eg)
                    t_d = V.tt(f4(dT[:]), f4(dT[:]), C("decay").unsqueeze(1).broadcast_to([128, 4, 128]), ALU.add, t_d)
                    t_d = A.act(dT[:], dT[:], ACT.Exp, 1.0, None, t_d)
                    yield
                    PE.wait(t_k, t_q, *b5.free, *b6.free)
                    for i in range(4):
                        s = slice(128 * i, 128 * i + 128)
                        PE.mm(b5.ap[:, s], kT[:, s], qT[:, s], True, True)
                    for i in range(4):
                        s = slice(128 * i, 128 * i + 128)
                        tkk = PE.mm(b6.ap[:, s], kT[:, s], kT[:, s], True, True, signal=i == 3)
                    for p in range(2):
                        r = slice(64 * p, 64 * p + 64)
                        t_at = V.tt(aT[r, h, :, :], f4(b5.ap[:])[r, :, r], f4(dT[:])[r, :, r], ALU.mult, tkk, t_d)
                    b5.free = (t_at,)
                    t_l = V.tt(lT[:], b6.ap[:], dT[:], ALU.mult, tkk, t_d, *rec.get("lT", ()))
                    b6.free = (t_l,)
                    rec["dT"] = (t_at, t_l)
                    t_qg = V.tt(qT, qT, eg[:], ALU.mult, t_eg, tkk)
                    rec["eg"] = (t_qg,)
                    rec[("q", h)] = t_qg
                    rec[("a", h)] = t_at
                    for i in range(4):
                        s = slice(128 * i, 128 * i + 128)
                        t1 = PE.tr(b7.ap[:, s], kT[:, s], ident, *(b7.free if i == 0 else ()), signal=i == 3)
                    bc = lambda j: gcol[:, :, 4 * j + h:4 * j + h + 1].broadcast_to([128, 4, 128])
                    t_kb = V.tt(f4(kb[:]), f4(b7.ap[:]), bc(0), ALU.mult, t1, *t_col, *rec.get("kb", ()))
                    t_kd = V.tt(kd[:, h, :, :], f4(b7.ap[:]), bc(1), ALU.mult, t1, *t_col)
                    b7.free = (t_kb, t_kd)
                    rec[("kd", h)] = t_kd
                    yield
                    sel = ident[:, h:h + 1].broadcast_to([128, 128])
                    tB = PE.mm(b4.ap[:], sel, rw[:], True, True, *b4.free, signal=True)
                    t_l = V.tt(lT[:], lT[:], b4.ap[:], ALU.mult, tB, t_l)
                    b4.free = (t_l,)
                    for i in range(4):
                        s = slice(128 * i, 128 * i + 128)
                        t1 = PE.tr(b7.ap[:, s], vf[:, h, s], ident, *((small[("qkv", 8 + h)],) + tuple(b7.free) if i == 0 else ()), signal=i == 3)
                    t_vb = V.tt(f4(vb[:]), f4(b7.ap[:]), bc(2), ALU.mult, t1, *rec.get("vb", ()))
                    b7.free = (t_vb,)
                    yield
                    lv = C("levels").rearrange("p (n i) -> p n i", n=6)
                    idb = ident.unsqueeze(1).broadcast_to([128, 4, 128])
                    tX = tXT = None
                    for n in range(6):
                        tm = V.tt(f4(mT[:]), f4(lT[:]), lv[:, n, :].unsqueeze(1).broadcast_to([128, 4, 128]), ALU.mult, t_l, *rec.get("mT", ()))
                        if n == 0:
                            for i in range(4):
                                s = slice(128 * i, 128 * i + 128)
                                t = PE.mm(b4.ap[:, s], mT[:, s], ident, True, True, *((tm,) + tuple(b4.free) if i == 0 else ()), signal=i == 3)
                            tX = V.tt(f4(X[:]), idb, f4(b4.ap[:]), ALU.subtract, t, *rec.get("X", ()))
                            tXT = V.tt(f4(XT[:]), idb, f4(mT[:]), ALU.subtract, tm, *rec.get("XT", ()))
                            b4.free = (tX,)
                            rec["mT"] = (tXT, t)
                            yield
                            continue
                        for i in range(4):
                            s = slice(128 * i, 128 * i + 128)
                            t = PE.mm(b4.ap[:, s], mT[:, s], X[:, s], True, True, *((tm, tX) + tuple(b4.free) if i == 0 else ()), signal=i == 3)
                        rec["mT"] = (t,)
                        tY = A.cp(Y[:], b4.ap[:], t, *rec.get("Y", ()))
                        b4.free = (tY,)
                        yield
                        PE.wait(tY, tXT, *b5.free, *b6.free)
                        for i in range(4):
                            s = slice(128 * i, 128 * i + 128)
                            if n < 5:
                                PE.mm(b5.ap[:, s], XT[:, s], Y[:, s], True, True)
                            t = PE.mm(b6.ap[:, s], Y[:, s], XT[:, s], True, True, signal=i == 3)
                        rec["Y"] = (t,)
                        if n < 5:
                            tX = V.tt(X[:], X[:], b5.ap[:], ALU.subtract, t, tX)
                            b5.free = (tX,)
                        else:
                            rec["X"] = (t,)
                        tXT = V.tt(XT[:], XT[:], b6.ap[:], ALU.subtract, t, tXT)
                        b6.free = (tXT,)
                        yield
                    rec["lT"] = (tm,)
                    PE.wait(tXT, t_kb, t_vb, *b4.free, *b5.free)
                    for i in range(4):
                        s = slice(128 * i, 128 * i + 128)
                        PE.mm(b4.ap[:, s], XT[:, s], vb[:, s], True, True)
                        t = PE.mm(b5.ap[:, s], kb[:, s], XT[:, s], True, True, signal=i == 3)
                    rec["vb"] = rec["kb"] = rec["XT"] = (t,)
                    rec[("u", h)] = A.cp(vf[:, h, :], b4.ap[:], t)
                    b4.free = (rec[("u", h)],)
                    rec[("w", h)] = A.cp(kf[:, h, :], b5.ap[:], t)
                    b5.free = (rec[("w", h)],)
                    yield
                u4 = vf[:].rearrange("p h (b d) -> p h b d", b=4)
                tS = tvn = tPS = t_o = None
                t_hn = V.ts(colx[:, 1:2], K(f"onorm{l}"), 0.5, ALU.mult, None, None, t_lam)
                for n in range(8):
                    i, p = n // 2, n % 2
                    r = slice(64 * p, 64 * p + 64)
                    cs = slice(64 * n, 64 * n + 64)
                    b4 = bank[4]
                    if n > 0:
                        PE.wait(tS, *b4.free, *[rec[("w", h)] for h in range(4)])
                        for h in range(4):
                            t = PE.mm(b4.ap[r, 128 * h:128 * h + 128], kf[:, h, cs], Sx[:, h, :], True, True, signal=h == 3)
                        V.wait(*[rec[("u", h)] for h in range(4)])
                        tvn = V.tt(vn[r, :, :], u4[r, :, i, :], b4.ap[r, :].rearrange("p (h d) -> p h d", h=4), ALU.subtract, t, tPS)
                        b4.free = (tvn,)
                    else:
                        tvn = V.cp(vn[r, :, :], u4[r, :, i, :], *[rec[("u", h)] for h in range(4)])
                    yield
                    ob, Sb = bank[6], bank[7]
                    PE.wait(tvn, *Sb.free, *[rec[("kd", h)] for h in range(4)])
                    for h in range(4):
                        t_s = PE.mm(Sb.ap[:, 128 * h:128 * h + 128], kd[r, h, i, :], vn[r, h, :], True, True, signal=h == 3)
                    PE.wait(*(ob.free if p == 0 else ()), *[rec[("q", h)] for h in range(4)], *[rec[("a", h)] for h in range(4)])
                    for h in range(4):
                        o = ob.ap[:, 128 * h + 64 * p:128 * h + 64 * p + 64]
                        if n > 0:
                            PE.mm(o, Sx[:, h, :], qf[:, h, cs], True, False, share=True)
                        t_o = PE.mm(o, vn[r, h, :], aT[r, h, i, :], n == 0, True, signal=h == 3, share=True)
                    tPS = t_o
                    if n == 0:
                        tS = V.cp(Sx[:].rearrange("p h d -> p (h d)"), Sb.ap[:], t_s)
                    else:
                        e = egl[:, p, i, :].unsqueeze(2).broadcast_to([128, 4, 128])
                        tS = V.tt(Sx[:], Sx[:], e, ALU.mult, t_o, tS, t_gl)
                        tS = V.tt(Sx[:].rearrange("p h d -> p (h d)"), Sx[:].rearrange("p h d -> p (h d)"), Sb.ap[:], ALU.add, t_s, tS)
                    Sb.free = (tS,)
                    if p == 0:
                        yield
                        continue
                    a, o = sts(2)
                    t = A.cp(o.ap[:], ob.ap[:], t_o, *o.free)
                    ob.free = (t,)
                    t = A.act(a.ap[:], o.ap[:], ACT.Square, 1.0, None, t, *a.free)
                    yield
                    b = bank[5]
                    t = PE.mm(b.ap[:], ones, a.ap[:], True, True, t, *b.free, signal=True)
                    t = rnorm(a.ap[:], b.ap[:], 1.0 / 128.0, t)
                    b.free = (t,)
                    t = V.stt(o.ap[:], o.ap[:], colx[:, 1:2], a.ap[:], ALU.mult, ALU.mult, t, t_hn)
                    a.free = (t,)
                    s = slice(128 * i, 128 * i + 128)
                    ov = o.ap[:].rearrange("p (h t) -> p h t", h=4)
                    t = V.tt(za[:, :, s], ov, za[:, :, s], ALU.mult, t, *[small[("za", c)] for c in range(4)])
                    o.free = (t,)
                    small[("yA", i)] = t
                    yield

            dtmp = ExitStack()
            dT, eg, lT, mT, X, XT, Y, kb, vb = [sb(f"{n}{l}", [128, T], stack=dtmp) for n in ("dT", "eg", "lT", "mT", "X", "XT", "Y", "kb", "vb")]
            aT = sb(f"aT{l}", [128, 4, 4, 64], stack=dtmp)
            kd = sb(f"kd{l}", [128, 4, 4, 128], stack=dtmp)
            Sx = sb(f"Sx{l}", [128, 4, 128], stack=dtmp)
            vn = sb(f"vn{l}", [128, 4, 128], stack=dtmp)
            stl = [Slot(sb(f"sd{l}{i}", [128, T], stack=dtmp)) for i in range(2)]
            sno = [0]

            def sts(k):
                out = [stl[(sno[0] + i) % len(stl)] for i in range(k)]
                sno[0] += k
                return out

            for _ in phase1():
                pass
            tap(f"qf{l}", qf[:], V.last(), A.last())
            weave(phase2(), delta(), 1, 2)
            tap(f"yA{l}", za[:], V.last(), A.last())
            barrier()
            dtmp.close()
            dn.close()
            p3 = ExitStack()
            vs = sb(f"vs{l}", [128, 4, 512], stack=p3)
            zc = sb(f"zc{l}", [128, 4, T], stack=p3)
            acc = sb(f"acc{l}", [128, 8, T], stack=p3)
            yh, yl = [sb(f"{n}{l}", [128, 4, T], F32R, stack=p3) for n in ("yh", "yl")]
            sc, bias3 = [sb(f"{n}{l}", [128, T], stack=p3) for n in ("sc", "bias")]
            pw = sb(f"pw{l}", [128, 4, 128], stack=p3)
            m8 = sb(f"m8{l}", [128, 16], stack=p3)
            st2 = sb(f"stat{l}", [128, 8], stack=p3)
            Lx = [Slot(sb(f"Lx{l}{i}", [128, T], stack=p3)) for i in range(2)]
            Px = [Slot(sb(f"Px{l}{i}", [128, 4, 128], stack=p3)) for i in range(2)]
            hb2, = [sb(f"hb{l}", [128, 24], stack=p3)]
            s_pw = sem(f"s_pw{l}")
            S.wait(A.last(), V.last(), PE.last())
            S.dma(pw[:], poolw[l], s_pw)
            t_hb = V.ts(hb2[:], col[:, names[f"gateb{l}"][0]:names[f"gateb{l}"][1]], 0.5, ALU.mult, None, None)
            yt = {}

            def vtok():
                for b in range(4):
                    PE.wait(*bank[b].free)
                for j in range(4):
                    i = take(("v", l, j))
                    for b in range(4):
                        s = slice(128 * b, 128 * b + 128)
                        for kk in range(2):
                            k = 2 * j + kk
                            w = slice(512 * kk, 512 * kk + 512)
                            PE.mm(bank[b].ap[:], hh[:, k, s], wh[i][:, w], k == 0, False)
                            PE.mm(bank[b].ap[:], hl[:, k, s], wh[i][:, w], False, False)
                            t = PE.mm(bank[b].ap[:], hh[:, k, s], wl[i][:, w], False, k == 7, signal=kk == 1)
                        if j == 3:
                            yt[("v", b)] = A.cp(vs[:, b, :], bank[b].ap[:], t)
                            bank[b].free = (yt[("v", b)],)
                    done(i, t)
                    yield

            def pool():
                for g in range(4):
                    t = yield from project(("p", l, 2568 + 128 * g), 0)
                    z, = tmps(1)
                    V.wait(*z.free)
                    tz = silu2(z.ap[:], bank[0].ap[:], t)
                    bank[0].free = (tz,)
                    yield
                    t = yield from project(("p", l, 2056 + 128 * g), 1)
                    p0, p1 = pads(2)
                    tu = A.cp(p0.ap[:, 16:16 + T], bank[1].ap[:], t, *p0.free)
                    bank[1].free = (tu,)
                    u, = tmps(1)
                    t0 = V.cp(u.ap[:], p0.ap[:, 16:16 + T], tu, *u.free)
                    tz0 = V.set(p0.ap[:, 0:16], 0.0, *p0.free)
                    tz1 = V.set(p1.ap[:, 0:16], 0.0, *p1.free)
                    a, b_ = p0, p1
                    tt_ = tz0
                    for n in range(g + 1):
                        s = 2 ** n
                        tt_ = V.tt(b_.ap[:, 16:16 + T], a.ap[:, 16:16 + T], a.ap[:, 16 - s:16 - s + T], ALU.add, tt_, t0, tz1, tu)
                        a, b_ = b_, a
                    win = 2 ** (g + 1)
                    cnt = C("count").rearrange("p (g n) -> p g n", g=4)
                    th = V.tt(m8[:], a.ap[:, 16:32], cnt[:, g, :], ALU.mult, tt_, *yt.get("m8", ()))
                    th = V.tt(m8[:], m8[:], u.ap[:, 0:16], ALU.subtract, th)
                    tp = V.stt(u.ap[:], a.ap[:, 16:16 + T], 1.0 / win, u.ap[:], ALU.mult, ALU.subtract, th)
                    tp = V.cp(u.ap[:, 0:16], m8[:], tp)
                    yt["m8"] = (tp,)
                    p0.free = (tp,)
                    p1.free = (tp,)
                    yield
                    tm = PE.mm(bank[2].ap[:], pw[:, g, :], u.ap[:], True, True, tp, (s_pw, 16), *bank[2].free, signal=True)
                    u.free = (tm,)
                    ty = V.stt(z.ap[:], bank[2].ap[:], K(f"pscale{l}", g), z.ap[:], ALU.mult, ALU.mult, tm, tz)
                    bank[2].free = (ty,)
                    ty = V.ts(z.ap[:], z.ap[:], 0.5, ALU.mult, None, None, ty)
                    th, tl = pair(yh[:, g, :], yl[:, g, :], z.ap[:], ty)
                    z.free = (th, tl)
                    yt[("B", g)] = (th, tl)
                for p in pad:
                    V.wait(*p.free)
                    p.free = (V.set(p.ap[:, 0:3], 0.0),)

            def zproj():
                for c in range(4):
                    t = yield from project(("p", l, 4616 + 128 * c), c % 3)
                    yt[("zc", c)] = silu2(zc[:, c, :], bank[c % 3].ap[:], t)
                    bank[c % 3].free = (yt[("zc", c)],)
                    yield

            def parts(src, toks):
                t_pe = PE.last()
                out = []
                for c in range(4):
                    A.wait(t_pe, *toks)
                    out += pair(yh[:, c, :], yl[:, c, :], src[:, c, :], toks[-1])
                return out

            def merge(n, ytoks, first):
                PE.wait(*ytoks)
                for m in range(8):
                    if m % 2 == 0:
                        ib = take(("br", l, n, m // 2))
                        bb = (0, 1)
                        for mm_ in range(2):
                            PE.wait(*bank[bb[mm_]].free)
                            for k in range(4):
                                w = slice(512 * mm_ + 128 * k, 512 * mm_ + 128 * k + 128)
                                tb = prod3(bank[bb[mm_]].ap[:], ib, w, yh[:, k, :], yl[:, k, :], k == 0, k == 3)
                            yt[("pb", mm_)] = tb
                        done(ib, tb)
                        yield
                    gb = 2 + m % 2
                    t = yield from project(("p", l, 5452 + 1024 * n + 128 * m), gb)
                    g, = tmps(1)
                    tg = A.act(g.ap[:], bank[gb].ap[:], ACT.Tanh, 0.5, hb2[:, 8 * n + m:8 * n + m + 1], t, t_hb, *g.free)
                    bank[gb].free = (tg,)
                    pb = bank[m % 2]
                    if first:
                        ta = V.stt(acc[:, m, :], g.ap[:], 1.0, pb.ap[:], ALU.add, ALU.mult, tg, yt[("pb", m % 2)])
                        g.free = pb.free = (ta,)
                    else:
                        ta = V.stt(g.ap[:], g.ap[:], 1.0, pb.ap[:], ALU.add, ALU.mult, tg, yt[("pb", m % 2)])
                        pb.free = (ta,)
                        ta = V.tt(acc[:, m, :], acc[:, m, :], g.ap[:], ALU.add, ta, yt[("acc", m)])
                        g.free = (ta,)
                    yt[("acc", m)] = ta
                    yield

            def sparse():
                cb = C("causal")
                n_u = 0
                L0 = {}
                for b in range(4):
                    nk = 128 * (b + 1)
                    qsl = slice(128 * b, 128 * b + 128)
                    if b == 0:
                        t_b = V.cp(bias3[:, 0:128], cb[:, 384:512], *L0.get("bias", ()))
                    else:
                        ta = None
                        for h in range(4):
                            bk = bank[4 + h % 2]
                            t = PE.mm(bk.ap[:, 0:nk], qi[:, h // 2, qsl], ki[:, h % 2, 0:nk], True, True, *bk.free, *sa["ki"], sa[("qi", h // 2)], signal=True)
                            r, = [Lx[h % 2]]
                            t = A.act(r.ap[:, 0:nk], bk.ap[:, 0:nk], ACT.Relu, 1.0, None, t, *r.free)
                            bk.free = (t,)
                            if h == 0:
                                ta = V.ts(sc[:, 0:nk], r.ap[:, 0:nk], wi[:, b, 0:1], ALU.mult, None, None, t, sa["wi"], *L0.get("sc", ()))
                            else:
                                ta = V.stt(sc[:, 0:nk], r.ap[:, 0:nk], wi[:, b, h:h + 1], sc[:, 0:nk], ALU.mult, ALU.add, t, ta)
                            r.free = (ta,)
                            yield
                        ta = V.tt(sc[:, nk - 128:nk], sc[:, nk - 128:nk], cb[:, 384:512], ALU.add, ta)
                        for r in range(16):
                            tm = V.max8(m8[:, 0:8], sc[:, 0:nk], ta)
                            ta = V.replace(sc[:, 0:nk], m8[:, 0:8], sc[:, 0:nk], MARK, tm)
                            if r % 4 == 3:
                                yield
                        t_b = V.ts(bias3[:, 0:nk], sc[:, 0:nk], -2.0e38, ALU.is_gt, NEG, ALU.mult, ta, *L0.get("bias", ()))
                        L0["sc"] = (t_b,)
                    ob = bank[7]
                    for h in range(4):
                        bk = bank[4 + n_u % 2]
                        L, P = Lx[n_u % 2], Px[n_u % 2]
                        n_u += 1
                        t = PE.mm(bk.ap[:, 0:nk], qs[:, h, qsl], ks[:, h, 0:nk], True, True, *bk.free, sa[("qk", h)], sa[("qk", 4 + h)], signal=True)
                        mx, sm = st2[:, 2 * (n_u % 2):2 * (n_u % 2) + 1], st2[:, 2 * (n_u % 2) + 1:2 * (n_u % 2) + 2]
                        t = V.addred(L.ap[:, 0:nk], bk.ap[:, 0:nk], bias3[:, 0:nk], -(128.0 ** -0.5), 3.0e38, ALU.min, mx, t, t_b, *L.free)
                        bk.free = (t,)
                        t = A.act(L.ap[:, 0:nk], L.ap[:, 0:nk], ACT.Exp, -1.0, mx, t, acc=sm)
                        tr = V.rec(sm, sm, t)
                        tn = V.ts(L.ap[:, 0:nk], L.ap[:, 0:nk], sm, ALU.mult, None, None, tr, t)
                        yield
                        b6 = bank[6]
                        for i in range(b + 1):
                            t = PE.tr(b6.ap[:, 128 * i:128 * i + 128], L.ap[:, 128 * i:128 * i + 128], ident, *((tn, *b6.free) if i == 0 else ()), signal=i == b)
                        L.free = (t,)
                        tp = A.cp(P.ap[:, 0:b + 1, :].rearrange("p a b -> p (a b)"), b6.ap[:, 0:nk], t, *P.free)
                        b6.free = (tp,)
                        yield
                        PE.wait(tp, *(ob.free if h == 0 else ()), *[yt[("v", i)] for i in range(b + 1)])
                        for i in range(b + 1):
                            t = PE.mm(ob.ap[:, 128 * h:128 * h + 128], vs[:, i, 128 * h:128 * h + 128], P.ap[:, i, :], i == 0, i == b, signal=i == b, share=True)
                        P.free = (t,)
                    L0["bias"] = (V.last(),)
                    ty = V.stt(zc[:, :, qsl], zc[:, :, qsl], 0.5, ob.ap[:].rearrange("p (h t) -> p h t", h=4), ALU.mult, ALU.mult, t, *[yt[("zc", c)] for c in range(4)])
                    ob.free = (ty,)
                    yt[("C", b)] = ty
                    yield

            def front():
                yield from vtok()
                yield from pool()
                yield from zproj()
                yield from merge(1, sum([yt[("B", g)] for g in range(4)], ()), True)
                yield from merge(0, parts(za, [small[("yA", i)] for i in range(4)]), False)

            def after_z():
                while ("zc", 3) not in yt:
                    yield
                yield from sparse()

            weave(front(), after_z(), 1, 2)
            for _ in merge(2, parts(zc, [yt[("C", b)] for b in range(4)]), False):
                pass
            t_h = PE.last()
            mt = []
            for m in range(8):
                ta = V.ts(acc[:, m, :], acc[:, m, :], 0.5, ALU.mult, None, None, yt[("acc", m)])
                th = A.cp(hh[:, m, :], acc[:, m, :], ta, t_h)
                tl = V.tt(hl[:, m, :], acc[:, m, :], hh[:, m, :].bitcast(F32), ALU.subtract, ta, th)
                mt += [th, tl]
            tap(f"acc{l}", acc[:], *mt)
            last = barrier()
            p3.close()
            lay.close()
            xstack = ExitStack()
            xt = sb(f"xt{l}", [128, 8, T], stack=xstack)
            S.wait(*last)
            if l > 0:
                S.wait((s_sc, scn[0]))
            xn[0] += 16
            S.dma(xt[:], x_src, s_x)
            t_x = (s_x, xn[0])
            PE.wait(*mt)
            x_toks = []
            for m in range(8):
                for _ in project(("o", l, m), m % 4):
                    pass
                t = PE.last()
                tx = V.tt(xt[:, m, :], xt[:, m, :], bank[m % 4].ap[:], ALU.add, t, t_x)
                bank[m % 4].free = (tx,)
                x_toks.append(tx)
            A.wait(x_toks[-1])
            A.dma(scratch, xt[:], s_sc)
            scn[0] += 16
            x_src = scratch
            for q in (PE, V, A, G):
                q.wait((s_sc, scn[0]))
            tap(f"x{l}", xt[:], x_toks[-1])

        S.dma(tabs[:, 0:bpack.n], tabB, s_tab, PE.last(), V.last(), A.last())
        for q in (PE, V, A):
            q.wait((s_tab, 32))

        def TB(name):
            a, b = bpack.at[name]
            return tabs[:, a:b]

        norm_into_h(xt, x_toks, "nrmA")
        last = barrier()
        xstack.close()

        b2, comp = ExitStack(), ExitStack()
        q2 = sb("q2", [128, 4, T], stack=b2)
        kz = sb("kz", [128, 4, T], stack=b2)
        vt = sb("vt", [128, 4, 280], stack=b2)
        gs = sb("gs", [128, 4, 24], stack=b2)
        kcz = sb("kcz", [128, 2, 31], stack=b2)
        vcm = sb("vcm", [31, 2, 64], stack=b2)
        onT = sb("onT", [128, 4, T], stack=b2)
        lw = sb("lw", [128, 2, 8, 128], stack=b2)
        lc = sb("lc", [128, 40], stack=b2)
        oh, ol = [sb(n, [128, 8, T], F32R, stack=b2) for n in ("oh", "ol")]
        kc, kg, ph, zt = (sb("kc", [128, T], stack=comp), sb("kg", [128, 2, T], stack=comp),
                          sb("ph", [128, 8, 256], stack=comp), sb("zt", [128, 16, 62], stack=comp))
        vc = sb("vc", [128, T], stack=comp)
        p2 = sb("p2", [128, 2, 2, 64], stack=comp)
        ge = [sb(f"ge{i}", [62, 256], stack=comp) for i in range(3)]
        hid = sb("hid", [128, 2, 62], stack=comp)
        s_lw = sem("s_lw")
        S.wait(*last)
        S.dma(lw[:], lruw, s_lw)
        S.dma(p2[:], phi2, s_lw)
        y2 = {}
        CP = 8.0

        lam = col[:, names["lam"][0]:names["lam"][1]]
        t = A.act(lc[:, 0:8], lam, ACT.Abs, 1.0, None, *last)
        t = A.act(lc[:, 0:8], lc[:, 0:8], ACT.Exp, -1.0, None, t)
        t = A.act(lc[:, 0:8], lc[:, 0:8], ACT.Ln, 1.0, 1.0, t)
        t1 = V.ts(lc[:, 8:16], lam, -1.0, ALU.mult, 0.0, ALU.max, *last)
        t = V.tt(lc[:, 8:16], lc[:, 8:16], lc[:, 0:8], ALU.add, t, t1)
        t = V.ts(lc[:, 8:16], lc[:, 8:16], CP, ALU.mult, None, None, t)
        t = V.ts(lc[:, 0:8], lc[:, 8:16], -1.0, ALU.mult, None, None, t)
        t1 = V.ts(lc[:, 16:24], col[:, names["ba"][0]:names["ba"][1]], 0.5, ALU.mult, None, None, *last)
        t2 = V.ts(lc[:, 24:32], col[:, names["bx"][0]:names["bx"][1]], 0.5, ALU.mult, None, None, *last)
        t_lc = (t, t1, t2)
        t_kz = V.set(kz[:].rearrange("p a b -> p (a b)"), 0.0, *last)
        t_kcz = V.set(kcz[:].rearrange("p a b -> p (a b)"), 0.0, *last)

        def headnorm(x, t, wcol, b, width=T):
            a, = tmps(1)
            t1 = A.act(a.ap[:, 0:width], x, ACT.Square, 1.0, None, t, *a.free)
            yield
            tm = PE.mm(bank[b].ap[:, 0:width], blk, a.ap[:, 0:width], True, True, t1, *bank[b].free, signal=True)
            tr = rnorm(a.ap[:, 0:width], bank[b].ap[:, 0:width], 1.0 / 64.0, tm)
            bank[b].free = (tr,)
            tq = V.stt(x, x, wcol, a.ap[:, 0:width], ALU.mult, ALU.mult, tr, t)
            a.free = (tq,)
            yield
            return tq

        def proj2():
            for c in range(4):
                t = yield from project(("q2", c), c % 3)
                x, = tmps(1)
                t = A.cp(x.ap[:], bank[c % 3].ap[:], t, *x.free)
                bank[c % 3].free = (t,)
                t = yield from headnorm(x.ap[:], t, K("qn2"), 3)
                t = rope(q2[:, c, :], x.ap[:], TB("r16"), TB("cos"), TB("sin"), 3, t)
                x.free = (t,)
                y2[("q", c)] = t
            for j, (at, dst) in enumerate(((512, kc), (640, vc))):
                t = yield from project(("c2", at), j)
                t = A.cp(dst[:], bank[j].ap[:], t)
                bank[j].free = (t,)
                y2[("c", j)] = t
                yield
            for j, at in enumerate((768, 1024)):
                t = yield from project(("c2", at), j)
                x, = tmps(1)
                t = A.cp(x.ap[:], bank[j].ap[:], t, *x.free)
                bank[j].free = (t,)
                t = yield from headnorm(x.ap[:], t, K("kn2", 1 + j), 3)
                r, = tmps(1)
                V.wait(*r.free)
                t = rope(r.ap[:], x.ap[:], TB("r16"), TB("cos"), TB("sin"), 3, t)
                x.free = (t,)
                y2[("k", j)] = [V.cp(kz[64 * g:64 * g + 64, 2 * j + g, :], r.ap[64 * g:64 * g + 64, :], t, t_kz) for g in range(2)]
                r.free = tuple(y2[("k", j)])
            for b in range(4):
                PE.wait(*bank[b].free)
            for j in range(3):
                i = take(("v2", j))
                k0, k1 = 3 * j, min(8, 3 * j + 3)
                for b in range(4):
                    s = slice(128 * b, 128 * b + 128)
                    o = bank[b].ap[:, 0:280]
                    for k in range(k0, k1):
                        w = slice(280 * (k - k0), 280 * (k - k0) + 280)
                        PE.mm(o, hh[:, k, s], wh[i][:, w], k == 0, False)
                        PE.mm(o, hl[:, k, s], wh[i][:, w], False, False)
                        t = PE.mm(o, hh[:, k, s], wl[i][:, w], False, k == 7, signal=k == k1 - 1)
                    if j == 2:
                        t1 = A.cp(vt[:, b, :], o, t)
                        bank[b].free = (t1,)
                        t2 = A.act(gs[:, b, :], vt[:, b, 256:280], ACT.Tanh, 0.5, None, t1)
                        y2[("v", b)] = V.ts(gs[:, b, :], gs[:, b, :], 1.0, ALU.add, 0.5, ALU.mult, t2)
                        y2[("vt", b)] = t1
                done(i, t)
                yield

        def compress():
            s_ph, s_kg = sem("s_ph"), sem("s_kg")
            n_ph = n_kg = 0
            t_ph = t_z = t_h = None
            for j, src in enumerate((kc, vc)):
                A.wait(y2[("c", j)], t_z)
                for g in range(2):
                    r = slice(64 * g, 64 * g + 64)
                    A.dma(kg[0:64, g, :], src[r, :], s_kg)
                    A.dma(kg[64:128, g, 0:T - 1], src[r, 1:T], s_kg)
                n_kg += 64
                pos = col[:, names[("posk", "posv")[j]][0]:names[("posk", "posv")[j]][1]]
                V.wait((s_kg, n_kg), t_h)
                for g in range(2):
                    for f in range(2):
                        view = kg[:, g, 16 * f:16 * f + 496].rearrange("p (n m) -> p m n", m=16)[:, 0:16:2, :]
                        t_z = V.tt(zt[:, 8 * f:8 * f + 8, 31 * g:31 * g + 31], view,
                                   pos[:, 8 * f:8 * f + 8].unsqueeze(2).broadcast_to([128, 8, 31]), ALU.add)
                b = bank[4]
                for f in range(2):
                    A.wait(t_ph)
                    A.dma(ph[:], phi1[j, :, 8 * f:8 * f + 8, :], s_ph)
                    n_ph += 16
                    yield
                    PE.wait(t_z, (s_ph, n_ph), *(b.free if f == 0 else ()))
                    for k in range(8):
                        t_ph = PE.mm(b.ap[0:62, 0:256], zt[:, 8 * f + k, :], ph[:, k, :], f == 0 and k == 0, f == 1 and k == 7, signal=k == 7)
                    yield
                t_h = t_ph
                t = A.cp(ge[0][:], b.ap[0:62, 0:256], t_ph)
                b.free = (t,)
                t1 = A.act(ge[1][:], ge[0][:], ACT.Square, 1.0, None, t)
                t1 = V.ts(ge[1][:], ge[1][:], 0.044715, ALU.mult, 1.0, ALU.add, t1)
                t1 = V.tt(ge[1][:], ge[1][:], ge[0][:], ALU.mult, t1, t)
                t1 = A.act(ge[1][:], ge[1][:], ACT.Tanh, 0.7978845608028654, None, t1)
                t1 = V.stt(ge[2][:], ge[1][:], 1.0, ge[0][:], ALU.add, ALU.mult, t1)
                yield
                b = bank[5]
                for f in range(2):
                    t = PE.tr(b.ap[:, 62 * f:62 * f + 62], ge[2][:, 128 * f:128 * f + 128], ident[0:62, 0:62], *((t1, *b.free) if f == 0 else ()), signal=f == 1)
                t = A.cp(hid[:].rearrange("p a b -> p (a b)"), b.ap[:, 0:124], t)
                b.free = (t,)
                yield
                PE.wait(t, (s_lw, 32), *bank[4].free)
                b = bank[4]
                if j == 0:
                    for g in range(2):
                        for f in range(2):
                            t = PE.mm(b.ap[64 * g:64 * g + 64, 0:31], p2[:, 0, f, :], hid[:, f, 31 * g:31 * g + 31], f == 0, f == 1, signal=f == 1)
                    x, r = tmps(2)
                    t = A.act(x.ap[:, 0:31], b.ap[:, 0:31], ACT.Copy, 0.5, None, t, *x.free)
                    b.free = (t,)
                    t = yield from headnorm(x.ap[:, 0:31], t, K("kn2", 0), 5, 31)
                    V.wait(*r.free)
                    t = rope(r.ap[:, 0:31], x.ap[:, 0:31], TB("r16"), TB("cosC"), TB("sinC"), 5, t, 31)
                    x.free = (t,)
                    y2["kcz"] = [V.cp(kcz[64 * g:64 * g + 64, g, :], r.ap[64 * g:64 * g + 64, 0:31], t, t_kcz) for g in range(2)]
                    r.free = tuple(y2["kcz"])
                else:
                    for g in range(2):
                        for f in range(2):
                            t = PE.mm(b.ap[0:31, 64 * g:64 * g + 64], hid[:, f, 31 * g:31 * g + 31], p2[:, 1, f, :], f == 0, f == 1, signal=f == 1)
                    t = A.act(vcm[:].rearrange("p a b -> p (a b)"), b.ap[0:31, 0:128], ACT.Copy, 0.5, None, t)
                    b.free = (t,)
                    y2["vcm"] = t
                yield

        def nsa():
            cb = C("causal")
            L0 = {}
            n_u = 0
            for b in range(4):
                nk = 128 * (b + 1)
                qsl = slice(128 * b, 128 * b + 128)
                bk = bank[4]
                PE.wait(*bk.free, *y2["kcz"], *[y2[("q", c)] for c in range(4)])
                for h in range(8):
                    t = PE.mm(bk.ap[:, 31 * h:31 * h + 31], q2[:, h % 4, qsl], kcz[:, h // 4, :], True, True, signal=h == 7)
                s3 = sC[:, 0:248].rearrange("p (h n) -> p h n", h=8)
                mask = TB("maskC").rearrange("p (b n) -> p b n", b=4)[:, b, :].unsqueeze(1).broadcast_to([128, 8, 31])
                t = V.tt(s3, bk.ap[:, 0:248].rearrange("p (h n) -> p h n", h=8), mask, ALU.add, t, *L0.get("sC", ()))
                bk.free = (t,)
                mx, sm = stc[:, 0:8], stc[:, 8:16]
                t1 = V.do(lambda e, mx=mx, s3=s3: e.tensor_reduce(mx, s3, AXX, ALU.max), (t,))
                t = V.tt(s3, s3, mx.unsqueeze(2).broadcast_to([128, 8, 31]), ALU.subtract, t1)
                t = A.act(sC[:, 0:248], sC[:, 0:248], ACT.Exp, 0.125, None, t)
                t1 = V.do(lambda e, sm=sm, s3=s3: e.tensor_reduce(sm, s3, AXX, ALU.add), (t,))
                t1 = V.rec(sm, sm, t1)
                t1 = V.tt(sm, sm, gs[:, b, 0:8], ALU.mult, t1, y2[("v", b)])
                t1 = V.ts(sm, sm, TB("validC")[:, b:b + 1], ALU.mult, None, None, t1)
                t = V.tt(s3, s3, sm.unsqueeze(2).broadcast_to([128, 8, 31]), ALU.mult, t1, t)
                yield
                for f in range(2):
                    bk = bank[4 + f]
                    for h in range(4):
                        c0 = 31 * (4 * f + h)
                        t2 = PE.tr(bk.ap[0:31, 128 * h:128 * h + 128], sC[:, c0:c0 + 31], ident, *((t, *bk.free) if h == 0 else ()), signal=h == 3)
                    t3 = A.cp(pC[:, 4 * f:4 * f + 4, :].rearrange("p a b -> p (a b)"), bk.ap[0:31, :], t2, *L0.get("pC", ()))
                    bk.free = (t3,)
                L0["sC"] = (t2,)
                yield
                ob = bank[7]
                for h in range(8):
                    g = h // 4
                    Ps = []
                    for j in range(2):
                        bk = bank[4 + n_u % 2]
                        L, P = Ln2[n_u % 2], Pn2[n_u % 2]
                        m, u = stc[:, 16 + 2 * (n_u % 2):17 + 2 * (n_u % 2)], stc[:, 17 + 2 * (n_u % 2):18 + 2 * (n_u % 2)]
                        n_u += 1
                        t = PE.mm(bk.ap[:, 0:nk], q2[:, h % 4, qsl], kz[:, 2 * j + g, 0:nk], True, True, *bk.free, *y2[("k", j)], signal=True)
                        t = V.addred(L.ap[:, 0:nk], bk.ap[:, 0:nk], cb[:, 384 - 128 * b:512], -0.125, 3.0e38, ALU.min, m, t, *L.free)
                        bk.free = (t,)
                        t = A.act(L.ap[:, 0:nk], L.ap[:, 0:nk], ACT.Exp, -1.0, m, t, acc=u)
                        t1 = V.rec(u, u, t)
                        t1 = V.tt(u, u, gs[:, b, 8 * (j + 1) + h:8 * (j + 1) + h + 1], ALU.mult, t1)
                        tn = V.ts(L.ap[:, 0:nk], L.ap[:, 0:nk], u, ALU.mult, None, None, t1, t)
                        Ps.append((L, P, tn))
                        yield
                    for j in range(2):
                        L, P, tn = Ps[j]
                        b6 = bank[6]
                        for i in range(b + 1):
                            t = PE.tr(b6.ap[:, 128 * i:128 * i + 128], L.ap[:, 128 * i:128 * i + 128], ident, *((tn, *b6.free) if i == 0 else ()), signal=i == b)
                        L.free = (t,)
                        tp = A.cp(P.ap[:, 0:b + 1, :].rearrange("p a b -> p (a b)"), b6.ap[:, 0:nk], t, *P.free)
                        b6.free = (tp,)
                        Ps[j] = (P, tp)
                        yield
                    o = ob.ap[:, 64 * h:64 * h + 64]
                    PE.mm(o, pC[:, h, :], vcm[:, g, :], True, False, t3, y2["vcm"], *(ob.free if h == 0 else ()), share=True)
                    for j in range(2):
                        P, tp = Ps[j]
                        PE.wait(tp, *[y2[("vt", i)] for i in range(b + 1)])
                        for i in range(b + 1):
                            t = PE.mm(o, P.ap[:, i, :], vt[:, i, 128 * j + 64 * g:128 * j + 64 * g + 64], False, j == 1 and i == b, signal=i == b, share=True)
                        P.free = (t,)
                L0["pC"] = (t,)
                L = Ln2[n_u % 2]
                t = A.cp(L.ap[:], ob.ap[:], t, *L.free)
                ob.free = (t,)
                yield
                b6 = bank[6]
                for c in range(4):
                    t1 = PE.tr(b6.ap[:, 128 * c:128 * c + 128], L.ap[:, 128 * c:128 * c + 128], ident, *((t, *b6.free) if c == 0 else ()), signal=c == 3)
                L.free = (t1,)
                t = A.cp(onT[:, :, qsl], b6.ap[:].rearrange("p (c t) -> p c t", c=4), t1)
                b6.free = (t,)
                y2[("o", b)] = t
                yield

        def lru():
            for c in range(8):
                t = yield from project(("c2", 1304 + 128 * c), 0)
                xc, rr, ii, aa = lt
                V.wait(*xc.free)
                A.wait(*xc.free)
                t_xc = conv(bank[0], t, "conv2", c, xc.ap[:], bias=K("convb", c))
                t_y = yield from project(("c2", 2328 + 128 * c), 1)
                PE.mm(bank[2].ap[:], lw[:, 0, c, :], xc.ap[:], True, True, t_xc, (s_lw, 32), *bank[2].free)
                t = PE.mm(bank[3].ap[:], lw[:, 1, c, :], xc.ap[:], True, True, *bank[2].free, *bank[3].free, signal=True)
                t1 = A.act(rr.ap[:], bank[2].ap[:], ACT.Tanh, 0.5, lc[:, 16 + c:17 + c], t, *t_lc, *rr.free)
                bank[2].free = (t1,)
                t1 = V.ts(rr.ap[:], rr.ap[:], 1.0, ALU.add, 0.5, ALU.mult, t1)
                t2 = A.act(ii.ap[:], bank[3].ap[:], ACT.Tanh, 0.5, lc[:, 24 + c:25 + c], t, *ii.free)
                bank[3].free = (t2,)
                t2 = V.stt(ii.ap[:], ii.ap[:], 1.0, xc.ap[:], ALU.add, ALU.mult, t2, t_xc)
                t3 = A.act(aa.ap[:], rr.ap[:], ACT.Exp, lc[:, c:c + 1], None, t1, *aa.free)
                t4 = A.act(rr.ap[:], rr.ap[:], ACT.Tanh, lc[:, 8 + c:9 + c], None, t1, t3)
                t5 = A.act(xc.ap[:], aa.ap[:], ACT.Square, 1.0, None, t3, t2, t)
                g1, g2 = tmps(2)
                t6 = A.cp(g1.ap[:], bank[1].ap[:], t_y, *g1.free)
                bank[1].free = (t6,)
                t7 = A.act(g2.ap[:], g1.ap[:], ACT.Square, 1.0, None, t6, *g2.free)
                t5 = V.stt(rr.ap[:], xc.ap[:], 1.0, rr.ap[:], ALU.add, ALU.mult, t5, t4)
                t5 = V.ts(rr.ap[:], rr.ap[:], 1e-18, ALU.max, None, None, t5)
                t7 = V.ts(g2.ap[:], g2.ap[:], 0.044715, ALU.mult, 1.0, ALU.add, t7)
                t7 = V.tt(g2.ap[:], g2.ap[:], g1.ap[:], ALU.mult, t7, t6)
                t7 = A.act(g2.ap[:], g2.ap[:], ACT.Tanh, 0.7978845608028654, None, t7)
                t5 = A.act(rr.ap[:], rr.ap[:], ACT.Ln, 1.0, None, t5)
                t5 = A.act(rr.ap[:], rr.ap[:], ACT.Exp, 0.5, None, t5)
                t5 = V.stt(ii.ap[:], ii.ap[:], 0.5, rr.ap[:], ALU.mult, ALU.mult, t5, t2)
                rr.free = (t5,)
                t8 = V.scan(xc.ap[:], aa.ap[:], ii.ap[:], 0.0, t5, t3)
                aa.free = ii.free = (t8,)
                t7 = V.stt(g2.ap[:], g2.ap[:], 1.0, g1.ap[:], ALU.add, ALU.mult, t7, t6)
                g1.free = (t7,)
                t8 = V.stt(xc.ap[:], xc.ap[:], 0.5, g2.ap[:], ALU.mult, ALU.mult, t8, t7)
                g2.free = (t8,)
                th, tl = pair(oh[:, c, :], ol[:, c, :], xc.ap[:], t8)
                xc.free = (th, tl)
                y2[("lru", c)] = (th, tl)
                yield

        def merge2():
            PE.wait(*sum([y2[("lru", c)] for c in range(8)], ()))
            for m in range(8):
                t = yield from project(("c2", 4376 + 128 * m), m % 2)
                g, = tmps(1)
                tg = A.act(g.ap[:], bank[m % 2].ap[:], ACT.Tanh, 0.5, None, t, *g.free)
                bank[m % 2].free = (tg,)
                pb = 2 + m % 2
                t = yield from project(("lup", m), pb, oh, ol)
                y2[("acc", m)] = V.stt(acc[:, m, :], g.ap[:], 1.0, bank[pb].ap[:], ALU.add, ALU.mult, tg, t)
                g.free = bank[pb].free = (y2[("acc", m)],)
                yield

        def merge3():
            out = []
            for c in range(4):
                out += pair(yh2[:, c, :], yl2[:, c, :], onT[:, c, :], y2[("o", 3)])
            PE.wait(*out)
            for m in range(8):
                if m % 2 == 0:
                    ib = take(("nup", m // 2))
                    for j in range(2):
                        PE.wait(*bank[j].free)
                        for k in range(4):
                            w = slice(512 * j + 128 * k, 512 * j + 128 * k + 128)
                            t = prod3(bank[j].ap[:], ib, w, yh2[:, k, :], yl2[:, k, :], k == 0, k == 3)
                        y2[("pb", j)] = t
                    done(ib, t)
                gb = 2 + m % 2
                t = yield from project(("c2", 3352 + 128 * m), gb)
                g, = tmps(1)
                tg = A.act(g.ap[:], bank[gb].ap[:], ACT.Tanh, 0.5, None, t, *g.free)
                bank[gb].free = (tg,)
                pb = bank[m % 2]
                ta = V.stt(g.ap[:], g.ap[:], 1.0, pb.ap[:], ALU.add, ALU.mult, tg, y2[("pb", m % 2)])
                pb.free = (ta,)
                ta = V.tt(acc[:, m, :], acc[:, m, :], g.ap[:], ALU.add, ta, y2[("acc", m)])
                g.free = (ta,)
                y2[("acc", m)] = ta

        for _ in proj2():
            pass
        for _ in compress():
            pass
        tap("q2", q2[:], A.last(), V.last())
        last = barrier()
        comp.close()
        m3 = ExitStack()
        acc = sb("acc_2", [128, 8, T], stack=m3)
        lt = [Slot(sb(f"lt{i}", [128, T], stack=m3)) for i in range(4)]
        Ln2 = [Slot(sb(f"Ln{i}", [128, T], stack=m3)) for i in range(2)]
        Pn2 = [Slot(sb(f"Pn{i}", [128, 4, 128], stack=m3)) for i in range(2)]
        sC = sb("sC", [128, 256], stack=m3)
        pC = sb("pC", [31, 8, 128], stack=m3)
        stc = sb("stc", [128, 24], stack=m3)
        yh2, yl2 = oh[:, 0:4, :], ol[:, 0:4, :]

        def mains():
            yield from lru()
            yield from merge2()

        weave(mains(), nsa(), 1, 2)
        tap("nsa", onT[:], A.last(), V.last())
        tap("lru_h", oh[:].bitcast(F32), A.last(), V.last())
        t_pe = PE.last()
        A.wait(t_pe)
        V.wait(t_pe)
        for _ in merge3():
            pass
        t_h = PE.last()
        mt = []
        for m in range(8):
            ta = V.ts(acc[:, m, :], acc[:, m, :], 0.5, ALU.mult, None, None, y2[("acc", m)])
            th = A.cp(hh[:, m, :], acc[:, m, :], ta, t_h)
            tl = V.tt(hl[:, m, :], acc[:, m, :], hh[:, m, :].bitcast(F32), ALU.subtract, ta, th)
            mt += [th, tl]
        last = barrier()
        m3.close()
        b2.close()
        xt = sb("xt_2", [128, 8, T])
        S.wait(*last)
        xn[0] += 16
        S.dma(xt[:], x_src, s_x)
        PE.wait(*mt)
        x_toks = []
        for m in range(8):
            for _ in project(("o2", m), m % 4):
                pass
            tx = V.tt(xt[:, m, :], xt[:, m, :], bank[m % 4].ap[:], ALU.add, PE.last(), (s_x, xn[0]))
            bank[m % 4].free = (tx,)
            x_toks.append(tx)
        norm_into_h(xt, x_toks, "nrmB")
        fh, fl = sb("fh", [128, 16, T], F32R), sb("fl", [128, 16, T], F32R)
        s_o = sem("s_out")
        for half in range(2):
            ft = []
            t_f2 = PE.last()
            for j in range(16):
                for _ in project(("f1", 16 * half + j), j % 4):
                    pass
                r, = tmps(1)
                t = A.act(r.ap[:], bank[j % 4].ap[:], ACT.Relu, 1.0, None, PE.last(), *r.free)
                bank[j % 4].free = (t,)
                t = V.tt(r.ap[:], r.ap[:], r.ap[:], ALU.mult, t)
                th = A.cp(fh[:, j, :], r.ap[:], t, t_f2 if half else None)
                tl = V.tt(fl[:, j, :], r.ap[:], fh[:, j, :].bitcast(F32), ALU.subtract, t, th, t_f2 if half else None)
                r.free = (th, tl)
                ft += [th, tl]
            PE.wait(*ft)
            for m in range(8):
                b = bank[m % 4]
                PE.wait(*b.free)
                for jj in range(2):
                    i = take(("f2", 2 * half + jj, m))
                    for k in range(8):
                        t = prod3(b.ap[:], i, slice(128 * k, 128 * k + 128), fh[:, 8 * jj + k, :], fl[:, 8 * jj + k, :],
                                  jj == 0 and k == 0, jj == 1 and k == 7, signal=k == 7)
                    done(i, t)
                tx = V.tt(xt[:, m, :], xt[:, m, :], b.ap[:], ALU.add, t, x_toks[m])
                b.free = (tx,)
                x_toks[m] = tx
                if half == 1:
                    A.dma(x_out[:, m, :], xt[:, m, :], s_o, tx)
        A.wait((s_o, 16 * 8))
        block = ctx.enter_context(nc.Block())

        @block.sync
        def _(e):
            S.play(e)

        @block.tensor
        def _(e):
            PE.play(e)

        @block.vector
        def _(e):
            V.play(e)

        @block.scalar
        def _(e):
            A.play(e)

        @block.gpsimd
        def _(e):
            G.play(e)


def layouts(I):
    x = np.ascontiguousarray(I["x"][0].reshape(T, 8, 128).transpose(2, 1, 0))
    cpack, apack, bpack = constants(), tables_a(), tables_b()
    return {
        "x": x, "units": pack_units(I), "consts": cpack.array(), "tabA": apack.array(), "tabB": bpack.array(),
        "cols": pack_columns(I), "poolw": np.ascontiguousarray(I["pool_w"].transpose(0, 2, 1, 3)),
        "lruw": np.ascontiguousarray(np.stack([I["lru_wa_2"][0], I["lru_wx_2"][0]]).transpose(2, 0, 1, 3)),
        "phi1": np.ascontiguousarray(np.stack([I["phi_k_w1_2"][0], I["phi_v_w1_2"][0]]).reshape(2, 16, 128, 256).transpose(0, 2, 1, 3)),
        "phi2": np.ascontiguousarray(np.stack([I["phi_k_w2_2"][0], I["phi_v_w2_2"][0]]).reshape(2, 2, 128, 64).transpose(2, 0, 1, 3)),
    }, cpack, apack, bpack


def make(nc, arrays, packs, debug=None):
    ap = {n: nc.dram_tensor(n, list(a.shape), F32, kind="ExternalInput").ap() for n, a in arrays.items()}
    out = nc.dram_tensor("out", [128, 8, T], F32, kind="ExternalOutput").ap()
    build(nc, ap["units"], ap["consts"], ap["tabA"], ap["tabB"], ap["cols"], ap["poolw"], ap["lruw"], ap["phi1"],
          ap["phi2"], ap["x"], out, *packs, debug=debug)


def kernel(**inputs):
    from concourse import bacc
    from concourse.bass_utils import run_bass_kernel_spmd

    arrays, *packs = layouts({k: np.asarray(v) for k, v in inputs.items()})
    nc = bacc.Bacc("TRN2", target_bir_lowering=False, num_devices=1)
    make(nc, arrays, packs)
    r = run_bass_kernel_spmd(nc, [arrays], core_ids=[0])
    y = np.asarray(r.results[0]["out"])
    return np.ascontiguousarray(y.transpose(2, 1, 0).reshape(1, T, D))
```

```python
import math
from contextlib import ExitStack
from itertools import islice

import numpy as np

import concourse.bass as bass
from concourse import mybir

F32 = mybir.dt.float32
F32R = mybir.dt.float32r
ACT = mybir.ActivationFunctionType
ALU = mybir.AluOpType
AXX = mybir.AxisListType.X

T = 512
D = 1024
NK = 8
NEG = -1.0e30
MARK = -3.0e38
EPS = 1e-6
U = 1024
RATES = (0.75, 0.5, 0.4, 1.5)



def plan():
    out = []
    for l in range(2):
        out += [("small", l)]
        out += [("p", l, 128 * c) for c in range(12)]
        out += [("p", l, 5128), ("p", l, 5256), ("ik", l)]
        out += [("p", l, 3080 + 128 * c) for c in range(8)]
        out += [("p", l, 5452 + 1024 * n + 128 * m) for n in (1, 0, 2) for m in range(8)]
        out += [("v", l, j) for j in range(4)]
        out += [("p", l, 1536 + 128 * c) for c in range(4)]
        out += [("p", l, 4616 + 128 * c) for c in range(4)]
        for g in range(4):
            out += [("p", l, 2568 + 128 * g), ("p", l, 2056 + 128 * g)]
        out += [("br", l, n, mp) for n in (1, 0, 2) for mp in range(4)]
        out += [("o", l, m) for m in range(8)]
    out += [("q2", c) for c in range(4)]
    out += [("c2", 512), ("c2", 640), ("c2", 768), ("c2", 1024)]
    out += [("v2", j) for j in range(3)]
    for c in range(8):
        out += [("c2", 1304 + 128 * c), ("c2", 2328 + 128 * c)]
    for m in range(8):
        out += [("c2", 4376 + 128 * m), ("lup", m)]
    for m in range(8):
        if m % 2 == 0:
            out.append(("nup", m // 2))
        out += [("c2", 3352 + 128 * m)]
    out += [("o2", m) for m in range(8)]
    for h in range(2):
        out += [("f1", 16 * h + j) for j in range(16)]
        out += [("f2", 2 * h + jj, m) for m in range(8) for jj in range(2)]
    return out


def q2_columns(c):
    return np.concatenate([np.arange(64 * c, 64 * c + 64), np.arange(64 * (4 + c), 64 * (4 + c) + 64)])


def pack_units(I):
    keys = plan()
    units = np.zeros((len(keys), 128, U), np.float32)

    def kmajor(w):
        k, n = w.shape[0] // 128, w.shape[1]
        return w.reshape(k, 128, n).transpose(1, 0, 2).reshape(128, k * n)

    w2 = I["w_in_2"][0]
    vg = np.concatenate([w2[:, 896:1024], w2[:, 1152:1280], w2[:, 1280:1304]], axis=1)
    for n, key in enumerate(keys):
        kind = key[0]
        if kind == "small":
            u = units[n].reshape(128, 8, 128)
            w = I["w_in"][key[1]]
            for c0, at in ((2048, 0), (2052, 32), (5448, 64)):
                u[:, :, at:at + 4] = kmajor(w[:, c0:c0 + 4]).reshape(128, 8, 4)
        elif kind == "p":
            units[n] = kmajor(I["w_in"][key[1]][:, key[2]:key[2] + 128])
        elif kind == "ik":
            w = I["w_in"][key[1]][:, 5384:5448]
            units[n].reshape(128, 8, 128)[:, :, 0:64] = kmajor(w).reshape(128, 8, 64)
            units[n].reshape(128, 8, 128)[:, :, 64:128] = kmajor(w).reshape(128, 8, 64)
        elif kind == "v":
            j = key[2]
            units[n] = kmajor(I["w_in"][key[1]][256 * j:256 * j + 256, 4104:4616])
        elif kind == "br":
            w = I["w_branch"][key[1], key[2]][:, 256 * key[3]:256 * key[3] + 256]
            units[n] = w.reshape(4, 128, 2, 128).transpose(1, 2, 0, 3).reshape(128, U)
        elif kind == "o":
            units[n] = kmajor(I["w_out"][key[1]][:, 128 * key[2]:128 * key[2] + 128])
        elif kind == "q2":
            units[n] = kmajor(w2[:, q2_columns(key[1])])
        elif kind == "c2":
            units[n] = kmajor(w2[:, key[1]:key[1] + 128])
        elif kind == "v2":
            k0, k1 = 3 * key[1], min(8, 3 * key[1] + 3)
            units[n, :, 0:280 * (k1 - k0)] = kmajor(vg[128 * k0:128 * k1])
        elif kind == "lup":
            units[n] = kmajor(I["w_lru_up_2"][0][:, 128 * key[1]:128 * key[1] + 128])
        elif kind == "nup":
            w = I["w_nsa_up_2"][0][:, 256 * key[1]:256 * key[1] + 256]
            units[n] = w.reshape(4, 128, 2, 128).transpose(1, 2, 0, 3).reshape(128, U)
        elif kind == "o2":
            units[n] = kmajor(I["w_o_2"][0][:, 128 * key[1]:128 * key[1] + 128])
        elif kind == "f1":
            units[n] = kmajor(I["w_ff1_2"][0][:, 128 * key[1]:128 * key[1] + 128])
        elif kind == "f2":
            j, m = key[1], key[2]
            units[n] = kmajor(I["w_ff2_2"][0][1024 * j:1024 * j + 1024, 128 * m:128 * m + 128])
    return units



class Packed:

    def __init__(self):
        self.at, self.parts, self.n = {}, [], 0

    def add(self, name, a):
        a = np.asarray(a, np.float32)
        a = a.reshape(128, -1)
        self.at[name] = (self.n, self.n + a.shape[1])
        self.parts.append(a)
        self.n += a.shape[1]

    def array(self):
        return np.ascontiguousarray(np.concatenate(self.parts, axis=1))


def rope_np(seq, dim, theta):
    inv = theta ** (-np.arange(0, dim, 2, dtype=np.float32) / np.float32(dim))
    ang = np.arange(seq, dtype=np.float32)[:, None] * inv[None, :].astype(np.float32)
    return np.cos(ang).astype(np.float32), np.sin(ang).astype(np.float32)


def constants():
    c = Packed()
    i = np.arange(128)
    c.add("ident", np.eye(128))
    c.add("ones", np.ones((128, 128)))
    c.add("mean", np.full((128, 128), 1.0 / 128.0))
    c.add("blk", (i[:, None] // 64 == i[None, :] // 64))
    same = i[:, None] // 64 == i[None, :] // 64
    c.add("decay", np.where(same & (i[:, None] <= i[None, :]), 0.0, NEG))
    c.add("last", i[:, None] == 64 * (i[None, :] // 64) + 63)
    levels = []
    for n in range(6):
        s = 2 ** n
        j, k = i[:, None], i[None, :]
        levels.append((j // (2 * s) == k // (2 * s)) & (j // s % 2 == 0) & (k // s % 2 == 1))
    c.add("levels", np.stack(levels, 1))
    r128 = np.zeros((128, 128))
    for k in range(64):
        r128[k + 64, k] = -1.0
        r128[k, k + 64] = 1.0
    c.add("r128", r128)
    r64 = np.zeros((128, 128))
    for b in (0, 64):
        for k in range(32):
            r64[b + k + 32, b + k] = -1.0
            r64[b + k, b + k + 32] = 1.0
    c.add("r64", r64)
    reset = np.ones((128, T))
    reset[:, ::64] = 0.0
    c.add("reset", reset)
    cnt = np.zeros((4, 16), np.float32)
    for g, w in enumerate((2, 4, 8, 16)):
        cnt[g] = np.float32(1.0) / np.minimum(np.arange(1, 17), w).astype(np.float32)
    c.add("count", np.broadcast_to(cnt[None], (128, 4, 16)))
    c.add("eps", np.full((128, 1), EPS))
    c.add("causal", np.where((np.arange(512)[None, :] - 384) <= i[:, None], 0.0, NEG))
    return c


def tables_a():
    c = Packed()
    co, si = rope_np(T, 128, 10000.0)
    c.add("cosA", np.concatenate([co.T, co.T]))
    c.add("sinA", np.concatenate([si.T, si.T]))
    co, si = rope_np(T, 64, 10000.0)
    c.add("cosI", np.concatenate([co.T] * 4))
    c.add("sinI", np.concatenate([si.T] * 4))
    return c


def tables_b():
    c = Packed()
    inv = np.float32(500000.0) ** (-np.arange(8, dtype=np.float32) / np.float32(8))
    ang = np.arange(T, dtype=np.float32)[:, None] * inv[None, :]
    co, si = np.ones((128, T), np.float32), np.zeros((128, T), np.float32)
    r = np.zeros((128, 128))
    for b in (0, 64):
        for h in (0, 8):
            co[b + h:b + h + 8] = np.cos(ang).T
            si[b + h:b + h + 8] = np.sin(ang).T
        for k in range(8):
            r[b + k + 8, b + k] = -1.0
            r[b + k, b + k + 8] = 1.0
    c.add("cos", co)
    c.add("sin", si)
    end = 16 * np.arange(31) + 31
    c.add("cosC", co[:, end])
    c.add("sinC", si[:, end])
    c.add("r16", r)
    t = np.arange(128)[:, None, None] + 128 * np.arange(4)[None, :, None]
    c.add("maskC", np.where(end[None, None, :] <= t, 0.0, NEG))
    c.add("validC", (t[:, :, 0] >= 31))
    return c


def column_names():
    at, n = {}, 0
    sizes = []
    for l in range(2):
        sizes += [(f"norm{l}", 8), (f"gateb{l}", 24), (f"conv{l}", 48), (f"alog{l}", 1), (f"dt{l}", 1),
                  (f"onorm{l}", 1), (f"pscale{l}", 4), (f"qn{l}", 1), (f"kn{l}", 1)]
    sizes += [("nrmA", 8), ("nrmB", 8), ("qn2", 1), ("kn2", 3), ("conv2", 32), ("convb", 8), ("ba", 8),
              ("bx", 8), ("lam", 8), ("posk", 16), ("posv", 16)]
    for name, k in sizes:
        at[name] = (n, n + k)
        n += k
    return at, n


def pack_columns(I):
    at, n = column_names()
    c = np.zeros((128, n), np.float32)

    def put(name, a):
        c[:, at[name][0]:at[name][1]] = a

    def chunks(v):
        return v.reshape(-1, 128).T

    for l in range(2):
        put(f"norm{l}", chunks(I["norm_g"][l]))
        put(f"gateb{l}", chunks(I["gate_b"][l].reshape(-1)))
        put(f"conv{l}", I["conv_w"][l].reshape(4, 12, 128).transpose(2, 1, 0).reshape(128, 48))
        c[32:36, at[f"alog{l}"][0]] = I["a_log"][l]
        c[32:36, at[f"dt{l}"][0]] = I["dt_bias"][l]
        put(f"onorm{l}", I["dn_onorm"][l][:, None])
        put(f"pscale{l}", chunks(I["pool_scale"][l]))
        put(f"qn{l}", I["q_norm"][l][:, None])
        put(f"kn{l}", I["k_norm"][l][:, None])
    put("nrmA", chunks(I["norm1_w_2"][0]))
    put("nrmB", chunks(I["norm2_w_2"][0]))
    put("qn2", np.concatenate([I["q_norm_w_2"][0]] * 2)[:, None])
    put("kn2", np.concatenate([I["k_norm_w_2"][0].T] * 2))
    put("conv2", I["conv_w_2"][0].reshape(4, 8, 128).transpose(2, 1, 0).reshape(128, 32))
    put("convb", chunks(I["conv_b_2"][0]))
    put("ba", I["lru_ba_2"][0].T)
    put("bx", I["lru_bx_2"][0].T)
    put("lam", chunks(I["lru_lambda_2"][0]))
    put("posk", I["phi_k_pos_2"][0].reshape(16, 128).T)
    put("posv", I["phi_v_pos_2"][0].reshape(16, 128).T)
    return c



class Queue:

    def __init__(self, sem):
        self.sem, self.n, self.items, self.waited = sem, 0, [], {}

    def wait(self, *tokens):
        for t in tokens:
            if t is None:
                continue
            sem, value = t
            if self.waited.get(sem.name, 0) < value:
                self.waited[sem.name] = value
                self.items.append(lambda e, s=sem, v=value: e.wait_ge(s, v))

    def do(self, f, after=(), signal=True):
        self.wait(*after)
        if not signal:
            self.items.append(f)
            return None
        self.n += 1
        self.items.append(lambda e, s=self.sem: f(e).then_inc(s, 1))
        return (self.sem, self.n)

    def last(self):
        return (self.sem, self.n) if self.n else None

    def dma(self, out, in_, sem, *after):
        self.do(lambda e: e.dma_start(out, in_).then_inc(sem, 16), after, signal=False)

    def play(self, e):
        for f in self.items:
            f(e)


class Vec(Queue):
    def tt(self, out, a, b, op, *after):
        return self.do(lambda e: e.tensor_tensor(out, a, b, op), after)

    def ts(self, out, a, s1, op0, s2, op1, *after):
        if s2 is None:
            return self.do(lambda e: e.tensor_scalar(out, a, s1, None, op0), after)
        return self.do(lambda e: e.tensor_scalar(out, a, s1, s2, op0, op1), after)

    def stt(self, out, a, s, b, op0, op1, *after):
        return self.do(lambda e: e.scalar_tensor_tensor(out=out, in0=a, scalar=s, in1=b, op0=op0, op1=op1), after)

    def cp(self, out, a, *after):
        return self.do(lambda e: e.tensor_copy(out, a), after)

    def set(self, out, v, *after):
        return self.do(lambda e: e.memset(out, v), after)

    def scan(self, out, a, b, initial, *after):
        return self.do(lambda e: e.tensor_tensor_scan(out, a, b, initial, ALU.mult, ALU.add), after)

    def max8(self, out, a, *after):
        return self.do(lambda e: e.max(out, a), after)

    def replace(self, out, vals, a, v, *after):
        return self.do(lambda e: e.match_replace(out, vals, a, v), after)

    def addred(self, out, a, b, scale, init, red, acc, *after):
        return self.do(lambda e: e.tensor_tensor_reduce(out, a, b, scale, init, ALU.add, red, acc), after)

    def rec(self, out, a, *after):
        return self.do(lambda e: e.reciprocal(out, a), after)


class Act(Queue):
    both = False

    def act(self, out, a, func, scale, bias, *after, acc=None):
        if func == ACT.Ln and not self.both:
            self.items.append(lambda e: e.preload_act_table_set("natural_log_exp_and_others"))
        if func in (ACT.Ln, ACT.Tanh):
            self.both = func == ACT.Ln

        def f(e):
            kw = {}
            if bias is not None:
                kw["bias"] = bias
            if acc is not None:
                kw["accum_out"] = acc
            return e.activation(out, a, func, scale=scale, **kw)
        return self.do(f, after)

    def cp(self, out, a, *after):
        return self.do(lambda e: e.activation(out, a, ACT.Copy), after)


class Ten(Queue):
    def mm(self, out, lhsT, rhs, start, stop, *after, signal=False, share=False):
        return self.do(lambda e: e.matmul(out, lhsT, rhs, start=start, stop=stop, skip_group_check=share),
                       after, signal)

    def tr(self, out, a, ident, *after, signal=False):
        return self.do(lambda e: e.transpose(out, a, ident), after, signal)


class Slot:

    def __init__(self, ap):
        self.ap, self.free = ap, ()


def weave(main, *sides):
    sides = [[g, rate, 0.0, True] for g, rate in sides]
    for _ in main:
        for s in sides:
            s[2] += s[1]
            while s[3] and s[2] >= 1.0:
                s[2] -= 1.0
                s[3] = next(s[0], "end") != "end"
    left = [s[0] for s in sides if s[3]]
    while left:
        left = [g for g in left if next(g, "end") != "end"]


def staggered(a, b):
    next(a, None)
    while True:
        x, y = next(b, "end"), next(a, "end")
        if x == "end" and y == "end":
            return
        yield



def build(nc, units, consts, tabA, tabB, cols, poolw, lruw, phi1, phi2, x_in, x_out, cpack, apack, bpack, debug=None):
    keys = plan()
    with ExitStack() as ctx:
        def sb(name, shape, dt=F32, stack=ctx):
            return stack.enter_context(nc.sbuf_tensor(name, shape, dt))

        def sem(name):
            return ctx.enter_context(nc.semaphore(name))

        PE, V, A, G = Ten(sem("s_pe")), Vec(sem("s_dve")), Act(sem("s_act")), Vec(sem("s_pool"))
        S = Queue(sem("s_sp"))

        def fence():
            last = [q.last() for q in (PE, V, A, G)]
            for q in (V, A, G):
                q.wait(*last)
            return last

        bank = [Slot(ctx.enter_context(nc.psum_tensor(f"bank{i}", [128, 512], F32))) for i in range(8)]
        n_cst = cpack.at["causal"][0]
        cst = sb("cst", [128, n_cst])
        col = sb("col", [128, cols.shape[1]])
        colx = sb("colx", [128, 96])
        hh = sb("hh", [128, 8, T], F32R)
        hl = sb("hl", [128, 8, T], F32R)
        tmp = [Slot(sb(f"tmp{i}", [128, T])) for i in range(4)]
        tno = [0]

        def tmps(k):
            out = [tmp[(tno[0] + i) % len(tmp)] for i in range(k)]
            tno[0] = (tno[0] + k) % len(tmp)
            return out

        def C(name):
            a, b = cpack.at[name]
            return cst[:, a:b]

        names, _ = column_names()

        def K(name, i=0, rows=slice(0, 128)):
            return col[rows, names[name][0] + i:names[name][0] + i + 1]

        ident, ones, mean, blk, eps = C("ident"), C("ones"), C("mean"), C("blk"), C("eps")

        s_c = sem("s_consts")
        S.dma(col[:], cols, s_c)
        S.dma(cst[:], consts[:, 0:n_cst], s_c)
        t_const = (s_c, 32)
        for q in (PE, V, A, G):
            q.wait(t_const)

        NS, NH, AHEAD = 3, 3, 3
        stage = [Slot(sb(f"st{i}", [128, U])) for i in range(NS)]
        wh = [sb(f"wh{i}", [128, U], F32R) for i in range(NH)]
        wl = [sb(f"wl{i}", [128, U], F32R) for i in range(NH)]
        s_st = [sem(f"s_st{i}") for i in range(NS)]
        wfree = [None] * NH
        st = {"loaded": 0, "split": 0, "used": 0}
        split_tok = {}

        def load(n):
            s = stage[n % NS]
            S.wait(*s.free)
            S.dma(s.ap[:], units[n], s_st[n % NS])

        def split(n):
            src, i = stage[n % NS], n % NH
            landed = (s_st[n % NS], 16 * (n // NS + 1))
            thi = A.cp(wh[i][:], src.ap[:], landed, wfree[i])
            tlo = G.tt(wl[i][:], src.ap[:], wh[i][:].bitcast(F32), ALU.subtract, thi, landed)
            src.free = (thi, tlo)
            split_tok[n] = (thi, tlo)

        def feed():
            while st["loaded"] < min(st["split"] + NS, len(keys)):
                load(st["loaded"])
                st["loaded"] += 1

        def ahead(n):
            while st["split"] < min(n, len(keys)):
                feed()
                split(st["split"])
                st["split"] += 1
            feed()

        def take(key):
            n = st["used"]
            assert keys[n] == key, (keys[n], key)
            st["used"] += 1
            ahead(n + AHEAD)
            PE.wait(*split_tok.pop(n))
            return n % NH

        def done(i, tok):
            wfree[i] = tok

        def prod3(out, i, wsl, xh, xl, first, last, signal=None):
            PE.mm(out, wh[i][:, wsl], xh, first, False)
            PE.mm(out, wh[i][:, wsl], xl, False, False)
            return PE.mm(out, wl[i][:, wsl], xh, False, last, signal=last if signal is None else signal)

        def project(key, b, xh=None, xl=None, nk=8):
            xh, xl = hh if xh is None else xh, hl if xl is None else xl
            i = take(key)
            PE.wait(*bank[b].free)
            for k in range(nk):
                if xh is hh:
                    PE.wait(*h_tok[k])
                t = prod3(bank[b].ap[:], i, slice(128 * k, 128 * k + 128), xh[:, k, :], xl[:, k, :], k == 0, k == nk - 1)
                if k == 3:
                    yield
            done(i, t)
            return t

        def pair(dst_h, dst_l, src, tok, lo=None):
            th = A.cp(dst_h, src, tok)
            tl = (lo or V).tt(dst_l, src, dst_h.bitcast(F32), ALU.subtract, tok, th)
            return th, tl

        def rnorm(dst, src, *after):
            t1 = A.act(dst, src, ACT.Ln, 1.0, eps, *after)
            return A.act(dst, dst, ACT.Exp, -0.5, None, t1)

        nacc = sb("nacc", [128, T])
        nr = sb("nr", [128, T])
        nm = {"t": None}

        def square(xt, k, tok):
            sq, = tmps(1)
            if k == 0:
                t = A.act(nacc[:], xt[:, k, :], ACT.Square, D ** -0.5, None, tok, nm["t"])
            else:
                t = A.act(sq.ap[:], xt[:, k, :], ACT.Square, D ** -0.5, None, tok, *sq.free)
                t = V.tt(nacc[:], nacc[:], sq.ap[:], ALU.add, t, nm["t"])
                sq.free = (t,)
            nm["t"] = t

        def norm_into_h(xt, gname):
            b = bank[7]
            t = PE.mm(b.ap[:], ones, nacc[:], True, True, nm["t"], *b.free, signal=True)
            nm["t"] = t
            t_r = rnorm(nr[:], b.ap[:], t)
            b.free = (t_r,)
            last = PE.last()
            late = None
            for k in range(8):
                hb, = tmps(1)
                th = V.stt(hb.ap[:], xt[:, k, :], K(gname, k), nr[:], ALU.mult, ALU.mult, t_r, *hb.free)
                t_hi = A.cp(hh[:, k, :], hb.ap[:], th, last)
                if late:
                    late()

                def late(k=k, hb=hb, th=th, t_hi=t_hi):
                    q = G if k % 4 == 3 else V
                    t_lo = q.tt(hl[:, k, :], hb.ap[:], hh[:, k, :].bitcast(F32), ALU.subtract, th, t_hi, last)
                    hb.free = (t_hi, t_lo)
                    h_tok[k] = (t_hi, t_lo)
            late()

        def halve(acc, m, tok, t_h):
            th = A.act(hh[:, m, :], acc[:, m, :], ACT.Copy, 0.5, None, tok, t_h)
            tl = V.stt(hl[:, m, :], acc[:, m, :], 0.5, hh[:, m, :].bitcast(F32), ALU.mult, ALU.subtract, tok, th)
            h_tok[m] = (th, tl)

        h_tok = [()] * 8

        dbg = {}

        def tap(name, ap, *toks):
            if debug is not None and name in debug:
                if "sem" not in dbg:
                    dbg["sem"] = sem("s_dbg")
                dbg["n"] = dbg.get("n", 0) + 16
                A.wait(*toks)
                A.dma(debug[name], ap, dbg["sem"])
                A.wait((dbg["sem"], dbg["n"]))

        s_x = sem("s_x")
        s_x8 = [sem(f"s_x{k}") for k in range(8)]
        xn = [0]
        scratch = nc.dram_tensor("x_scratch", [128, 8, T], F32).ap()
        s_sc = sem("s_scratch")
        scn = [0]

        def spill(dst, slot, t):
            i = tmp.index(slot)
            S.dma(dst, slot.ap[:], s_gd[i], t)
            n_gd[i] += 16
            slot.free = ((s_gd[i], n_gd[i]),)

        def conv(ps, tok, wname, c, dst, bias=None):
            xp, = pads(1)
            t0 = A.cp(xp.ap[:, 3:3 + T], ps.ap[:], tok, *xp.free)
            w = lambda j: K(wname, 4 * c + j)
            t1 = A.act(dst, ps.ap[:], ACT.Identity, w(3), bias if bias is not None else 0.0)
            ps.free = (t1,)
            t = V.stt(dst, xp.ap[:, 2:2 + T], w(2), dst, ALU.mult, ALU.add, t0, t1)
            t = V.stt(dst, xp.ap[:, 1:1 + T], w(1), dst, ALU.mult, ALU.add, t)
            t = V.stt(dst, xp.ap[:, 0:T], w(0), dst, ALU.mult, ALU.add, t)
            xp.free = (t,)
            return t

        pad = [Slot(sb(f"pad{i}", [128, 16 + T])) for i in range(2)]
        pno = [0]
        for p in pad:
            p.free = (V.set(p.ap[:, 0:3], 0.0),)

        def pads(k):
            out = [pad[(pno[0] + i) % 2] for i in range(k)]
            pno[0] += k
            return out

        def silu2(dst, src, tok, *after):
            th, = tmps(1)
            t1 = A.act(th.ap[:], src, ACT.Tanh, 0.5, None, tok, *th.free)
            t2 = V.stt(dst, th.ap[:], 1.0, src, ALU.add, ALU.mult, t1, tok, *after)
            th.free = (t2,)
            return t2

        def rope(dst, src, rot, cos, sin, b, tok, width=T, take_tiles=None):
            t_p = PE.mm(bank[b].ap[:, 0:width], rot, src, True, True, tok, *bank[b].free, signal=True)
            s1, = (take_tiles or tmps)(1)
            t1 = V.tt(s1.ap[:, 0:width], bank[b].ap[:, 0:width], sin, ALU.mult, t_p, *s1.free)
            bank[b].free = (t1,)
            t2 = V.tt(dst, src, cos, ALU.mult, tok, t_p)
            t3 = V.tt(dst, dst, s1.ap[:, 0:width], ALU.add, t1, t2)
            s1.free = (t3,)
            return t3

        tabs = sb("tabs", [128, max(apack.n, bpack.n)])
        xstack = ExitStack()
        xt = sb("xt_in", [128, 8, T], stack=xstack)
        for k in range(8):
            S.dma(xt[:, k, :], x_in[:, k, :], s_x8[k])
            square(xt, k, (s_x8[k], 16))
        feed()
        x_src = x_in
        s_tab = sem("s_tab")
        S.dma(tabs[:, 0:apack.n], tabA, s_tab)
        t_lam = V.set(colx[:], 0.0)
        gates_d = nc.dram_tensor("gates", [24, 128, T], F32).ap()
        s_gd = [sem(f"s_gd{i}") for i in range(4)]
        n_gd = [0] * 4
        qk_d = nc.dram_tensor("qk", [128, 8, T], F32).ap()
        cd_d = consts[:, n_cst:cpack.n]
        s_gl = [sem(f"s_gl{i}") for i in range(3)]
        n_gl = [0] * 3

        for l in range(2):
            def TA(name):
                a, b = apack.at[name]
                return tabs[:, a:b]

            norm_into_h(xt, f"norm{l}")
            ahead(AHEAD)
            fence()
            for q in (V, A, G):
                q.wait((s_sc, scn[0]) if l else None)
            xstack.close()

            lay, dn = ExitStack(), ExitStack()
            yA = sb(f"yA{l}", [128, 4, T], stack=lay)
            bias3 = sb(f"bias{l}", [128, 256 + 384 + 512], stack=lay)
            wi = sb(f"wi{l}", [128, 4, 4], stack=lay)
            qi, ki = [sb(f"{n}i{l}", [128, 2, T], stack=dn) for n in "qk"]
            rw = sb(f"rw{l}", [128, T], stack=dn)
            tpc = sb(f"tpc{l}", [128, 2, 4, 4], stack=dn)
            gcol = sb(f"gcol{l}", [128, 4, 16], stack=dn)
            egl = sb(f"egl{l}", [128, 2, 4, 4], stack=dn)
            qf, kf, vf = [sb(f"{n}f{l}", [128, 4, T], stack=dn) for n in "qkv"]
            hb2 = sb(f"hb{l}", [128, 24], stack=dn)
            t_z = V.set(rw[:], 0.0)
            t_hb = V.ts(hb2[:], col[:, names[f"gateb{l}"][0]:names[f"gateb{l}"][1]], 0.5, ALU.mult, None, None)

            small = {}

            def phase1():
                t = yield from project(("small", l), 0)
                b = bank[0]
                e1, z1 = tmps(2)
                z2, z3 = tmps(2)
                R0, R1, R2 = slice(0, 4), slice(32, 36), slice(64, 68)
                ta = A.act(e1.ap[R0, :], b.ap[R0, :], ACT.Tanh, 0.5, None, t, *e1.free)
                tb = V.ts(rw[R0, :], e1.ap[R0, :], 1.0, ALU.add, 0.5, ALU.mult, ta, t_z)
                e1.free = (tb,)
                tc = V.ts(z1.ap[R1, :], b.ap[R1, :], K(f"dt{l}", 0, R1), ALU.add, None, None, ta, *z1.free)
                td = A.act(z2.ap[R1, :], z1.ap[R1, :], ACT.Abs, 1.0, None, tc, *z2.free)
                te = A.act(z2.ap[R1, :], z2.ap[R1, :], ACT.Exp, -1.0, None, td)
                te = A.act(z2.ap[R1, :], z2.ap[R1, :], ACT.Ln, 1.0, 1.0, te)
                tf = V.stt(z1.ap[R1, :], z1.ap[R1, :], 0.0, z2.ap[R1, :], ALU.max, ALU.add, te, tc)
                z2.free = (tf,)
                tg = A.act(colx[R1, 0:1], K(f"alog{l}", 0, R1), ACT.Exp, 1.0, None, t_lam)
                tf = V.ts(z1.ap[R1, :], z1.ap[R1, :], colx[R1, 0:1], ALU.mult, -1.0, ALU.mult, tf, tg)
                th = V.scan(rw[R1, :], C("reset")[R1, :], z1.ap[R1, :], 0.0, tf, t_z)
                z1.free = (th,)
                ti = V.ts(rw[R2, :], b.ap[R2, :], 1.0 / 16.0, ALU.mult, None, None, ta, t_z)
                b.free = (ta, tc, ti)
                small["rw"] = (tb, th, ti)
                for c in range(12):
                    b = (c + 1) % 3
                    t = yield from project(("p", l, 128 * c), b)
                    dst = (qf, kf, vf)[c // 4][:, c % 4, :]
                    cv, = tmps(1)
                    V.wait(*cv.free)
                    A.wait(*cv.free)
                    tcv = conv(bank[b], t, f"conv{l}", c, cv.ap[:])
                    small[("qkv", c)] = silu2(dst, cv.ap[:], tcv)
                    cv.free = (small[("qkv", c)],)
                    yield
            sa = {}

            def phase2():
                V.wait((s_tab, 16))
                for c in range(2):
                    t = yield from project(("p", l, 5128 + 128 * c), c)
                    r, = tmps(1)
                    ta = A.cp(r.ap[:], bank[c].ap[:], t, *r.free)
                    bank[c].free = (ta,)
                    yield
                    sa[("qi", c)] = rope(qi[:, c, :], r.ap[:], C("r64"), TA("cosI"), TA("sinI"), 3, ta)
                    r.free = (sa[("qi", c)],)
                t = yield from project(("ik", l), 0)
                r, r2 = tmps(2)
                ta = A.cp(r.ap[:], bank[0].ap[:], t, *r.free)
                bank[0].free = (ta,)
                V.wait(*r2.free)
                yield
                tk = rope(r2.ap[:], r.ap[:], C("r64"), TA("cosI"), TA("sinI"), 3, ta)
                r.free = (tk,)
                sa["ki"] = [V.cp(ki[0:64, 0, :], r2.ap[0:64, :], tk), V.cp(ki[64:128, 1, :], r2.ap[64:128, :], tk),
                            V.set(ki[64:128, 0, :], 0.0), V.set(ki[0:64, 1, :], 0.0)]
                r2.free = tuple(sa["ki"])
                for c in range(8):
                    b = c % 2
                    t = yield from project(("p", l, 3080 + 128 * c), b)
                    x1, x2 = tmps(2)
                    tx = A.cp(x1.ap[:], bank[b].ap[:], t, *x1.free)
                    bank[b].free = (tx,)
                    ts_ = A.act(x2.ap[:], x1.ap[:], ACT.Square, 1.0, None, tx, *x2.free)
                    yield
                    tm = PE.mm(bank[3].ap[:], mean, x2.ap[:], True, True, ts_, *bank[3].free, signal=True)
                    tr = rnorm(x2.ap[:], bank[3].ap[:], tm)
                    bank[3].free = (tr,)
                    name = f"qn{l}" if c < 4 else f"kn{l}"
                    tq = V.stt(x1.ap[:], x1.ap[:], K(name), x2.ap[:], ALU.mult, ALU.mult, tr, tx)
                    x2.free = (tq,)
                    yield
                    d, = tmps(1)
                    V.wait(*d.free)
                    t = rope(d.ap[:], x1.ap[:], C("r128"), TA("cosA"), TA("sinA"), 3, tq)
                    x1.free = (t,)
                    spill(qk_d[:, c, :], d, t)

                for j in range(24):
                    n, m = (1, 0, 2)[j // 8], j % 8
                    t = yield from project(("p", l, 5452 + 1024 * n + 128 * m), j % 2)
                    g, = tmps(1)
                    t = A.act(g.ap[:], bank[j % 2].ap[:], ACT.Tanh, 0.5, hb2[:, 8 * n + m:8 * n + m + 1], t, t_hb, *g.free)
                    bank[j % 2].free = (t,)
                    spill(gates_d[8 * n + m], g, t)
                    yield

            def delta():
                for f in range(2):
                    aa = sts(2) + [Slot(XX[0]), Slot(XX[1])]
                    tt_ = []
                    for c in range(4 * f, 4 * f + 4):
                        dst = (qf, kf)[f][:, c % 4, :]
                        a, b = aa[c % 4], bank[4 + c % 4]
                        t = A.act(a.ap[:], dst, ACT.Square, 0.5, None, small[("qkv", c)], *a.free, small.get(("n", c - 4)))
                        tt_.append(PE.mm(b.ap[:], ones, a.ap[:], True, True, t, *b.free, signal=True))
                    yield
                    for c in range(4):
                        tt_[c] = rnorm(aa[c].ap[:], bank[4 + c].ap[:], tt_[c])
                        bank[4 + c].free = (tt_[c],)
                    for c in range(4):
                        dst = (qf, kf)[f][:, c, :]
                        t = V.stt(dst, dst, 0.5 * (1.0 if f else 128.0 ** -0.5), aa[c].ap[:], ALU.mult, ALU.mult, tt_[c])
                        aa[c].free = (t,)
                        small[("n", 4 * f + c)] = t
                    yield
                b = bank[4]
                PE.wait(*small["rw"])
                for i in range(4):
                    t = PE.tr(b.ap[:, 128 * i:128 * i + 128], rw[:, 128 * i:128 * i + 128], ident, *(b.free if i == 0 else ()), signal=i == 3)
                bv = b.ap[:].rearrange("p (a b) -> p a b", a=4)
                gc, beta = tpc[:, 0, :, :], tpc[:, 1, :, :]
                V.cp(gc, bv[:, :, 32:36], t)
                t_c = V.cp(beta, bv[:, :, 0:4])
                t_wi = V.cp(wi[:], bv[:, :, 64:68])
                b.free = (t_wi,)
                sa["wi"] = t_wi
                yield
                b = bank[5]
                last = C("last")
                PE.mm(b.ap[:, 0:16], last, gc, True, True, t_c, *b.free, share=True)
                for p in range(2):
                    sel = ident[:, 63 + 64 * p:64 + 64 * p].broadcast_to([128, 128])
                    t = PE.mm(b.ap[:, 16 + 16 * p:32 + 16 * p], sel, gc, True, True, share=True, signal=p == 1)
                t_gl = A.act(egl[:].rearrange("p a b c -> p (a b c)"), b.ap[:, 16:48], ACT.Exp, 1.0, None, t)
                t1 = V.tt(gcol[:, :, 4:8], b.ap[:, 0:16].rearrange("p (a b) -> p a b", a=4), gc, ALU.subtract, t_gl, t_c)
                b.free = (t_gl, t1)
                t2 = A.act(gcol[:, :, 4:8], gcol[:, :, 4:8], ACT.Exp, 1.0, None, t1)
                t3 = A.act(gcol[:, :, 0:4], gc, ACT.Exp, 1.0, None, t_c)
                t4 = V.tt(gcol[:, :, 0:4], gcol[:, :, 0:4], beta, ALU.mult, t3)
                t5 = V.ts(gcol[:, :, 8:12], beta, 0.5, ALU.mult, None, None, t_c)
                t_col = (t2, t4, t5)
                yield
                f4 = lambda ap: ap.rearrange("p (a b) -> p a b", a=4)
                R, frec = {}, ({}, {})

                def head(h, e):
                    rec = frec[e]
                    lT, mT, Y, X, XT, kb, vb = hset[e]
                    dT, eg = mT, Y
                    kT, qT = kf[:, h, :], qf[:, h, :]
                    t_k, t_q = small[("n", 4 + h)], small[("n", h)]
                    b4, b5, b6, b7 = bank[4 + e], bank[6], bank[7], bank[4 + e]
                    sel = ident[:, 32 + h:33 + h].broadcast_to([128, 128])
                    tG = PE.mm(b4.ap[:], sel, rw[:], True, True, *b4.free, signal=True)
                    t_eg = A.act(eg[:], b4.ap[:], ACT.Exp, 1.0, None, tG, *rec.get("Y", ()))
                    t_d = V.tt(f4(dT[:]), f4(b4.ap[:]), gc[:, :, h:h + 1].broadcast_to([128, 4, 128]), ALU.subtract, t_eg, *rec.get("mT", ()))
                    b4.free = (t_d, t_eg)
                    t_d = V.tt(f4(dT[:]), f4(dT[:]), C("decay").unsqueeze(1).broadcast_to([128, 4, 128]), ALU.add, t_d)
                    t_d = A.act(dT[:], dT[:], ACT.Exp, 1.0, None, t_d)
                    yield
                    PE.wait(t_k, t_q, *b5.free, *b6.free)
                    for i in range(4):
                        s = slice(128 * i, 128 * i + 128)
                        PE.mm(b5.ap[:, s], kT[:, s], qT[:, s], True, True)
                    for i in range(4):
                        s = slice(128 * i, 128 * i + 128)
                        tkk = PE.mm(b6.ap[:, s], kT[:, s], kT[:, s], True, True, signal=i == 3)
                    for p in range(2):
                        r = slice(64 * p, 64 * p + 64)
                        t_at = V.tt(aT[r, h, :, :], f4(b5.ap[:])[r, :, r], f4(dT[:])[r, :, r], ALU.mult, tkk, t_d)
                    b5.free = (t_at,)
                    t_l = V.tt(lT[:], b6.ap[:], dT[:], ALU.mult, tkk, t_d, *rec.get("lT", ()))
                    b6.free = (t_l,)
                    rec["mT"] = (t_at, t_l)
                    t_qg = V.tt(qT, qT, eg[:], ALU.mult, t_eg, tkk)
                    rec["Y"] = (t_qg,)
                    R[("q", h)] = t_qg
                    R[("a", h)] = t_at
                    for i in range(4):
                        s = slice(128 * i, 128 * i + 128)
                        t1 = PE.tr(b7.ap[:, s], kT[:, s], ident, *(b7.free if i == 0 else ()), signal=i == 3)
                    bc = lambda j: gcol[:, :, 4 * j + h:4 * j + h + 1].broadcast_to([128, 4, 128])
                    t_kb = V.tt(f4(kb[:]), f4(b7.ap[:]), bc(0), ALU.mult, t1, *t_col, *rec.get("kb", ()))
                    t_kd = V.tt(kd[:, h, :, :], f4(b7.ap[:]), bc(1), ALU.mult, t1, *t_col)
                    b7.free = (t_kb, t_kd)
                    R[("kd", h)] = t_kd
                    yield
                    sel = ident[:, h:h + 1].broadcast_to([128, 128])
                    tB = PE.mm(b4.ap[:], sel, rw[:], True, True, *b4.free, signal=True)
                    t_l = V.tt(lT[:], lT[:], b4.ap[:], ALU.mult, tB, t_l)
                    b4.free = (t_l,)
                    for i in range(4):
                        s = slice(128 * i, 128 * i + 128)
                        t1 = PE.tr(b7.ap[:, s], vf[:, h, s], ident, *((small[("qkv", 8 + h)],) + tuple(b7.free) if i == 0 else ()), signal=i == 3)
                    t_vb = V.tt(f4(vb[:]), f4(b7.ap[:]), bc(2), ALU.mult, t1, *rec.get("vb", ()))
                    b7.free = (t_vb,)
                    yield
                    lv = C("levels").rearrange("p (n i) -> p n i", n=6)
                    idb = ident.unsqueeze(1).broadcast_to([128, 4, 128])
                    tX = tXT = None
                    for n in range(6):
                        tm = V.tt(f4(mT[:]), f4(lT[:]), lv[:, n, :].unsqueeze(1).broadcast_to([128, 4, 128]), ALU.mult, t_l, *rec.get("mT", ()))
                        if n == 0:
                            for i in range(4):
                                s = slice(128 * i, 128 * i + 128)
                                t = PE.mm(b4.ap[:, s], mT[:, s], ident, True, True, *((tm,) + tuple(b4.free) if i == 0 else ()), signal=i == 3)
                            tX = V.tt(f4(X[:]), idb, f4(b4.ap[:]), ALU.subtract, t, *rec.get("X", ()))
                            tXT = V.tt(f4(XT[:]), idb, f4(mT[:]), ALU.subtract, tm, *rec.get("XT", ()))
                            b4.free = (tX,)
                            rec["mT"] = (tXT, t)
                            yield
                            continue
                        for i in range(4):
                            s = slice(128 * i, 128 * i + 128)
                            t = PE.mm(b4.ap[:, s], mT[:, s], X[:, s], True, True, *((tm, tX) + tuple(b4.free) if i == 0 else ()), signal=i == 3)
                        rec["mT"] = (t,)
                        tY = A.cp(Y[:], b4.ap[:], t, *rec.get("Y", ()))
                        b4.free = (tY,)
                        yield
                        PE.wait(tY, tXT, *b5.free, *b6.free)
                        for i in range(4):
                            s = slice(128 * i, 128 * i + 128)
                            if n < 5:
                                PE.mm(b5.ap[:, s], XT[:, s], Y[:, s], True, True)
                            t = PE.mm(b6.ap[:, s], Y[:, s], XT[:, s], True, True, signal=i == 3)
                        rec["Y"] = (t,)
                        if n < 5:
                            tX = V.tt(X[:], X[:], b5.ap[:], ALU.subtract, t, tX)
                            b5.free = (tX,)
                        else:
                            rec["X"] = (t,)
                        tXT = V.tt(XT[:], XT[:], b6.ap[:], ALU.subtract, t, tXT)
                        b6.free = (tXT,)
                        yield
                    rec["lT"] = (tm,)
                    PE.wait(tXT, t_kb, t_vb, *b4.free, *b5.free)
                    for i in range(4):
                        s = slice(128 * i, 128 * i + 128)
                        PE.mm(b4.ap[:, s], XT[:, s], vb[:, s], True, True)
                        t = PE.mm(b5.ap[:, s], kb[:, s], XT[:, s], True, True, signal=i == 3)
                    rec["vb"] = rec["kb"] = rec["XT"] = (t,)
                    R[("u", h)] = A.cp(vf[:, h, :], b4.ap[:], t)
                    b4.free = (R[("u", h)],)
                    R[("w", h)] = A.cp(kf[:, h, :], b5.ap[:], t)
                    b5.free = (R[("w", h)],)
                    yield
                yield from staggered(head(0, 0), head(1, 1))
                yield from staggered(head(2, 0), head(3, 1))
                rec = R
                u4 = vf[:].rearrange("p h (b d) -> p h b d", b=4)
                tS = tvn = tPS = t_o = None
                t_hn = V.ts(colx[:, 1:2], K(f"onorm{l}"), 0.5, ALU.mult, None, None, t_lam)
                for n in range(8):
                    i, p = n // 2, n % 2
                    r = slice(64 * p, 64 * p + 64)
                    cs = slice(64 * n, 64 * n + 64)
                    b4 = bank[4]
                    if n > 0:
                        PE.wait(tS, *b4.free, *[rec[("w", h)] for h in range(4)])
                        for h in range(4):
                            t = PE.mm(b4.ap[r, 128 * h:128 * h + 128], kf[:, h, cs], Sx[:, h, :], True, True, signal=h == 3)
                        V.wait(*[rec[("u", h)] for h in range(4)])
                        tvn = V.tt(vn[r, :, :], u4[r, :, i, :], b4.ap[r, :].rearrange("p (h d) -> p h d", h=4), ALU.subtract, t, tPS)
                        b4.free = (tvn,)
                    else:
                        tvn = V.cp(vn[r, :, :], u4[r, :, i, :], *[rec[("u", h)] for h in range(4)])
                    yield
                    ob, Sb = bank[6], bank[7]
                    PE.wait(tvn, *Sb.free, *[rec[("kd", h)] for h in range(4)])
                    for h in range(4):
                        t_s = PE.mm(Sb.ap[:, 128 * h:128 * h + 128], kd[r, h, i, :], vn[r, h, :], True, True, signal=h == 3)
                    PE.wait(*(ob.free if p == 0 else ()), *[rec[("q", h)] for h in range(4)], *[rec[("a", h)] for h in range(4)])
                    for h in range(4):
                        o = ob.ap[:, 128 * h + 64 * p:128 * h + 64 * p + 64]
                        if n > 0:
                            PE.mm(o, Sx[:, h, :], qf[:, h, cs], True, False, share=True)
                        t_o = PE.mm(o, vn[r, h, :], aT[r, h, i, :], n == 0, True, signal=h == 3, share=True)
                    tPS = t_o
                    if n == 0:
                        tS = V.cp(Sx[:].rearrange("p h d -> p (h d)"), Sb.ap[:], t_s)
                    else:
                        e = egl[:, p, i, :].unsqueeze(2).broadcast_to([128, 4, 128])
                        tS = V.tt(Sx[:], Sx[:], e, ALU.mult, t_o, tS, t_gl)
                        tS = V.tt(Sx[:].rearrange("p h d -> p (h d)"), Sx[:].rearrange("p h d -> p (h d)"), Sb.ap[:], ALU.add, t_s, tS)
                    Sb.free = (tS,)
                    if p == 1:
                        t = A.cp(yA[:, :, 128 * i:128 * i + 128], ob.ap[:].rearrange("p (h t) -> p h t", h=4), t_o)
                        ob.free = (t,)
                    yield
                aa = sts(2) + [Slot(XX[0]), Slot(XX[1])]
                tt_ = []
                for c in range(4):
                    a, b = aa[c], bank[4 + c]
                    ta = A.act(a.ap[:], yA[:, c, :], ACT.Square, 1.0, None, t, *a.free)
                    tt_.append(PE.mm(b.ap[:], mean, a.ap[:], True, True, ta, *b.free, signal=True))
                yield
                for c in range(4):
                    tt_[c] = rnorm(aa[c].ap[:], bank[4 + c].ap[:], tt_[c])
                    bank[4 + c].free = (tt_[c],)
                for c in range(4):
                    t = V.stt(yA[:, c, :], yA[:, c, :], colx[:, 1:2], aa[c].ap[:], ALU.mult, ALU.mult, tt_[c], t_hn)
                    aa[c].free = (t,)
                    small[("yA", c)] = t
                yield

            dtmp = ExitStack()
            hset = [[sb(f"{n}{e}{l}", [128, T], stack=dtmp) for n in ("lT", "mT", "Y", "X", "XT", "kb", "vb")] for e in range(2)]
            XX = [hset[0][3], hset[1][3]]
            aT = sb(f"aT{l}", [128, 4, 4, 64], stack=dtmp)
            kd = sb(f"kd{l}", [128, 4, 4, 128], stack=dtmp)
            Sx = sb(f"Sx{l}", [128, 4, 128], stack=dtmp)
            vn = sb(f"vn{l}", [128, 4, 128], stack=dtmp)
            stl = [Slot(sb(f"sd{l}{i}", [128, T], stack=dtmp)) for i in range(2)]
            sno = [0]

            def sts(k):
                out = [stl[(sno[0] + i) % 2] for i in range(k)]
                sno[0] += k
                return out

            def select():
                m8, sc = m8s, scs
                ta = None
                for b in range(1, 4):
                    while ("wi" not in sa) or ("ki" not in sa):
                        yield
                    nk = 128 * (b + 1)
                    qsl = slice(128 * b, 128 * b + 128)
                    for h in range(4):
                        bk = bank[2]
                        t = PE.mm(bk.ap[:, 0:nk], qi[:, h // 2, qsl], ki[:, h % 2, 0:nk], True, True, *bk.free, *sa["ki"], sa[("qi", h // 2)], signal=True)
                        t = A.act(bk.ap[:, 0:nk], bk.ap[:, 0:nk], ACT.Relu, 1.0, None, t)
                        yield
                        if h == 0:
                            ta = V.ts(sc[:, 0:nk], bk.ap[:, 0:nk], wi[:, b, 0:1], ALU.mult, None, None, t, sa["wi"], ta)
                        else:
                            ta = V.stt(sc[:, 0:nk], bk.ap[:, 0:nk], wi[:, b, h:h + 1], sc[:, 0:nk], ALU.mult, ALU.add, t, ta)
                        bk.free = (ta,)
                    ta = V.tt(sc[:, nk - 128:nk], sc[:, nk - 128:nk], cdiag[:], ALU.add, ta, t_cd)
                    for r in range(16):
                        tm = V.max8(m8[:, 0:8], sc[:, 0:nk], ta)
                        ta = V.replace(sc[:, 0:nk], m8[:, 0:8], sc[:, 0:nk], MARK, tm)
                        if r % 2 == 1:
                            yield
                    o = (0, 0, 256, 640)[b]
                    ta = V.ts(bias3[:, o:o + nk], sc[:, 0:nk], -2.0e38, ALU.is_gt, NEG, ALU.mult, ta)
                    sa[("sel", b)] = ta
                    yield

            m8s = sb(f"m8s{l}", [128, 8], stack=dtmp)
            scs = sb(f"scs{l}", [128, T], stack=dtmp)
            cdiag = sb(f"cdiag{l}", [128, 128], stack=dtmp)
            s_cd = sem(f"s_cd{l}")
            S.wait(V.last(), A.last())
            S.dma(cdiag[:], cd_d[:, 384:512], s_cd)
            t_cd = (s_cd, 16)
            for _ in phase1():
                pass
            tap(f"qf{l}", qf[:], V.last(), A.last())
            weave(phase2(), (delta(), RATES[0]), (select(), RATES[1]))
            tap(f"yA{l}", yA[:], V.last(), A.last())
            fence()
            dtmp.close()
            dn.close()
            p3 = ExitStack()
            qs, ks, vs, zc = [sb(f"{n}{l}", [128, 4, T], stack=p3) for n in ("qs", "ks", "vs", "zc")]
            acc = sb(f"acc{l}", [128, 8, T], stack=p3)
            yh, yl = [sb(f"{n}{l}", [128, 4, T], F32R, stack=p3) for n in ("yh", "yl")]
            cdg = sb(f"cdg{l}", [128, 128], stack=p3)
            pw = sb(f"pw{l}", [128, 4, 128], stack=p3)
            m8 = sb(f"m8{l}", [128, 16], stack=p3)
            st2 = sb(f"stat{l}", [128, 8], stack=p3)
            Lx = [Slot(sb(f"Lx{l}{i}", [128, T], stack=p3)) for i in range(3)]
            Px = [Slot(sb(f"Px{l}{i}", [128, 4, 128], stack=p3)) for i in range(2)]
            gt = [Slot(sb(f"gt{l}{i}", [128, T], stack=p3)) for i in range(3)]
            s_pw = sem(f"s_pw{l}")
            S.wait(A.last(), V.last(), PE.last(), *[(s_gd[i], n_gd[i]) for i in range(4)])
            S.dma(pw[:], poolw[l], s_pw)
            S.dma(cdg[:], cd_d[:, 384:512], s_pw)
            S.dma(qs[:], qk_d[:, 0:4, :], s_pw)
            S.dma(ks[:], qk_d[:, 4:8, :], s_pw)
            t_pw = (s_pw, 64)
            yt = {}
            order = [8 * n + m for n in (1, 0, 2) for m in range(8)]
            gq = {"n": 0}

            def gate_loads(upto):
                while gq["n"] < min(upto, 24):
                    j = gq["n"]
                    g = gt[j % 3]
                    S.dma(g.ap[:], gates_d[order[j]], s_gl[j % 3], *g.free)
                    n_gl[j % 3] += 16
                    g.tok = (s_gl[j % 3], n_gl[j % 3])
                    gq["n"] += 1

            gate_loads(3)

            def vtok():
                for b in range(4):
                    PE.wait(*bank[b].free)
                for j in range(4):
                    i = take(("v", l, j))
                    for b in range(4):
                        s = slice(128 * b, 128 * b + 128)
                        for kk in range(2):
                            k = 2 * j + kk
                            w = slice(512 * kk, 512 * kk + 512)
                            PE.mm(bank[b].ap[:], hh[:, k, s], wh[i][:, w], k == 0, False)
                            PE.mm(bank[b].ap[:], hl[:, k, s], wh[i][:, w], False, False)
                            t = PE.mm(bank[b].ap[:], hh[:, k, s], wl[i][:, w], False, k == 7, signal=kk == 1)
                        if j == 3:
                            yt[("v", b)] = A.cp(vs[:, b, :], bank[b].ap[:], t)
                            bank[b].free = (yt[("v", b)],)
                    done(i, t)
                    yield

            def pool():
                for g in range(4):
                    t = yield from project(("p", l, 2568 + 128 * g), 0)
                    z, = tmps(1)
                    V.wait(*z.free)
                    tz = silu2(z.ap[:], bank[0].ap[:], t)
                    bank[0].free = (tz,)
                    yield
                    t = yield from project(("p", l, 2056 + 128 * g), 1)
                    p0, p1 = pads(2)
                    tu = A.cp(p0.ap[:, 16:16 + T], bank[1].ap[:], t, *p0.free)
                    bank[1].free = (tu,)
                    u, = tmps(1)
                    t0 = V.cp(u.ap[:], p0.ap[:, 16:16 + T], tu, *u.free)
                    tz0 = V.set(p0.ap[:, 0:16], 0.0, *p0.free)
                    tz1 = V.set(p1.ap[:, 0:16], 0.0, *p1.free)
                    a, b_ = p0, p1
                    tt_ = tz0
                    for n in range(g + 1):
                        s = 2 ** n
                        tt_ = V.tt(b_.ap[:, 16:16 + T], a.ap[:, 16:16 + T], a.ap[:, 16 - s:16 - s + T], ALU.add, tt_, t0, tz1, tu)
                        a, b_ = b_, a
                    win = 2 ** (g + 1)
                    cnt = C("count").rearrange("p (g n) -> p g n", g=4)
                    th = V.tt(m8[:], a.ap[:, 16:32], cnt[:, g, :], ALU.mult, tt_, *yt.get("m8", ()))
                    th = V.tt(m8[:], m8[:], u.ap[:, 0:16], ALU.subtract, th)
                    tp = V.stt(u.ap[:], a.ap[:, 16:16 + T], 1.0 / win, u.ap[:], ALU.mult, ALU.subtract, th)
                    tp = V.cp(u.ap[:, 0:16], m8[:], tp)
                    yt["m8"] = (tp,)
                    p0.free = (tp,)
                    p1.free = (tp,)
                    yield
                    tm = PE.mm(bank[2].ap[:], pw[:, g, :], u.ap[:], True, True, tp, t_pw, *bank[2].free, signal=True)
                    u.free = (tm,)
                    ty = V.stt(z.ap[:], bank[2].ap[:], K(f"pscale{l}", g), z.ap[:], ALU.mult, ALU.mult, tm, tz)
                    bank[2].free = (ty,)
                    ty = V.ts(z.ap[:], z.ap[:], 0.5, ALU.mult, None, None, ty)
                    th, tl = pair(yh[:, g, :], yl[:, g, :], z.ap[:], ty)
                    z.free = (th, tl)
                    yt[("B", g)] = (th, tl)
                for p in pad:
                    V.wait(*p.free)
                    p.free = (V.set(p.ap[:, 0:3], 0.0),)

            def zproj():
                for c in range(4):
                    t = yield from project(("p", l, 1536 + 128 * c), c % 3)
                    z, = tmps(1)
                    t = silu2(z.ap[:], bank[c % 3].ap[:], t, *z.free)
                    bank[c % 3].free = (t,)
                    yt[("A", c)] = V.tt(yA[:, c, :], yA[:, c, :], z.ap[:], ALU.mult, t, small[("yA", c)])
                    z.free = (yt[("A", c)],)
                    yield
                for c in range(4):
                    t = yield from project(("p", l, 4616 + 128 * c), c % 3)
                    yt[("zc", c)] = silu2(zc[:, c, :], bank[c % 3].ap[:], t)
                    bank[c % 3].free = (yt[("zc", c)],)
                    yield

            def parts(src, toks):
                t_pe = PE.last()
                out = []
                for c in range(4):
                    A.wait(t_pe, *toks)
                    out += pair(yh[:, c, :], yl[:, c, :], src[:, c, :], toks[-1])
                return out

            def merge(n, ytoks):
                t_h = PE.last()
                for c in range(4):
                    PE.wait(*ytoks[2 * c:2 * c + 2])
                for mp in range(4):
                    ib = take(("br", l, n, mp))
                    for j in range(2):
                        m = 2 * mp + j
                        b = bank[m % 4]
                        PE.wait(*b.free)
                        for k in range(4):
                            w = slice(512 * j + 128 * k, 512 * j + 128 * k + 128)
                            tb = prod3(b.ap[:], ib, w, yh[:, k, :], yl[:, k, :], k == 0, k == 3)
                        if j == 1:
                            done(ib, tb)
                        i = order.index(8 * n + m)
                        gate_loads(i + 1)
                        g = gt[i % 3]
                        if n == 1:
                            ta = V.stt(acc[:, m, :], g.ap[:], 1.0, b.ap[:], ALU.add, ALU.mult, g.tok, tb)
                            b.free = (ta,)
                        else:
                            ta = V.stt(g.ap[:], g.ap[:], 1.0, b.ap[:], ALU.add, ALU.mult, g.tok, tb)
                            b.free = (ta,)
                            ta = V.tt(acc[:, m, :], acc[:, m, :], g.ap[:], ALU.add, ta, yt[("acc", m)])
                        g.free = (ta,)
                        gate_loads(i + 4)
                        yt[("acc", m)] = ta
                        if n == 2:
                            halve(acc, m, ta, t_h)
                        yield

            def sparse():
                u = [(b, h) for b in range(4) for h in range(4)]
                while ("zc", 3) not in yt:
                    yield
                t_sc, t_p = {}, {}
                for n in range(len(u) + 2):
                    if n >= 2:
                        b, h = u[n - 2]
                        ob, P = bank[7], Px[n % 2]
                        PE.wait(t_p[n - 2], *(ob.free if h == 0 else ()), *[yt[("v", i)] for i in range(b + 1)])
                        for i in range(b + 1):
                            t = PE.mm(ob.ap[:, 128 * h:128 * h + 128], vs[:, i, 128 * h:128 * h + 128], P.ap[:, i, :], i == 0, i == b, signal=i == b, share=True)
                        P.free = (t,)
                        if h == 3:
                            q = slice(128 * b, 128 * b + 128)
                            t = V.stt(zc[:, :, q], zc[:, :, q], 0.5, ob.ap[:].rearrange("p (h t) -> p h t", h=4), ALU.mult, ALU.mult, t, *[yt[("zc", c)] for c in range(4)])
                            ob.free = (t,)
                            yt[("C", b)] = t
                    if 1 <= n <= len(u):
                        b, h = u[n - 1]
                        bk, L, P = bank[4 + (n - 1) % 3], Lx[(n - 1) % 3], Px[(n - 1) % 2]
                        for i in range(b + 1):
                            t = PE.tr(bk.ap[:, 128 * i:128 * i + 128], L.ap[:, 128 * i:128 * i + 128], ident, *((t_sc[n - 1], *bk.free) if i == 0 else ()), signal=i == b)
                        L.free = (t,)
                        t_p[n - 1] = A.cp(P.ap[:, 0:b + 1, :].rearrange("p a b -> p (a b)"), bk.ap[:, 0:128 * (b + 1)], t, *P.free)
                        bk.free = (t_p[n - 1],)
                    if n < len(u):
                        b, h = u[n]
                        nk = 128 * (b + 1)
                        bk, L = bank[4 + n % 3], Lx[n % 3]
                        t = PE.mm(bk.ap[:, 0:nk], qs[:, h, 128 * b:128 * b + 128], ks[:, h, 0:nk], True, True, *bk.free, t_pw, signal=True)
                        mx, sm = st2[:, 2 * (n % 3):2 * (n % 3) + 1], st2[:, 2 * (n % 3) + 1:2 * (n % 3) + 2]
                        o = (0, 0, 256, 640)[b]
                        bias, t_b = (cdg[:], t_pw) if b == 0 else (bias3[:, o:o + nk], sa[("sel", b)])
                        t = V.addred(L.ap[:, 0:nk], bk.ap[:, 0:nk], bias, -(128.0 ** -0.5), 3.0e38, ALU.min, mx, t, t_b, *L.free)
                        bk.free = (t,)
                        t = A.act(L.ap[:, 0:nk], L.ap[:, 0:nk], ACT.Exp, -1.0, mx, t, acc=sm)
                        tr = V.rec(sm, sm, t)
                        t_sc[n] = V.ts(L.ap[:, 0:nk], L.ap[:, 0:nk], sm, ALU.mult, None, None, tr, t)
                    yield

            def front():
                yield from vtok()
                yield from zproj()
                yield from pool()
                yield from merge(1, sum([yt[("B", g)] for g in range(4)], ()))
                yield from merge(0, parts(yA, [yt[("A", c)] for c in range(4)]))

            weave(front(), (sparse(), RATES[2]))
            for _ in merge(2, parts(zc, [yt[("C", b)] for b in range(4)])):
                pass
            last = fence()
            p3.close()
            lay.close()
            xstack = ExitStack()
            xt = sb(f"xt{l}", [128, 8, T], stack=xstack)
            S.wait(*last)
            if l > 0:
                S.wait((s_sc, scn[0]))
            xn[0] += 16
            S.dma(xt[:], x_src, s_x)
            t_x = (s_x, xn[0])
            x_toks = []
            for m in range(8):
                for _ in project(("o", l, m), m % 4):
                    pass
                t = PE.last()
                tx = V.tt(xt[:, m, :], xt[:, m, :], bank[m % 4].ap[:], ALU.add, t, t_x)
                bank[m % 4].free = (tx,)
                x_toks.append(tx)
                square(xt, m, tx)
            S.dma(scratch, xt[:], s_sc, x_toks[-1])
            scn[0] += 16
            x_src = scratch
            tap(f"x{l}", xt[:], x_toks[-1])

        S.dma(tabs[:, 0:bpack.n], tabB, s_tab, PE.last(), V.last(), A.last())
        for q in (PE, V, A):
            q.wait((s_tab, 32))

        def TB(name):
            a, b = bpack.at[name]
            return tabs[:, a:b]

        norm_into_h(xt, "nrmA")
        last = fence()
        for q in (V, A, G, S):
            q.wait((s_sc, scn[0]))
        xstack.close()

        b2, comp = ExitStack(), ExitStack()
        q2 = sb("q2", [128, 4, T], stack=b2)
        kz = sb("kz", [128, 4, T], stack=b2)
        vt = sb("vt", [128, 4, 280], stack=b2)
        gs = sb("gs", [128, 4, 24], stack=b2)
        kcz = sb("kcz", [128, 2, 31], stack=b2)
        vcm = sb("vcm", [31, 2, 64], stack=b2)
        onT = sb("onT", [128, 4, T], stack=b2)
        lw = [Slot(sb(f"lw{i}", [128, 2, 128], stack=b2)) for i in range(2)]
        s_lr = [sem(f"s_lr{i}") for i in range(2)]
        cau = sb("cau", [128, 512], stack=b2)
        lc = sb("lc", [128, 40], stack=b2)
        oh, ol = [sb(n, [128, 8, T], F32R, stack=b2) for n in ("oh", "ol")]
        lt = [Slot(sb(f"lt{i}", [128, T], stack=b2)) for i in range(4)]
        kc, kg, ph, zt = (sb("kc", [128, T], stack=comp), sb("kg", [128, 2, T], stack=comp),
                          sb("ph", [128, 8, 256], stack=comp), sb("zt", [128, 16, 62], stack=comp))
        vc = sb("vc", [128, T], stack=comp)
        p2 = sb("p2", [128, 2, 2, 64], stack=comp)
        ge = [sb(f"ge{i}", [62, 256], stack=comp) for i in range(3)]
        hid = sb("hid", [128, 2, 62], stack=comp)
        ctile = [Slot(sb(f"ctile{i}", [128, 32], stack=comp)) for i in range(4)]
        cno = [0]

        def ctiles(k):
            cno[0] += k
            return [ctile[(cno[0] - k + i) % 4] for i in range(k)]

        s_lw = sem("s_lw")
        S.wait(*last)
        for c in range(2):
            S.dma(lw[c].ap[:], lruw[:, :, c, :], s_lr[c])
        S.dma(p2[:], phi2, s_lw)
        S.dma(cau[:], cd_d, s_lw)
        y2 = {}
        CP = 8.0

        lam = col[:, names["lam"][0]:names["lam"][1]]
        t = A.act(lc[:, 0:8], lam, ACT.Abs, 1.0, None, *last)
        t = A.act(lc[:, 0:8], lc[:, 0:8], ACT.Exp, -1.0, None, t)
        t = A.act(lc[:, 0:8], lc[:, 0:8], ACT.Ln, 1.0, 1.0, t)
        t1 = V.ts(lc[:, 8:16], lam, -1.0, ALU.mult, 0.0, ALU.max, *last)
        t = V.tt(lc[:, 8:16], lc[:, 8:16], lc[:, 0:8], ALU.add, t, t1)
        t = V.ts(lc[:, 8:16], lc[:, 8:16], CP, ALU.mult, None, None, t)
        t = V.ts(lc[:, 0:8], lc[:, 8:16], -1.0, ALU.mult, None, None, t)
        t1 = V.ts(lc[:, 16:24], col[:, names["ba"][0]:names["ba"][1]], 0.5, ALU.mult, None, None, *last)
        t2 = V.ts(lc[:, 24:32], col[:, names["bx"][0]:names["bx"][1]], 0.5, ALU.mult, None, None, *last)
        t_lc = (t, t1, t2)
        t_kz = V.set(kz[:].rearrange("p a b -> p (a b)"), 0.0, *last)
        t_kcz = V.set(kcz[:].rearrange("p a b -> p (a b)"), 0.0, *last)

        def headnorm(x, t, wcol, b, width=T, take_tiles=None):
            a, = (take_tiles or tmps)(1)
            t1 = A.act(a.ap[:, 0:width], x, ACT.Square, 0.125, None, t, *a.free)
            yield
            tm = PE.mm(bank[b].ap[:, 0:width], blk, a.ap[:, 0:width], True, True, t1, *bank[b].free, signal=True)
            tr = rnorm(a.ap[:, 0:width], bank[b].ap[:, 0:width], tm)
            bank[b].free = (tr,)
            tq = V.stt(x, x, wcol, a.ap[:, 0:width], ALU.mult, ALU.mult, tr, t)
            a.free = (tq,)
            yield
            return tq

        def proj2():
            for c in range(4):
                t = yield from project(("q2", c), c % 3)
                x, = tmps(1)
                t = A.cp(x.ap[:], bank[c % 3].ap[:], t, *x.free)
                bank[c % 3].free = (t,)
                t = yield from headnorm(x.ap[:], t, K("qn2"), 3)
                t = rope(q2[:, c, :], x.ap[:], TB("r16"), TB("cos"), TB("sin"), 3, t)
                x.free = (t,)
                y2[("q", c)] = t
            for j, (at, dst) in enumerate(((512, kc), (640, vc))):
                t = yield from project(("c2", at), j)
                t = A.cp(dst[:], bank[j].ap[:], t)
                bank[j].free = (t,)
                y2[("c", j)] = t
                yield
            for j, at in enumerate((768, 1024)):
                t = yield from project(("c2", at), j)
                x, = tmps(1)
                t = A.cp(x.ap[:], bank[j].ap[:], t, *x.free)
                bank[j].free = (t,)
                t = yield from headnorm(x.ap[:], t, K("kn2", 1 + j), 3)
                r, = tmps(1)
                V.wait(*r.free)
                t = rope(r.ap[:], x.ap[:], TB("r16"), TB("cos"), TB("sin"), 3, t)
                x.free = (t,)
                y2[("k", j)] = [V.cp(kz[64 * g:64 * g + 64, 2 * j + g, :], r.ap[64 * g:64 * g + 64, :], t, t_kz) for g in range(2)]
                r.free = tuple(y2[("k", j)])
            for b in range(4):
                PE.wait(*bank[b].free)
            for j in range(3):
                i = take(("v2", j))
                k0, k1 = 3 * j, min(8, 3 * j + 3)
                for b in range(4):
                    s = slice(128 * b, 128 * b + 128)
                    o = bank[b].ap[:, 0:280]
                    for k in range(k0, k1):
                        w = slice(280 * (k - k0), 280 * (k - k0) + 280)
                        PE.mm(o, hh[:, k, s], wh[i][:, w], k == 0, False)
                        PE.mm(o, hl[:, k, s], wh[i][:, w], False, False)
                        t = PE.mm(o, hh[:, k, s], wl[i][:, w], False, k == 7, signal=k == k1 - 1)
                    if j == 2:
                        t1 = A.cp(vt[:, b, :], o, t)
                        bank[b].free = (t1,)
                        t2 = A.act(gs[:, b, :], vt[:, b, 256:280], ACT.Tanh, 0.5, None, t1)
                        y2[("v", b)] = V.ts(gs[:, b, :], gs[:, b, :], 1.0, ALU.add, 0.5, ALU.mult, t2)
                        y2[("vt", b)] = t1
                done(i, t)
                yield

        def compress():
            s_ph, s_kg = sem("s_ph"), sem("s_kg")
            n_ph = n_kg = 0
            t_ph = t_z = t_h = None
            for j, src in enumerate((kc, vc)):
                A.wait(y2[("c", j)], t_z)
                for g in range(2):
                    r = slice(64 * g, 64 * g + 64)
                    A.dma(kg[0:64, g, :], src[r, :], s_kg)
                    A.dma(kg[64:128, g, 0:T - 1], src[r, 1:T], s_kg)
                n_kg += 64
                pos = col[:, names[("posk", "posv")[j]][0]:names[("posk", "posv")[j]][1]]
                V.wait((s_kg, n_kg), t_h)
                for g in range(2):
                    for f in range(2):
                        view = kg[:, g, 16 * f:16 * f + 496].rearrange("p (n m) -> p m n", m=16)[:, 0:16:2, :]
                        t_z = V.tt(zt[:, 8 * f:8 * f + 8, 31 * g:31 * g + 31], view,
                                   pos[:, 8 * f:8 * f + 8].unsqueeze(2).broadcast_to([128, 8, 31]), ALU.add)
                b = bank[4]
                for f in range(2):
                    A.wait(t_ph)
                    A.dma(ph[:], phi1[j, :, 8 * f:8 * f + 8, :], s_ph)
                    n_ph += 16
                    yield
                    PE.wait(t_z, (s_ph, n_ph), *(b.free if f == 0 else ()))
                    for k in range(8):
                        t_ph = PE.mm(b.ap[0:62, 0:256], zt[:, 8 * f + k, :], ph[:, k, :], f == 0 and k == 0, f == 1 and k == 7, signal=k == 7)
                    yield
                t_h = t_ph
                t = A.cp(ge[0][:], b.ap[0:62, 0:256], t_ph)
                b.free = (t,)
                t1 = A.act(ge[1][:], ge[0][:], ACT.Square, 1.0, None, t)
                t1 = V.ts(ge[1][:], ge[1][:], 0.044715, ALU.mult, 1.0, ALU.add, t1)
                t1 = V.tt(ge[1][:], ge[1][:], ge[0][:], ALU.mult, t1, t)
                t1 = A.act(ge[1][:], ge[1][:], ACT.Tanh, 0.7978845608028654, None, t1)
                t1 = V.stt(ge[2][:], ge[1][:], 1.0, ge[0][:], ALU.add, ALU.mult, t1)
                yield
                b = bank[5]
                for f in range(2):
                    t = PE.tr(b.ap[:, 62 * f:62 * f + 62], ge[2][:, 128 * f:128 * f + 128], ident[0:62, 0:62], *((t1, *b.free) if f == 0 else ()), signal=f == 1)
                t = A.cp(hid[:].rearrange("p a b -> p (a b)"), b.ap[:, 0:124], t)
                b.free = (t,)
                yield
                PE.wait(t, (s_lw, 32), *bank[4].free)
                b = bank[4]
                if j == 0:
                    for g in range(2):
                        for f in range(2):
                            t = PE.mm(b.ap[64 * g:64 * g + 64, 0:31], p2[:, 0, f, :], hid[:, f, 31 * g:31 * g + 31], f == 0, f == 1, signal=f == 1)
                    x, r = ctiles(2)
                    t = A.act(x.ap[:, 0:31], b.ap[:, 0:31], ACT.Copy, 0.5, None, t, *x.free)
                    b.free = (t,)
                    t = yield from headnorm(x.ap[:, 0:31], t, K("kn2", 0), 5, 31, ctiles)
                    V.wait(*r.free)
                    t = rope(r.ap[:, 0:31], x.ap[:, 0:31], TB("r16"), TB("cosC"), TB("sinC"), 5, t, 31, ctiles)
                    x.free = (t,)
                    y2["kcz"] = [V.cp(kcz[64 * g:64 * g + 64, g, :], r.ap[64 * g:64 * g + 64, 0:31], t, t_kcz) for g in range(2)]
                    r.free = tuple(y2["kcz"])
                else:
                    for g in range(2):
                        for f in range(2):
                            t = PE.mm(b.ap[0:31, 64 * g:64 * g + 64], hid[:, f, 31 * g:31 * g + 31], p2[:, 1, f, :], f == 0, f == 1, signal=f == 1)
                    t = A.act(vcm[:].rearrange("p a b -> p (a b)"), b.ap[0:31, 0:128], ACT.Copy, 0.5, None, t)
                    b.free = (t,)
                    y2["vcm"] = t
                yield

        def nsa():
            cb = cau
            L0 = {}
            n_u = 0
            for b in range(4):
                nk = 128 * (b + 1)
                qsl = slice(128 * b, 128 * b + 128)
                bk = bank[4]
                PE.wait(*bk.free, *y2["kcz"], *[y2[("q", c)] for c in range(4)])
                for h in range(8):
                    t = PE.mm(bk.ap[:, 31 * h:31 * h + 31], q2[:, h % 4, qsl], kcz[:, h // 4, :], True, True, signal=h == 7)
                s3 = sC[:, 0:248].rearrange("p (h n) -> p h n", h=8)
                mask = TB("maskC").rearrange("p (b n) -> p b n", b=4)[:, b, :].unsqueeze(1).broadcast_to([128, 8, 31])
                t = V.tt(s3, bk.ap[:, 0:248].rearrange("p (h n) -> p h n", h=8), mask, ALU.add, t, *L0.get("sC", ()))
                bk.free = (t,)
                mx, sm = stc[:, 0:8], stc[:, 8:16]
                t1 = V.do(lambda e, mx=mx, s3=s3: e.tensor_reduce(mx, s3, AXX, ALU.max), (t,))
                t = V.tt(s3, s3, mx.unsqueeze(2).broadcast_to([128, 8, 31]), ALU.subtract, t1)
                t = A.act(sC[:, 0:248], sC[:, 0:248], ACT.Exp, 0.125, None, t)
                t1 = V.do(lambda e, sm=sm, s3=s3: e.tensor_reduce(sm, s3, AXX, ALU.add), (t,))
                t1 = V.rec(sm, sm, t1)
                t1 = V.tt(sm, sm, gs[:, b, 0:8], ALU.mult, t1, y2[("v", b)])
                t1 = V.ts(sm, sm, TB("validC")[:, b:b + 1], ALU.mult, None, None, t1)
                t = V.tt(s3, s3, sm.unsqueeze(2).broadcast_to([128, 8, 31]), ALU.mult, t1, t)
                yield
                for f in range(2):
                    bk = bank[4 + f]
                    for h in range(4):
                        c0 = 31 * (4 * f + h)
                        t2 = PE.tr(bk.ap[0:31, 128 * h:128 * h + 128], sC[:, c0:c0 + 31], ident, *((t, *bk.free) if h == 0 else ()), signal=h == 3)
                    t3 = A.cp(pC[:, 4 * f:4 * f + 4, :].rearrange("p a b -> p (a b)"), bk.ap[0:31, :], t2, *L0.get("pC", ()))
                    bk.free = (t3,)
                L0["sC"] = (t2,)
                yield
                ob = bank[7]
                u = [(h, j) for h in range(8) for j in range(2)]
                t_sc, t_p = {}, {}
                for n in range(len(u) + 2):
                    if n >= 2:
                        h, j = u[n - 2]
                        g, P = h // 4, Pn2[n % 2]
                        o = ob.ap[:, 64 * h:64 * h + 64]
                        if j == 0:
                            PE.mm(o, pC[:, h, :], vcm[:, g, :], True, False, t3, y2["vcm"], *(ob.free if h == 0 else ()), share=True)
                        PE.wait(t_p[n - 2], *[y2[("vt", i)] for i in range(b + 1)])
                        for i in range(b + 1):
                            t = PE.mm(o, P.ap[:, i, :], vt[:, i, 128 * j + 64 * g:128 * j + 64 * g + 64], False, j == 1 and i == b, signal=i == b, share=True)
                        P.free = (t,)
                        t_o = t
                    if 1 <= n <= len(u):
                        bk, L, P = bank[4 + (n - 1) % 3], Ln2[(n - 1) % 2], Pn2[(n - 1) % 2]
                        for i in range(b + 1):
                            t = PE.tr(bk.ap[:, 128 * i:128 * i + 128], L.ap[:, 128 * i:128 * i + 128], ident, *((t_sc[n - 1], *bk.free) if i == 0 else ()), signal=i == b)
                        L.free = (t,)
                        t_p[n - 1] = A.cp(P.ap[:, 0:b + 1, :].rearrange("p a b -> p (a b)"), bk.ap[:, 0:nk], t, *P.free)
                        bk.free = (t_p[n - 1],)
                    if n < len(u):
                        h, j = u[n]
                        bk, L = bank[4 + n % 3], Ln2[n % 2]
                        m, w = stc[:, 16 + 2 * (n % 3):17 + 2 * (n % 3)], stc[:, 17 + 2 * (n % 3):18 + 2 * (n % 3)]
                        t = PE.mm(bk.ap[:, 0:nk], q2[:, h % 4, qsl], kz[:, 2 * j + h // 4, 0:nk], True, True, *bk.free, *y2[("k", j)], signal=True)
                        t = V.addred(L.ap[:, 0:nk], bk.ap[:, 0:nk], cb[:, 384 - 128 * b:512], -0.125, 3.0e38, ALU.min, m, t, (s_lw, 32), *L.free)
                        bk.free = (t,)
                        t = A.act(L.ap[:, 0:nk], L.ap[:, 0:nk], ACT.Exp, -1.0, m, t, acc=w)
                        t1 = V.rec(w, w, t)
                        t1 = V.tt(w, w, gs[:, b, 8 * (j + 1) + h:8 * (j + 1) + h + 1], ALU.mult, t1)
                        t_sc[n] = V.ts(L.ap[:, 0:nk], L.ap[:, 0:nk], w, ALU.mult, None, None, t1, t)
                    yield
                L0["pC"] = (t_o,)
                L = Ln2[0]
                t = A.cp(L.ap[:], ob.ap[:], t_o, *L.free)
                ob.free = (t,)
                yield
                b6 = bank[6]
                for c in range(4):
                    t1 = PE.tr(b6.ap[:, 128 * c:128 * c + 128], L.ap[:, 128 * c:128 * c + 128], ident, *((t, *b6.free) if c == 0 else ()), signal=c == 3)
                L.free = (t1,)
                t = A.cp(onT[:, :, qsl], b6.ap[:].rearrange("p (c t) -> p c t", c=4), t1)
                b6.free = (t,)
                y2[("o", b)] = t
                yield

        def lru():
            for c in range(8):
                t = yield from project(("c2", 1304 + 128 * c), 0)
                xc, rr, ii, aa = lt
                V.wait(*xc.free)
                A.wait(*xc.free)
                t_xc = conv(bank[0], t, "conv2", c, xc.ap[:], bias=K("convb", c))
                t_y = yield from project(("c2", 2328 + 128 * c), 1)
                w = lw[c % 2]
                PE.mm(bank[2].ap[:], w.ap[:, 0, :], xc.ap[:], True, True, t_xc, (s_lr[c % 2], 16 * (c // 2 + 1)), *bank[2].free)
                t = PE.mm(bank[3].ap[:], w.ap[:, 1, :], xc.ap[:], True, True, *bank[3].free, signal=True)
                if c + 2 < 8:
                    S.dma(w.ap[:], lruw[:, :, c + 2, :], s_lr[c % 2], t)
                t1 = A.act(rr.ap[:], bank[2].ap[:], ACT.Tanh, 0.5, lc[:, 16 + c:17 + c], t, *t_lc, *rr.free)
                bank[2].free = (t1,)
                t1 = V.ts(rr.ap[:], rr.ap[:], 1.0, ALU.add, 0.5, ALU.mult, t1)
                t2 = A.act(ii.ap[:], bank[3].ap[:], ACT.Tanh, 0.5, lc[:, 24 + c:25 + c], t, *ii.free)
                bank[3].free = (t2,)
                t2 = V.stt(ii.ap[:], ii.ap[:], 1.0, xc.ap[:], ALU.add, ALU.mult, t2, t_xc)
                t3 = A.act(aa.ap[:], rr.ap[:], ACT.Exp, lc[:, c:c + 1], None, t1, *aa.free)
                t4 = A.act(rr.ap[:], rr.ap[:], ACT.Tanh, lc[:, 8 + c:9 + c], None, t1, t3)
                t5 = A.act(xc.ap[:], aa.ap[:], ACT.Square, 1.0, None, t3, t2, t)
                g1, g2 = tmps(2)
                t6 = A.cp(g1.ap[:], bank[1].ap[:], t_y, *g1.free)
                bank[1].free = (t6,)
                t7 = A.act(g2.ap[:], g1.ap[:], ACT.Square, 1.0, None, t6, *g2.free)
                t5 = V.stt(rr.ap[:], xc.ap[:], 1.0, rr.ap[:], ALU.add, ALU.mult, t5, t4)
                t5 = V.ts(rr.ap[:], rr.ap[:], 1e-18, ALU.max, None, None, t5)
                t7 = V.ts(g2.ap[:], g2.ap[:], 0.044715, ALU.mult, 1.0, ALU.add, t7)
                t7 = V.tt(g2.ap[:], g2.ap[:], g1.ap[:], ALU.mult, t7, t6)
                t7 = A.act(g2.ap[:], g2.ap[:], ACT.Tanh, 0.7978845608028654, None, t7)
                t5 = A.act(rr.ap[:], rr.ap[:], ACT.Ln, 1.0, None, t5)
                t5 = A.act(rr.ap[:], rr.ap[:], ACT.Exp, 0.5, None, t5)
                t5 = V.stt(ii.ap[:], ii.ap[:], 0.5, rr.ap[:], ALU.mult, ALU.mult, t5, t2)
                rr.free = (t5,)
                t8 = V.scan(xc.ap[:], aa.ap[:], ii.ap[:], 0.0, t5, t3)
                aa.free = ii.free = (t8,)
                t7 = V.stt(g2.ap[:], g2.ap[:], 1.0, g1.ap[:], ALU.add, ALU.mult, t7, t6)
                g1.free = (t7,)
                t8 = V.stt(xc.ap[:], xc.ap[:], 0.5, g2.ap[:], ALU.mult, ALU.mult, t8, t7)
                g2.free = (t8,)
                th, tl = pair(oh[:, c, :], ol[:, c, :], xc.ap[:], t8)
                xc.free = (th, tl)
                y2[("lru", c)] = (th, tl)
                yield

        def merge2():
            PE.wait(*sum([y2[("lru", c)] for c in range(8)], ()))
            for m in range(8):
                t = yield from project(("c2", 4376 + 128 * m), m % 2)
                g, = tmps(1)
                tg = A.act(g.ap[:], bank[m % 2].ap[:], ACT.Tanh, 0.5, None, t, *g.free)
                bank[m % 2].free = (tg,)
                pb = 2 + m % 2
                t = yield from project(("lup", m), pb, oh, ol)
                y2[("acc", m)] = V.stt(acc[:, m, :], g.ap[:], 1.0, bank[pb].ap[:], ALU.add, ALU.mult, tg, t)
                g.free = bank[pb].free = (y2[("acc", m)],)
                yield

        def merge3():
            out = []
            for c in range(4):
                out += pair(yh2[:, c, :], yl2[:, c, :], onT[:, c, :], y2[("o", 3)])
            PE.wait(*out)
            for m in range(8):
                if m % 2 == 0:
                    ib = take(("nup", m // 2))
                    for j in range(2):
                        PE.wait(*bank[j].free)
                        for k in range(4):
                            w = slice(512 * j + 128 * k, 512 * j + 128 * k + 128)
                            t = prod3(bank[j].ap[:], ib, w, yh2[:, k, :], yl2[:, k, :], k == 0, k == 3)
                        y2[("pb", j)] = t
                    done(ib, t)
                gb = 2 + m % 2
                t = yield from project(("c2", 3352 + 128 * m), gb)
                g, = tmps(1)
                tg = A.act(g.ap[:], bank[gb].ap[:], ACT.Tanh, 0.5, None, t, *g.free)
                bank[gb].free = (tg,)
                pb = bank[m % 2]
                ta = V.stt(g.ap[:], g.ap[:], 1.0, pb.ap[:], ALU.add, ALU.mult, tg, y2[("pb", m % 2)])
                pb.free = (ta,)
                ta = V.tt(acc[:, m, :], acc[:, m, :], g.ap[:], ALU.add, ta, y2[("acc", m)])
                g.free = (ta,)
                y2[("acc", m)] = ta

        for _ in proj2():
            pass
        lru_main = lru()
        weave(islice(lru_main, 12), (compress(), 1.75))
        tap("q2", q2[:], A.last(), V.last())
        last = fence()
        comp.close()
        m3 = ExitStack()
        acc = sb("acc_2", [128, 8, T], stack=m3)
        Ln2 = [Slot(sb(f"Ln{i}", [128, T], stack=m3)) for i in range(2)]
        Pn2 = [Slot(sb(f"Pn{i}", [128, 4, 128], stack=m3)) for i in range(2)]
        sC = sb("sC", [128, 256], stack=m3)
        pC = sb("pC", [31, 8, 128], stack=m3)
        stc = sb("stc", [128, 32], stack=m3)
        yh2, yl2 = oh[:, 0:4, :], ol[:, 0:4, :]

        def mains():
            yield from lru_main
            yield from merge2()

        weave(mains(), (nsa(), RATES[3]))
        tap("nsa", onT[:], A.last(), V.last())
        tap("lru_h", oh[:].bitcast(F32), A.last(), V.last())
        t_pe = PE.last()
        A.wait(t_pe)
        V.wait(t_pe)
        for _ in merge3():
            pass
        t_h = PE.last()
        for m in range(8):
            halve(acc, m, y2[("acc", m)], t_h)
        last = fence()
        m3.close()
        b2.close()
        xt = sb("xt_2", [128, 8, T])
        S.wait(*last)
        xn[0] += 16
        S.dma(xt[:], x_src, s_x)
        x_toks = []
        for m in range(8):
            for _ in project(("o2", m), m % 4):
                pass
            tx = V.tt(xt[:, m, :], xt[:, m, :], bank[m % 4].ap[:], ALU.add, PE.last(), (s_x, xn[0]))
            bank[m % 4].free = (tx,)
            x_toks.append(tx)
            square(xt, m, tx)
        norm_into_h(xt, "nrmB")
        fh, fl = sb("fh", [128, 16, T], F32R), sb("fl", [128, 16, T], F32R)
        s_o = sem("s_out")
        for half in range(2):
            ft = []
            t_f2 = PE.last()
            for j in range(16):
                for _ in project(("f1", 16 * half + j), j % 4):
                    pass
                r, = tmps(1)
                t = A.act(r.ap[:], bank[j % 4].ap[:], ACT.Relu, 1.0, None, PE.last(), *r.free)
                bank[j % 4].free = (t,)
                t = V.tt(r.ap[:], r.ap[:], r.ap[:], ALU.mult, t)
                th = A.cp(fh[:, j, :], r.ap[:], t, t_f2 if half else None)
                tl = V.tt(fl[:, j, :], r.ap[:], fh[:, j, :].bitcast(F32), ALU.subtract, t, th, t_f2 if half else None)
                r.free = (th, tl)
                ft += [th, tl]
            PE.wait(*ft)
            for m in range(8):
                b = bank[m % 4]
                PE.wait(*b.free)
                for jj in range(2):
                    i = take(("f2", 2 * half + jj, m))
                    for k in range(8):
                        t = prod3(b.ap[:], i, slice(128 * k, 128 * k + 128), fh[:, 8 * jj + k, :], fl[:, 8 * jj + k, :],
                                  jj == 0 and k == 0, jj == 1 and k == 7, signal=k == 7)
                    done(i, t)
                tx = V.tt(xt[:, m, :], xt[:, m, :], b.ap[:], ALU.add, t, x_toks[m])
                b.free = (tx,)
                x_toks[m] = tx
                if half == 1:
                    A.dma(x_out[:, m, :], xt[:, m, :], s_o, tx)
        A.wait((s_o, 16 * 8))
        block = ctx.enter_context(nc.Block())

        @block.sync
        def _(e):
            S.play(e)

        @block.tensor
        def _(e):
            PE.play(e)

        @block.vector
        def _(e):
            V.play(e)

        @block.scalar
        def _(e):
            A.play(e)

        @block.gpsimd
        def _(e):
            G.play(e)


def layouts(I):
    x = np.ascontiguousarray(I["x"][0].reshape(T, 8, 128).transpose(2, 1, 0))
    cpack, apack, bpack = constants(), tables_a(), tables_b()
    return {
        "x": x, "units": pack_units(I), "consts": cpack.array(), "tabA": apack.array(), "tabB": bpack.array(),
        "cols": pack_columns(I), "poolw": np.ascontiguousarray(I["pool_w"].transpose(0, 2, 1, 3)),
        "lruw": np.ascontiguousarray(np.stack([I["lru_wa_2"][0], I["lru_wx_2"][0]]).transpose(2, 0, 1, 3)),
        "phi1": np.ascontiguousarray(np.stack([I["phi_k_w1_2"][0], I["phi_v_w1_2"][0]]).reshape(2, 16, 128, 256).transpose(0, 2, 1, 3)),
        "phi2": np.ascontiguousarray(np.stack([I["phi_k_w2_2"][0], I["phi_v_w2_2"][0]]).reshape(2, 2, 128, 64).transpose(2, 0, 1, 3)),
    }, cpack, apack, bpack


def make(nc, arrays, packs, debug=None):
    ap = {n: nc.dram_tensor(n, list(a.shape), F32, kind="ExternalInput").ap() for n, a in arrays.items()}
    out = nc.dram_tensor("out", [128, 8, T], F32, kind="ExternalOutput").ap()
    build(nc, ap["units"], ap["consts"], ap["tabA"], ap["tabB"], ap["cols"], ap["poolw"], ap["lruw"], ap["phi1"],
          ap["phi2"], ap["x"], out, *packs, debug=debug)


def kernel(**inputs):
    from concourse import bacc
    from concourse.bass_utils import run_bass_kernel_spmd

    arrays, *packs = layouts({k: np.asarray(v) for k, v in inputs.items()})
    nc = bacc.Bacc("TRN2", target_bir_lowering=False, num_devices=1)
    make(nc, arrays, packs)
    r = run_bass_kernel_spmd(nc, [arrays], core_ids=[0])
    y = np.asarray(r.results[0]["out"])
    return np.ascontiguousarray(y.transpose(2, 1, 0).reshape(1, T, D))
```

```python
import math
from contextlib import ExitStack

import numpy as np

import concourse.bass as bass
from concourse import mybir

F32 = mybir.dt.float32
F32R = mybir.dt.float32r
ACT = mybir.ActivationFunctionType
ALU = mybir.AluOpType
AXX = mybir.AxisListType.X

T = 512
D = 1024
NK = 8
NEG = -1.0e30
MARK = -3.0e38
EPS = 1e-6
U = 1024
RATES = (0.8, 0.6, 0.42, 1.5, 0.65)



def plan():
    out = []
    for l in range(2):
        out += [("small", l)]
        out += [("p", l, 128 * c) for c in range(12)]
        out += [("p", l, 5128), ("p", l, 5256), ("ik", l)]
        out += [("p", l, 3080 + 128 * c) for c in range(8)]
        out += [("p", l, 5452 + 1024 * n + 128 * m) for n in (1, 0, 2) for m in range(8)]
        out += [("v", l, j) for j in range(4)]
        out += [("p", l, 4616 + 128 * c) for c in range(4)]
        for g in range(4):
            out += [("p", l, 2568 + 128 * g), ("p", l, 2056 + 128 * g)]
        out += [("p", l, 1536 + 128 * c) for c in range(4)]
        out += [("br", l, n, mp) for n in (1, 0, 2) for mp in range(4)]
        out += [("o", l, m) for m in range(8)]
    out += [("q2", c) for c in range(4)]
    out += [("c2", 512), ("c2", 640), ("c2", 768), ("c2", 1024)]
    out += [("v2", j) for j in range(3)]
    for c in range(8):
        out += [("c2", 1304 + 128 * c), ("c2", 2328 + 128 * c)]
    for m in range(8):
        out += [("c2", 4376 + 128 * m), ("lup", m)]
    out += [("c2", 3352 + 128 * m) for m in range(6)]
    for m in range(8):
        if m % 2 == 0:
            out.append(("nup", m // 2))
        if m >= 6:
            out.append(("c2", 3352 + 128 * m))
    out += [("o2", m) for m in range(8)]
    for h in range(2):
        out += [("f1", 16 * h + j) for j in range(16)]
        out += [("f2", 2 * h + jj, m) for m in range(8) for jj in range(2)]
    return out


def q2_columns(c):
    return np.concatenate([np.arange(64 * c, 64 * c + 64), np.arange(64 * (4 + c), 64 * (4 + c) + 64)])


def pack_units(I):
    keys = plan()
    units = np.zeros((len(keys), 128, U), np.float32)

    def kmajor(w):
        k, n = w.shape[0] // 128, w.shape[1]
        return w.reshape(k, 128, n).transpose(1, 0, 2).reshape(128, k * n)

    w2 = I["w_in_2"][0]
    vg = np.concatenate([w2[:, 896:1024], w2[:, 1152:1280], w2[:, 1280:1304]], axis=1)
    for n, key in enumerate(keys):
        kind = key[0]
        if kind == "small":
            u = units[n].reshape(128, 8, 128)
            w = I["w_in"][key[1]]
            for c0, at in ((2048, 0), (2052, 32), (5448, 64)):
                u[:, :, at:at + 4] = kmajor(w[:, c0:c0 + 4]).reshape(128, 8, 4)
        elif kind == "p":
            units[n] = kmajor(I["w_in"][key[1]][:, key[2]:key[2] + 128])
        elif kind == "ik":
            w = I["w_in"][key[1]][:, 5384:5448]
            units[n].reshape(128, 8, 128)[:, :, 0:64] = kmajor(w).reshape(128, 8, 64)
            units[n].reshape(128, 8, 128)[:, :, 64:128] = kmajor(w).reshape(128, 8, 64)
        elif kind == "v":
            j = key[2]
            units[n] = kmajor(I["w_in"][key[1]][256 * j:256 * j + 256, 4104:4616])
        elif kind == "br":
            w = I["w_branch"][key[1], key[2]][:, 256 * key[3]:256 * key[3] + 256]
            units[n] = w.reshape(4, 128, 2, 128).transpose(1, 2, 0, 3).reshape(128, U)
        elif kind == "o":
            units[n] = kmajor(I["w_out"][key[1]][:, 128 * key[2]:128 * key[2] + 128])
        elif kind == "q2":
            units[n] = kmajor(w2[:, q2_columns(key[1])])
        elif kind == "c2":
            units[n] = kmajor(w2[:, key[1]:key[1] + 128])
        elif kind == "v2":
            k0, k1 = 3 * key[1], min(8, 3 * key[1] + 3)
            units[n, :, 0:280 * (k1 - k0)] = kmajor(vg[128 * k0:128 * k1])
        elif kind == "lup":
            units[n] = kmajor(I["w_lru_up_2"][0][:, 128 * key[1]:128 * key[1] + 128])
        elif kind == "nup":
            w = I["w_nsa_up_2"][0][:, 256 * key[1]:256 * key[1] + 256]
            units[n] = w.reshape(4, 128, 2, 128).transpose(1, 2, 0, 3).reshape(128, U)
        elif kind == "o2":
            units[n] = kmajor(I["w_o_2"][0][:, 128 * key[1]:128 * key[1] + 128])
        elif kind == "f1":
            units[n] = kmajor(I["w_ff1_2"][0][:, 128 * key[1]:128 * key[1] + 128])
        elif kind == "f2":
            j, m = key[1], key[2]
            units[n] = kmajor(I["w_ff2_2"][0][1024 * j:1024 * j + 1024, 128 * m:128 * m + 128])
    return units



class Packed:

    def __init__(self):
        self.at, self.parts, self.n = {}, [], 0

    def add(self, name, a):
        a = np.asarray(a, np.float32)
        a = a.reshape(128, -1)
        self.at[name] = (self.n, self.n + a.shape[1])
        self.parts.append(a)
        self.n += a.shape[1]

    def array(self):
        return np.ascontiguousarray(np.concatenate(self.parts, axis=1))


def rope_np(seq, dim, theta):
    inv = theta ** (-np.arange(0, dim, 2, dtype=np.float32) / np.float32(dim))
    ang = np.arange(seq, dtype=np.float32)[:, None] * inv[None, :].astype(np.float32)
    return np.cos(ang).astype(np.float32), np.sin(ang).astype(np.float32)


def constants():
    c = Packed()
    i = np.arange(128)
    c.add("ident", np.eye(128))
    c.add("ones", np.ones((128, 128)))
    c.add("mean", np.full((128, 128), 1.0 / 128.0))
    c.add("blk", (i[:, None] // 64 == i[None, :] // 64))
    same = i[:, None] // 64 == i[None, :] // 64
    c.add("decay", np.where(same & (i[:, None] <= i[None, :]), 0.0, NEG))
    c.add("last", i[:, None] == 64 * (i[None, :] // 64) + 63)
    levels = []
    for n in range(6):
        s = 2 ** n
        j, k = i[:, None], i[None, :]
        levels.append((j // (2 * s) == k // (2 * s)) & (j // s % 2 == 0) & (k // s % 2 == 1))
    c.add("levels", np.stack(levels, 1))
    r128 = np.zeros((128, 128))
    for k in range(64):
        r128[k + 64, k] = -1.0
        r128[k, k + 64] = 1.0
    c.add("r128", r128)
    r64 = np.zeros((128, 128))
    for b in (0, 64):
        for k in range(32):
            r64[b + k + 32, b + k] = -1.0
            r64[b + k, b + k + 32] = 1.0
    c.add("r64", r64)
    reset = np.ones((128, T))
    reset[:, ::64] = 0.0
    c.add("reset", reset)
    cnt = np.zeros((4, 16), np.float32)
    for g, w in enumerate((2, 4, 8, 16)):
        cnt[g] = np.float32(1.0) / np.minimum(np.arange(1, 17), w).astype(np.float32)
    c.add("count", np.broadcast_to(cnt[None], (128, 4, 16)))
    c.add("eps", np.full((128, 1), EPS))
    c.add("causal", np.where((np.arange(512)[None, :] - 384) <= i[:, None], 0.0, NEG))
    return c


def tables_a():
    c = Packed()
    co, si = rope_np(T, 128, 10000.0)
    c.add("cosA", np.concatenate([co.T, co.T]))
    c.add("sinA", np.concatenate([si.T, si.T]))
    co, si = rope_np(T, 64, 10000.0)
    c.add("cosI", np.concatenate([co.T] * 4))
    c.add("sinI", np.concatenate([si.T] * 4))
    return c


def tables_b():
    c = Packed()
    inv = np.float32(500000.0) ** (-np.arange(8, dtype=np.float32) / np.float32(8))
    ang = np.arange(T, dtype=np.float32)[:, None] * inv[None, :]
    co, si = np.ones((128, T), np.float32), np.zeros((128, T), np.float32)
    r = np.zeros((128, 128))
    for b in (0, 64):
        for h in (0, 8):
            co[b + h:b + h + 8] = np.cos(ang).T
            si[b + h:b + h + 8] = np.sin(ang).T
        for k in range(8):
            r[b + k + 8, b + k] = -1.0
            r[b + k, b + k + 8] = 1.0
    c.add("cos", co)
    c.add("sin", si)
    end = 16 * np.arange(31) + 31
    c.add("cosC", co[:, end])
    c.add("sinC", si[:, end])
    c.add("r16", r)
    t = np.arange(128)[:, None, None] + 128 * np.arange(4)[None, :, None]
    c.add("maskC", np.where(end[None, None, :] <= t, 0.0, NEG))
    c.add("validC", (t[:, :, 0] >= 31))
    return c


def column_names():
    at, n = {}, 0
    sizes = []
    for l in range(2):
        sizes += [(f"norm{l}", 8), (f"gateb{l}", 24), (f"conv{l}", 48), (f"alog{l}", 1), (f"dt{l}", 1),
                  (f"onorm{l}", 1), (f"pscale{l}", 4), (f"qn{l}", 1), (f"kn{l}", 1)]
    sizes += [("nrmA", 8), ("nrmB", 8), ("qn2", 1), ("kn2", 3), ("conv2", 32), ("convb", 8), ("ba", 8),
              ("bx", 8), ("lam", 8), ("posk", 16), ("posv", 16)]
    for name, k in sizes:
        at[name] = (n, n + k)
        n += k
    return at, n


def pack_columns(I):
    at, n = column_names()
    c = np.zeros((128, n), np.float32)

    def put(name, a):
        c[:, at[name][0]:at[name][1]] = a

    def chunks(v):
        return v.reshape(-1, 128).T

    for l in range(2):
        put(f"norm{l}", chunks(I["norm_g"][l]))
        put(f"gateb{l}", chunks(I["gate_b"][l].reshape(-1)))
        put(f"conv{l}", I["conv_w"][l].reshape(4, 12, 128).transpose(2, 1, 0).reshape(128, 48))
        c[32:36, at[f"alog{l}"][0]] = I["a_log"][l]
        c[32:36, at[f"dt{l}"][0]] = I["dt_bias"][l]
        put(f"onorm{l}", I["dn_onorm"][l][:, None])
        put(f"pscale{l}", chunks(I["pool_scale"][l]))
        put(f"qn{l}", I["q_norm"][l][:, None])
        put(f"kn{l}", I["k_norm"][l][:, None])
    put("nrmA", chunks(I["norm1_w_2"][0]))
    put("nrmB", chunks(I["norm2_w_2"][0]))
    put("qn2", np.concatenate([I["q_norm_w_2"][0]] * 2)[:, None])
    put("kn2", np.concatenate([I["k_norm_w_2"][0].T] * 2))
    put("conv2", I["conv_w_2"][0].reshape(4, 8, 128).transpose(2, 1, 0).reshape(128, 32))
    put("convb", chunks(I["conv_b_2"][0]))
    put("ba", I["lru_ba_2"][0].T)
    put("bx", I["lru_bx_2"][0].T)
    put("lam", chunks(I["lru_lambda_2"][0]))
    put("posk", I["phi_k_pos_2"][0].reshape(16, 128).T)
    put("posv", I["phi_v_pos_2"][0].reshape(16, 128).T)
    return c



class Queue:

    def __init__(self, sem):
        self.sem, self.n, self.items, self.waited = sem, 0, [], {}

    def wait(self, *tokens):
        for t in tokens:
            if t is None:
                continue
            sem, value = t
            if self.waited.get(sem.name, 0) < value:
                self.waited[sem.name] = value
                self.items.append(lambda e, s=sem, v=value: e.wait_ge(s, v))

    def do(self, f, after=(), signal=True):
        self.wait(*after)
        if not signal:
            self.items.append(f)
            return None
        self.n += 1
        self.items.append(lambda e, s=self.sem: f(e).then_inc(s, 1))
        return (self.sem, self.n)

    def last(self):
        return (self.sem, self.n) if self.n else None

    def dma(self, out, in_, sem, *after):
        self.do(lambda e: e.dma_start(out, in_).then_inc(sem, 16), after, signal=False)

    def play(self, e):
        for f in self.items:
            f(e)


class Vec(Queue):
    def tt(self, out, a, b, op, *after):
        return self.do(lambda e: e.tensor_tensor(out, a, b, op), after)

    def ts(self, out, a, s1, op0, s2, op1, *after):
        if s2 is None:
            return self.do(lambda e: e.tensor_scalar(out, a, s1, None, op0), after)
        return self.do(lambda e: e.tensor_scalar(out, a, s1, s2, op0, op1), after)

    def stt(self, out, a, s, b, op0, op1, *after):
        return self.do(lambda e: e.scalar_tensor_tensor(out=out, in0=a, scalar=s, in1=b, op0=op0, op1=op1), after)

    def cp(self, out, a, *after):
        return self.do(lambda e: e.tensor_copy(out, a), after)

    def set(self, out, v, *after):
        return self.do(lambda e: e.memset(out, v), after)

    def scan(self, out, a, b, initial, *after):
        return self.do(lambda e: e.tensor_tensor_scan(out, a, b, initial, ALU.mult, ALU.add), after)

    def max8(self, out, a, *after):
        return self.do(lambda e: e.max(out, a), after)

    def replace(self, out, vals, a, v, *after):
        return self.do(lambda e: e.match_replace(out, vals, a, v), after)

    def addred(self, out, a, b, scale, init, red, acc, *after):
        return self.do(lambda e: e.tensor_tensor_reduce(out, a, b, scale, init, ALU.add, red, acc), after)

    def rec(self, out, a, *after):
        return self.do(lambda e: e.reciprocal(out, a), after)


class Act(Queue):
    both = False

    def act(self, out, a, func, scale, bias, *after, acc=None):
        if func == ACT.Ln and not self.both:
            self.items.append(lambda e: e.preload_act_table_set("natural_log_exp_and_others"))
        if func in (ACT.Ln, ACT.Tanh):
            self.both = func == ACT.Ln

        def f(e):
            kw = {}
            if bias is not None:
                kw["bias"] = bias
            if acc is not None:
                kw["accum_out"] = acc
            return e.activation(out, a, func, scale=scale, **kw)
        return self.do(f, after)

    def cp(self, out, a, *after):
        return self.do(lambda e: e.activation(out, a, ACT.Copy), after)


class Ten(Queue):
    def mm(self, out, lhsT, rhs, start, stop, *after, signal=False, share=False):
        return self.do(lambda e: e.matmul(out, lhsT, rhs, start=start, stop=stop, skip_group_check=share),
                       after, signal)

    def tr(self, out, a, ident, *after, signal=False):
        return self.do(lambda e: e.transpose(out, a, ident), after, signal)


class Slot:

    def __init__(self, ap):
        self.ap, self.free = ap, ()


def weave(main, *sides):
    sides = [[g, rate, 0.0, True] for g, rate in sides]
    for _ in main:
        for s in sides:
            s[2] += s[1]
            while s[3] and s[2] >= 1.0:
                s[2] -= 1.0
                s[3] = next(s[0], "end") != "end"
    left = [s[0] for s in sides if s[3]]
    while left:
        left = [g for g in left if next(g, "end") != "end"]


def staggered(a, b):
    next(a, None)
    while True:
        x, y = next(b, "end"), next(a, "end")
        if x == "end" and y == "end":
            return
        yield


def lagged(jobs):
    live = []

    def advance():
        live[:] = [g for g in live if next(g, "end") != "end"]

    for product, follow in jobs:
        next(product)
        advance()
        yield
        try:
            next(product)
        except StopIteration as e:
            t = e.value
        advance()
        live.append(follow(t))
        live[:] = live[:-1] + [g for g in live[-1:] if next(g, "end") != "end"]
        yield
    while live:
        advance()
        yield



def build(nc, units, consts, tabA, tabB, cols, poolw, lruw, phi1, phi2, x_in, x_out, cpack, apack, bpack):
    keys = plan()
    with ExitStack() as ctx:
        def sb(name, shape, dt=F32, stack=ctx):
            return stack.enter_context(nc.sbuf_tensor(name, shape, dt))

        def sem(name):
            return ctx.enter_context(nc.semaphore(name))

        PE, V, A, G = Ten(sem("s_pe")), Vec(sem("s_dve")), Act(sem("s_act")), Vec(sem("s_pool"))
        S = Queue(sem("s_sp"))

        def fence():
            return [q.last() for q in (PE, V, A, G)]

        bank = [Slot(ctx.enter_context(nc.psum_tensor(f"bank{i}", [128, 512], F32))) for i in range(8)]
        n_cst = cpack.at["causal"][0]
        cst = sb("cst", [128, n_cst])
        col = sb("col", [128, cols.shape[1]])
        colx = sb("colx", [128, 96])
        hh = sb("hh", [128, 8, T], F32R)
        hl = sb("hl", [128, 8, T], F32R)
        tmp = [Slot(sb(f"tmp{i}", [128, T])) for i in range(4)]
        tno = [0]

        def tmps(k):
            out = [tmp[(tno[0] + i) % len(tmp)] for i in range(k)]
            tno[0] = (tno[0] + k) % len(tmp)
            return out

        def C(name):
            a, b = cpack.at[name]
            return cst[:, a:b]

        names, _ = column_names()

        def K(name, i=0, rows=slice(0, 128)):
            return col[rows, names[name][0] + i:names[name][0] + i + 1]

        ident, ones, mean, blk, eps = C("ident"), C("ones"), C("mean"), C("blk"), C("eps")

        s_c = sem("s_consts")
        t_const = (s_c, 32)

        h_tok = [()] * 8

        NS, NH, AHEAD = 3, 3, 3
        stage = [Slot(sb(f"st{i}", [128, U])) for i in range(NS)]
        wh = [sb(f"wh{i}", [128, U], F32R) for i in range(NH)]
        wl = [sb(f"wl{i}", [128, U], F32R) for i in range(NH)]
        s_st = [sem(f"s_st{i}") for i in range(NS)]
        wfree = [None] * NH
        st = {"loaded": 0, "split": 0, "used": 0}
        split_tok = {}

        def load(n):
            s = stage[n % NS]
            S.wait(*s.free)
            S.dma(s.ap[:], units[n], s_st[n % NS])

        def split(n):
            src, i = stage[n % NS], n % NH
            landed = (s_st[n % NS], 16 * (n // NS + 1))
            thi = A.cp(wh[i][:], src.ap[:], landed, wfree[i])
            tlo = G.tt(wl[i][:], src.ap[:], wh[i][:].bitcast(F32), ALU.subtract, thi, landed)
            src.free = (thi, tlo)
            split_tok[n] = (thi, tlo)

        def feed():
            while st["loaded"] < min(st["split"] + NS, len(keys)):
                load(st["loaded"])
                st["loaded"] += 1

        def ahead(n):
            while st["split"] < min(n, len(keys)):
                feed()
                split(st["split"])
                st["split"] += 1
            feed()

        def take(key):
            n = st["used"]
            assert keys[n] == key, (keys[n], key)
            st["used"] += 1
            ahead(n + AHEAD)
            PE.wait(*split_tok.pop(n))
            return n % NH

        def done(i, tok):
            wfree[i] = tok

        def prod3(out, i, wsl, xh, xl, first, last, signal=None):
            PE.mm(out, wh[i][:, wsl], xh, first, False)
            PE.mm(out, wh[i][:, wsl], xl, False, False)
            return PE.mm(out, wl[i][:, wsl], xh, False, last, signal=last if signal is None else signal)

        def project(key, b, xh=None, xl=None, toks=None):
            nk = 8
            xh, xl, toks = (hh, hl, h_tok) if xh is None else (xh, xl, toks)
            i = take(key)
            PE.wait(*bank[b].free)
            for k in range(nk):
                PE.wait(*toks[k])
                t = prod3(bank[b].ap[:], i, slice(128 * k, 128 * k + 128), xh[:, k, :], xl[:, k, :], k == 0, k == nk - 1)
                if k == 3:
                    yield
            done(i, t)
            return t

        def pair(dst_h, dst_l, src, tok, lo=None):
            th = A.cp(dst_h, src, tok)
            tl = (lo or V).tt(dst_l, src, dst_h.bitcast(F32), ALU.subtract, tok, th)
            return th, tl

        def rnorm(dst, src, *after):
            t1 = A.act(dst, src, ACT.Ln, 1.0, eps, *after)
            return A.act(dst, dst, ACT.Exp, -0.5, None, t1)

        nacc = sb("nacc", [128, T])
        nr = sb("nr", [128, T])
        nm = {"t": None}

        def square(xt, k, tok):
            sq, = tmps(1)
            if k == 0:
                t = A.act(nacc[:], xt[:, k, :], ACT.Square, D ** -0.5, None, tok, nm["t"])
            else:
                t = A.act(sq.ap[:], xt[:, k, :], ACT.Square, D ** -0.5, None, tok, *sq.free)
                t = V.tt(nacc[:], nacc[:], sq.ap[:], ALU.add, t, nm["t"])
                sq.free = (t,)
            nm["t"] = t

        def norm_into_h(xt, gname):
            b = bank[7]
            t = PE.mm(b.ap[:], ones, nacc[:], True, True, nm["t"], *b.free, signal=True)
            nm["t"] = t
            t_r = rnorm(nr[:], b.ap[:], t)
            b.free = (t_r,)
            last = PE.last()
            late = None
            for k in range(8):
                hb, = tmps(1)
                th = V.stt(hb.ap[:], xt[:, k, :], K(gname, k), nr[:], ALU.mult, ALU.mult, t_r, *hb.free)
                t_hi = A.cp(hh[:, k, :], hb.ap[:], th, last)
                if late:
                    late()

                def late(k=k, hb=hb, th=th, t_hi=t_hi):
                    q = G if k % 4 == 3 else V
                    t_lo = q.tt(hl[:, k, :], hb.ap[:], hh[:, k, :].bitcast(F32), ALU.subtract, th, t_hi, last)
                    hb.free = (t_hi, t_lo)
                    h_tok[k] = (t_hi, t_lo)
            late()

        def halve(acc, m, tok, t_h):
            th = A.act(hh[:, m, :], acc[:, m, :], ACT.Copy, 0.5, None, tok, t_h)
            tl = V.stt(hl[:, m, :], acc[:, m, :], 0.5, hh[:, m, :].bitcast(F32), ALU.mult, ALU.subtract, tok, th)
            h_tok[m] = (th, tl)


        s_x = sem("s_x")
        s_x8 = [sem(f"s_x{k}") for k in range(8)]
        xn = [0]
        scratch = nc.dram_tensor("x_scratch", [128, 8, T], F32).ap()
        s_sc = sem("s_scratch")
        scn = [0]

        def spill(dst, slot, t):
            i = tmp.index(slot)
            S.dma(dst, slot.ap[:], s_gd[i], t)
            n_gd[i] += 16
            slot.free = ((s_gd[i], n_gd[i]),)

        def conv(ps, tok, wname, c, dst, bias=None):
            xp, = pads(1)
            t0 = A.cp(xp.ap[:, 3:3 + T], ps.ap[:], tok, *xp.free)
            w = lambda j: K(wname, 4 * c + j)
            t1 = A.act(dst, ps.ap[:], ACT.Identity, w(3), bias if bias is not None else 0.0)
            ps.free = (t1,)
            t = V.stt(dst, xp.ap[:, 2:2 + T], w(2), dst, ALU.mult, ALU.add, t0, t1)
            t = V.stt(dst, xp.ap[:, 1:1 + T], w(1), dst, ALU.mult, ALU.add, t)
            t = V.stt(dst, xp.ap[:, 0:T], w(0), dst, ALU.mult, ALU.add, t)
            xp.free = (t,)
            return t

        pad = [Slot(sb(f"pad{i}", [128, 16 + T])) for i in range(2)]
        pno = [0]
        for p in pad:
            p.free = (V.set(p.ap[:, 0:3], 0.0),)

        def pads(k):
            out = [pad[(pno[0] + i) % 2] for i in range(k)]
            pno[0] += k
            return out

        def silu2(dst, src, tok, *after):
            th, = tmps(1)
            t1 = A.act(th.ap[:], src, ACT.Tanh, 0.5, None, tok, *th.free)
            t2 = V.stt(dst, th.ap[:], 1.0, src, ALU.add, ALU.mult, t1, tok, *after)
            th.free = (t2,)
            return t2

        def rope(dst, src, rot, cos, sin, b, tok, width=T, take_tiles=None):
            t_p = PE.mm(bank[b].ap[:, 0:width], rot, src, True, True, tok, *bank[b].free, signal=True)
            s1, = (take_tiles or tmps)(1)
            t1 = V.tt(s1.ap[:, 0:width], bank[b].ap[:, 0:width], sin, ALU.mult, t_p, *s1.free)
            bank[b].free = (t1,)
            t2 = V.tt(dst, src, cos, ALU.mult, tok, t_p)
            t3 = V.tt(dst, dst, s1.ap[:, 0:width], ALU.add, t1, t2)
            s1.free = (t3,)
            return t3

        tabs = sb("tabs", [128, max(apack.n, bpack.n)])
        xstack = ExitStack()
        xt = sb("xt_in", [128, 8, T], stack=xstack)
        for k in range(8):
            S.dma(xt[:, k, :], x_in[:, k, :], s_x8[k])
            square(xt, k, (s_x8[k], 16))
        S.dma(col[:], cols, s_c)
        S.dma(cst[:], consts[:, 0:n_cst], s_c)
        for q in (PE, V, A, G):
            q.wait(t_const)
        ahead(1)
        x_src = x_in
        s_tab = sem("s_tab")
        S.dma(tabs[:, 0:apack.n], tabA, s_tab)
        t_lam = V.set(colx[:], 0.0)
        gates_d = nc.dram_tensor("gates", [24, 128, T], F32).ap()
        s_gd = [sem(f"s_gd{i}") for i in range(4)]
        n_gd = [0] * 4
        qk_d = nc.dram_tensor("qk", [128, 8, T], F32).ap()
        cd_d = consts[:, n_cst:cpack.n]
        s_gl = [sem(f"s_gl{i}") for i in range(3)]
        n_gl = [0] * 3

        for l in range(2):
            def TA(name):
                a, b = apack.at[name]
                return tabs[:, a:b]

            norm_into_h(xt, f"norm{l}")
            ahead(AHEAD)
            x_read = fence() + [(s_sc, scn[0]) if l else None]
            V.wait(*x_read)
            xstack.close()

            lay, dn = ExitStack(), ExitStack()
            yA = sb(f"yA{l}", [128, 4, T], stack=lay)
            bias3 = sb(f"bias{l}", [128, 256 + 384 + 512], stack=lay)
            wi = sb(f"wi{l}", [128, 4, 4], stack=lay)
            qi, ki = [sb(f"{n}i{l}", [128, 2, T], stack=dn) for n in "qk"]
            rw = sb(f"rw{l}", [128, T], stack=dn)
            tpc = sb(f"tpc{l}", [128, 2, 4, 4], stack=dn)
            gcol = sb(f"gcol{l}", [128, 4, 16], stack=dn)
            egl = sb(f"egl{l}", [128, 2, 4, 4], stack=dn)
            qf, kf, vf = [sb(f"{n}f{l}", [128, 4, T], stack=dn) for n in "qkv"]
            hb2 = sb(f"hb{l}", [128, 24], stack=dn)
            t_z = V.set(rw[:], 0.0)
            t_hb = V.ts(hb2[:], col[:, names[f"gateb{l}"][0]:names[f"gateb{l}"][1]], 0.5, ALU.mult, None, None)

            small = {}

            def phase1():
                t = yield from project(("small", l), 0)
                b = bank[0]
                e1, z1 = tmps(2)
                z2, z3 = tmps(2)
                R0, R1, R2 = slice(0, 4), slice(32, 36), slice(64, 68)
                ta = A.act(e1.ap[R0, :], b.ap[R0, :], ACT.Tanh, 0.5, None, t, *e1.free)
                tb = V.ts(rw[R0, :], e1.ap[R0, :], 1.0, ALU.add, 0.5, ALU.mult, ta, t_z)
                e1.free = (tb,)
                tc = V.ts(z1.ap[R1, :], b.ap[R1, :], K(f"dt{l}", 0, R1), ALU.add, None, None, ta, *z1.free)
                td = A.act(z2.ap[R1, :], z1.ap[R1, :], ACT.Abs, 1.0, None, tc, *z2.free)
                te = A.act(z2.ap[R1, :], z2.ap[R1, :], ACT.Exp, -1.0, None, td)
                te = A.act(z2.ap[R1, :], z2.ap[R1, :], ACT.Ln, 1.0, 1.0, te)
                tf = V.stt(z1.ap[R1, :], z1.ap[R1, :], 0.0, z2.ap[R1, :], ALU.max, ALU.add, te, tc)
                z2.free = (tf,)
                tg = A.act(colx[R1, 0:1], K(f"alog{l}", 0, R1), ACT.Exp, 1.0, None, t_lam)
                tf = V.ts(z1.ap[R1, :], z1.ap[R1, :], colx[R1, 0:1], ALU.mult, -1.0, ALU.mult, tf, tg)
                th = V.scan(rw[R1, :], C("reset")[R1, :], z1.ap[R1, :], 0.0, tf, t_z)
                z1.free = (th,)
                ti = V.ts(rw[R2, :], b.ap[R2, :], 1.0 / 16.0, ALU.mult, None, None, ta, t_z)
                b.free = (ta, tc, ti)
                small["rw"] = (tb, th, ti)
                for c in range(12):
                    b = (c + 1) % 3
                    t = yield from project(("p", l, 128 * c), b)
                    dst = (qf, kf, vf)[c // 4][:, c % 4, :]
                    cv, = tmps(1)
                    V.wait(*cv.free)
                    A.wait(*cv.free)
                    tcv = conv(bank[b], t, f"conv{l}", c, cv.ap[:])
                    small[("qkv", c)] = silu2(dst, cv.ap[:], tcv)
                    cv.free = (small[("qkv", c)],)
                    yield
            sa = {}

            def phase2():
                V.wait((s_tab, 16))
                def index_q(c, t):
                    r, = tmps(1)
                    ta = A.cp(r.ap[:], bank[c].ap[:], t, *r.free)
                    bank[c].free = (ta,)
                    yield
                    sa[("qi", c)] = rope(qi[:, c, :], r.ap[:], C("r64"), TA("cosI"), TA("sinI"), 3, ta)
                    r.free = (sa[("qi", c)],)

                def index_k(t):
                    r, r2 = tmps(2)
                    ta = A.cp(r.ap[:], bank[2].ap[:], t, *r.free)
                    bank[2].free = (ta,)
                    V.wait(*r2.free)
                    yield
                    tk = rope(r2.ap[:], r.ap[:], C("r64"), TA("cosI"), TA("sinI"), 3, ta)
                    r.free = (tk,)
                    sa["ki"] = [V.cp(ki[0:64, 0, :], r2.ap[0:64, :], tk), V.cp(ki[64:128, 1, :], r2.ap[64:128, :], tk),
                                V.set(ki[64:128, 0, :], 0.0), V.set(ki[0:64, 1, :], 0.0)]
                    r2.free = tuple(sa["ki"])

                def main_qk(c, t):
                    b = c % 2
                    x1, x2 = tmps(2)
                    tx = A.cp(x1.ap[:], bank[b].ap[:], t, *x1.free)
                    bank[b].free = (tx,)
                    ts_ = A.act(x2.ap[:], x1.ap[:], ACT.Square, 1.0, None, tx, *x2.free)
                    yield
                    tm = PE.mm(bank[3].ap[:], mean, x2.ap[:], True, True, ts_, *bank[3].free, signal=True)
                    tr = rnorm(x2.ap[:], bank[3].ap[:], tm)
                    bank[3].free = (tr,)
                    yield
                    name = f"qn{l}" if c < 4 else f"kn{l}"
                    tq = V.stt(x1.ap[:], x1.ap[:], K(name), x2.ap[:], ALU.mult, ALU.mult, tr, tx)
                    x2.free = (tq,)
                    yield
                    t = rope(x1.ap[:], x1.ap[:], C("r128"), TA("cosA"), TA("sinA"), 3, tq, take_tiles=lambda k: [x2])
                    spill(qk_d[:, c, :], x1, t)

                def gate(j, t):
                    n, m = (1, 0, 2)[j // 8], j % 8
                    g, = tmps(1)
                    t = A.act(g.ap[:], bank[j % 2].ap[:], ACT.Tanh, 0.5, hb2[:, 8 * n + m:8 * n + m + 1], t, t_hb, *g.free)
                    bank[j % 2].free = (t,)
                    spill(gates_d[8 * n + m], g, t)
                    yield

                def jobs():
                    for c in range(2):
                        yield project(("p", l, 5128 + 128 * c), c), lambda t, c=c: index_q(c, t)
                    yield project(("ik", l), 2), index_k
                    for c in range(8):
                        yield project(("p", l, 3080 + 128 * c), c % 2), lambda t, c=c: main_qk(c, t)
                    for j in range(24):
                        n, m = (1, 0, 2)[j // 8], j % 8
                        yield project(("p", l, 5452 + 1024 * n + 128 * m), j % 2), lambda t, j=j: gate(j, t)

                yield from lagged(jobs())

            def delta():
                A.wait(*x_read)
                for f in range(2):
                    aa = sts(2) + [Slot(XX[0]), Slot(XX[1])]
                    tt_ = []
                    for c in range(4 * f, 4 * f + 4):
                        dst = (qf, kf)[f][:, c % 4, :]
                        a = aa[c % 4]
                        tt_.append(A.act(a.ap[:], dst, ACT.Square, 0.5, None, small[("qkv", c)], *a.free, small.get(("n", c - 4))))
                    yield
                    for c in range(4):
                        b = bank[4 + c]
                        tt_[c] = PE.mm(b.ap[:], ones, aa[c].ap[:], True, True, tt_[c], *b.free, signal=True)
                    yield
                    for c in range(4):
                        tt_[c] = rnorm(aa[c].ap[:], bank[4 + c].ap[:], tt_[c])
                        bank[4 + c].free = (tt_[c],)
                    for c in range(4):
                        dst = (qf, kf)[f][:, c, :]
                        t = V.stt(dst, dst, 0.5 * (1.0 if f else 128.0 ** -0.5), aa[c].ap[:], ALU.mult, ALU.mult, tt_[c])
                        aa[c].free = (t,)
                        small[("n", 4 * f + c)] = t
                    yield
                b = bank[4]
                PE.wait(*small["rw"])
                for i in range(4):
                    t = PE.tr(b.ap[:, 128 * i:128 * i + 128], rw[:, 128 * i:128 * i + 128], ident, *(b.free if i == 0 else ()), signal=i == 3)
                bv = b.ap[:].rearrange("p (a b) -> p a b", a=4)
                gc, beta = tpc[:, 0, :, :], tpc[:, 1, :, :]
                V.cp(gc, bv[:, :, 32:36], t)
                t_c = V.cp(beta, bv[:, :, 0:4])
                t_wi = V.cp(wi[:], bv[:, :, 64:68])
                b.free = (t_wi,)
                sa["wi"] = t_wi
                yield
                b = bank[5]
                last = C("last")
                PE.mm(b.ap[:, 0:16], last, gc, True, True, t_c, *b.free, share=True)
                for p in range(2):
                    sel = ident[:, 63 + 64 * p:64 + 64 * p].broadcast_to([128, 128])
                    t = PE.mm(b.ap[:, 16 + 16 * p:32 + 16 * p], sel, gc, True, True, share=True, signal=p == 1)
                t_gl = A.act(egl[:].rearrange("p a b c -> p (a b c)"), b.ap[:, 16:48], ACT.Exp, 1.0, None, t)
                t1 = V.tt(gcol[:, :, 4:8], b.ap[:, 0:16].rearrange("p (a b) -> p a b", a=4), gc, ALU.subtract, t_gl, t_c)
                b.free = (t_gl, t1)
                t2 = A.act(gcol[:, :, 4:8], gcol[:, :, 4:8], ACT.Exp, 1.0, None, t1)
                t3 = A.act(gcol[:, :, 0:4], gc, ACT.Exp, 1.0, None, t_c)
                t4 = V.tt(gcol[:, :, 0:4], gcol[:, :, 0:4], beta, ALU.mult, t3)
                t5 = V.ts(gcol[:, :, 8:12], beta, 0.5, ALU.mult, None, None, t_c)
                t_col = (t2, t4, t5)
                yield
                f4 = lambda ap: ap.rearrange("p (a b) -> p a b", a=4)
                R, frec = {}, ({}, {})

                def head(h, e):
                    rec = frec[e]
                    lT, mT, Y, X, XT, kb, vb = hset[e]
                    dT, eg = mT, Y
                    kT, qT = kf[:, h, :], qf[:, h, :]
                    t_k, t_q = small[("n", 4 + h)], small[("n", h)]
                    b4, b5, b6, b7 = bank[4 + e], bank[6], bank[7], bank[4 + e]
                    sel = ident[:, 32 + h:33 + h].broadcast_to([128, 128])
                    tG = PE.mm(b4.ap[:], sel, rw[:], True, True, *b4.free, signal=True)
                    t_eg = A.act(eg[:], b4.ap[:], ACT.Exp, 1.0, None, tG, *rec.get("Y", ()))
                    t_d = V.tt(f4(dT[:]), f4(b4.ap[:]), gc[:, :, h:h + 1].broadcast_to([128, 4, 128]), ALU.subtract, t_eg, *rec.get("mT", ()))
                    b4.free = (t_d, t_eg)
                    t_d = V.tt(f4(dT[:]), f4(dT[:]), C("decay").unsqueeze(1).broadcast_to([128, 4, 128]), ALU.add, t_d)
                    t_d = A.act(dT[:], dT[:], ACT.Exp, 1.0, None, t_d)
                    yield
                    PE.wait(t_k, t_q, *b5.free, *b6.free)
                    for i in range(4):
                        s = slice(128 * i, 128 * i + 128)
                        PE.mm(b5.ap[:, s], kT[:, s], qT[:, s], True, True)
                    for i in range(4):
                        s = slice(128 * i, 128 * i + 128)
                        tkk = PE.mm(b6.ap[:, s], kT[:, s], kT[:, s], True, True, signal=i == 3)
                    for p in range(2):
                        r = slice(64 * p, 64 * p + 64)
                        t_at = V.tt(aT[r, h, :, :], f4(b5.ap[:])[r, :, r], f4(dT[:])[r, :, r], ALU.mult, tkk, t_d)
                    b5.free = (t_at,)
                    t_l = V.tt(lT[:], b6.ap[:], dT[:], ALU.mult, tkk, t_d, *rec.get("lT", ()))
                    b6.free = (t_l,)
                    rec["mT"] = (t_at, t_l)
                    t_qg = G.tt(qT, qT, eg[:], ALU.mult, t_eg, tkk)
                    rec["Y"] = (t_qg,)
                    R[("q", h)] = t_qg
                    R[("a", h)] = t_at
                    for i in range(4):
                        s = slice(128 * i, 128 * i + 128)
                        t1 = PE.tr(b7.ap[:, s], kT[:, s], ident, *(b7.free if i == 0 else ()), signal=i == 3)
                    bc = lambda j: gcol[:, :, 4 * j + h:4 * j + h + 1].broadcast_to([128, 4, 128])
                    t_kb = V.tt(f4(kb[:]), f4(b7.ap[:]), bc(0), ALU.mult, t1, *t_col, *rec.get("kb", ()))
                    t_kd = V.tt(kd[:, h, :, :], f4(b7.ap[:]), bc(1), ALU.mult, t1, *t_col)
                    b7.free = (t_kb, t_kd)
                    R[("kd", h)] = t_kd
                    yield
                    sel = ident[:, h:h + 1].broadcast_to([128, 128])
                    tB = PE.mm(b4.ap[:], sel, rw[:], True, True, *b4.free, signal=True)
                    t_l = V.tt(lT[:], lT[:], b4.ap[:], ALU.mult, tB, t_l)
                    b4.free = (t_l,)
                    for i in range(4):
                        s = slice(128 * i, 128 * i + 128)
                        t1 = PE.tr(b7.ap[:, s], vf[:, h, s], ident, *((small[("qkv", 8 + h)],) + tuple(b7.free) if i == 0 else ()), signal=i == 3)
                    t_vb = V.tt(f4(vb[:]), f4(b7.ap[:]), bc(2), ALU.mult, t1, *rec.get("vb", ()))
                    b7.free = (t_vb,)
                    yield
                    lv = C("levels").rearrange("p (n i) -> p n i", n=6)
                    idb = ident.unsqueeze(1).broadcast_to([128, 4, 128])
                    tX = tXT = None

                    def mask(n):
                        return V.tt(f4(mT[:]), f4(lT[:]), lv[:, n, :].unsqueeze(1).broadcast_to([128, 4, 128]), ALU.mult, t_l, *rec.get("mT", ()))

                    tm = mask(0)
                    for n in range(6):
                        if n == 0:
                            for i in range(4):
                                s = slice(128 * i, 128 * i + 128)
                                t = PE.mm(b4.ap[:, s], mT[:, s], ident, True, True, *((tm,) + tuple(b4.free) if i == 0 else ()), signal=i == 3)
                            tX = V.tt(f4(X[:]), idb, f4(b4.ap[:]), ALU.subtract, t, *rec.get("X", ()))
                            tXT = V.tt(f4(XT[:]), idb, f4(mT[:]), ALU.subtract, tm, *rec.get("XT", ()))
                            b4.free = (tX,)
                            rec["mT"] = (tXT, t)
                            tm = mask(1)
                            yield
                            continue
                        for i in range(4):
                            s = slice(128 * i, 128 * i + 128)
                            t = PE.mm(b4.ap[:, s], mT[:, s], X[:, s], True, True, *((tm, tX) + tuple(b4.free) if i == 0 else ()), signal=i == 3)
                        rec["mT"] = (t,)
                        tY = A.cp(Y[:], b4.ap[:], t, *rec.get("Y", ()))
                        b4.free = (tY,)
                        if n < 5:
                            tm = mask(n + 1)
                        yield
                        PE.wait(tY, tXT, *b5.free, *b6.free)
                        for i in range(4):
                            s = slice(128 * i, 128 * i + 128)
                            if n < 5:
                                PE.mm(b5.ap[:, s], XT[:, s], Y[:, s], True, True)
                            t = PE.mm(b6.ap[:, s], Y[:, s], XT[:, s], True, True, signal=i == 3)
                        rec["Y"] = (t,)
                        if n < 5:
                            tX = V.tt(X[:], X[:], b5.ap[:], ALU.subtract, t, tX)
                            b5.free = (tX,)
                        else:
                            rec["X"] = (t,)
                        tXT = V.tt(XT[:], XT[:], b6.ap[:], ALU.subtract, t, tXT)
                        b6.free = (tXT,)
                        yield
                    rec["lT"] = (tm,)
                    PE.wait(tXT, t_kb, t_vb, *b4.free, *b5.free)
                    for i in range(4):
                        s = slice(128 * i, 128 * i + 128)
                        PE.mm(b4.ap[:, s], XT[:, s], vb[:, s], True, True)
                        t = PE.mm(b5.ap[:, s], kb[:, s], XT[:, s], True, True, signal=i == 3)
                    rec["vb"] = rec["kb"] = rec["XT"] = (t,)
                    R[("u", h)] = A.cp(vf[:, h, :], b4.ap[:], t)
                    b4.free = (R[("u", h)],)
                    R[("w", h)] = A.cp(kf[:, h, :], b5.ap[:], t)
                    b5.free = (R[("w", h)],)
                    yield
                yield from staggered(head(0, 0), head(1, 1))
                yield from staggered(head(2, 0), head(3, 1))
                rec = R
                u4 = vf[:].rearrange("p h (b d) -> p h b d", b=4)
                tS = tvn = tPS = t_o = None
                t_hn = V.ts(colx[:, 1:2], K(f"onorm{l}"), 0.5, ALU.mult, None, None, t_lam)
                for n in range(8):
                    i, p = n // 2, n % 2
                    r = slice(64 * p, 64 * p + 64)
                    cs = slice(64 * n, 64 * n + 64)
                    b4 = bank[4]
                    if n > 0:
                        PE.wait(tS, *b4.free, *[rec[("w", h)] for h in range(4)])
                        for h in range(4):
                            t = PE.mm(b4.ap[r, 128 * h:128 * h + 128], kf[:, h, cs], Sx[:, h, :], True, True, signal=h == 3)
                        V.wait(*[rec[("u", h)] for h in range(4)])
                        tvn = V.tt(vn[r, :, :], u4[r, :, i, :], b4.ap[r, :].rearrange("p (h d) -> p h d", h=4), ALU.subtract, t, tPS)
                        b4.free = (tvn,)
                    else:
                        tvn = V.cp(vn[r, :, :], u4[r, :, i, :], *[rec[("u", h)] for h in range(4)])
                    yield
                    ob, Sb = bank[6], bank[7]
                    PE.wait(tvn, *Sb.free, *[rec[("kd", h)] for h in range(4)])
                    for h in range(4):
                        t_s = PE.mm(Sb.ap[:, 128 * h:128 * h + 128], kd[r, h, i, :], vn[r, h, :], True, True, signal=h == 3)
                    PE.wait(*(ob.free if p == 0 else ()), *[rec[("q", h)] for h in range(4)], *[rec[("a", h)] for h in range(4)])
                    for h in range(4):
                        o = ob.ap[:, 128 * h + 64 * p:128 * h + 64 * p + 64]
                        if n > 0:
                            PE.mm(o, Sx[:, h, :], qf[:, h, cs], True, False, share=True)
                        t_o = PE.mm(o, vn[r, h, :], aT[r, h, i, :], n == 0, True, signal=h == 3, share=True)
                    tPS = t_o
                    if n == 0:
                        tS = V.cp(Sx[:].rearrange("p h d -> p (h d)"), Sb.ap[:], t_s)
                    else:
                        e = egl[:, p, i, :].unsqueeze(2).broadcast_to([128, 4, 128])
                        tS = V.tt(Sx[:], Sx[:], e, ALU.mult, t_o, tS, t_gl)
                        tS = V.tt(Sx[:].rearrange("p h d -> p (h d)"), Sx[:].rearrange("p h d -> p (h d)"), Sb.ap[:], ALU.add, t_s, tS)
                    Sb.free = (tS,)
                    if p == 1:
                        t = A.cp(yA[:, :, 128 * i:128 * i + 128], ob.ap[:].rearrange("p (h t) -> p h t", h=4), t_o)
                        ob.free = (t,)
                    yield
                aa = sts(2) + [Slot(XX[0]), Slot(XX[1])]
                tt_ = []
                for c in range(4):
                    tt_.append(A.act(aa[c].ap[:], yA[:, c, :], ACT.Square, 1.0, None, t, *aa[c].free))
                yield
                for c in range(4):
                    b = bank[4 + c]
                    tt_[c] = PE.mm(b.ap[:], mean, aa[c].ap[:], True, True, tt_[c], *b.free, signal=True)
                yield
                for c in range(4):
                    tt_[c] = rnorm(aa[c].ap[:], bank[4 + c].ap[:], tt_[c])
                    bank[4 + c].free = (tt_[c],)
                for c in range(4):
                    t = V.stt(yA[:, c, :], yA[:, c, :], colx[:, 1:2], aa[c].ap[:], ALU.mult, ALU.mult, tt_[c], t_hn)
                    aa[c].free = (t,)
                    small[("yA", c)] = t
                yield

            dtmp = ExitStack()
            hset = [[sb(f"{n}{e}{l}", [128, T], stack=dtmp) for n in ("lT", "mT", "Y", "X", "XT", "kb", "vb")] for e in range(2)]
            XX = [hset[0][3], hset[1][3]]
            aT = sb(f"aT{l}", [128, 4, 4, 64], stack=dtmp)
            kd = sb(f"kd{l}", [128, 4, 4, 128], stack=dtmp)
            Sx = sb(f"Sx{l}", [128, 4, 128], stack=dtmp)
            vn = sb(f"vn{l}", [128, 4, 128], stack=dtmp)
            stl = [Slot(sb(f"sd{l}{i}", [128, T], stack=dtmp)) for i in range(2)]
            sno = [0]

            def sts(k):
                out = [stl[(sno[0] + i) % 2] for i in range(k)]
                sno[0] += k
                return out

            def select():
                m8, sc = m8s, scs
                ta = None
                for b in range(1, 4):
                    while ("wi" not in sa) or ("ki" not in sa):
                        yield
                    nk = 128 * (b + 1)
                    qsl = slice(128 * b, 128 * b + 128)
                    for h in range(4):
                        bk = bank[2]
                        t = PE.mm(bk.ap[:, 0:nk], qi[:, h // 2, qsl], ki[:, h % 2, 0:nk], True, True, *bk.free, *sa["ki"], sa[("qi", h // 2)], signal=True)
                        t = A.act(bk.ap[:, 0:nk], bk.ap[:, 0:nk], ACT.Relu, 1.0, None, t)
                        yield
                        if h == 0:
                            ta = V.ts(sc[:, 0:nk], bk.ap[:, 0:nk], wi[:, b, 0:1], ALU.mult, None, None, t, sa["wi"], ta)
                        else:
                            ta = V.stt(sc[:, 0:nk], bk.ap[:, 0:nk], wi[:, b, h:h + 1], sc[:, 0:nk], ALU.mult, ALU.add, t, ta)
                        bk.free = (ta,)
                    ta = V.tt(sc[:, nk - 128:nk], sc[:, nk - 128:nk], cdiag[:], ALU.add, ta, t_cd)
                    for r in range(16):
                        tm = V.max8(m8[:, 0:8], sc[:, 0:nk], ta)
                        ta = V.replace(sc[:, 0:nk], m8[:, 0:8], sc[:, 0:nk], MARK, tm)
                        if r % 2 == 1:
                            yield
                    o = (0, 0, 256, 640)[b]
                    ta = V.ts(bias3[:, o:o + nk], sc[:, 0:nk], -2.0e38, ALU.is_gt, NEG, ALU.mult, ta)
                    sa[("sel", b)] = ta
                    yield

            m8s = sb(f"m8s{l}", [128, 8], stack=dtmp)
            scs = sb(f"scs{l}", [128, T], stack=dtmp)
            cdiag = sb(f"cdiag{l}", [128, 128], stack=dtmp)
            s_cd = sem(f"s_cd{l}")
            S.wait(V.last(), A.last())
            S.dma(cdiag[:], cd_d[:, 384:512], s_cd)
            t_cd = (s_cd, 16)
            for _ in phase1():
                pass
            weave(phase2(), (delta(), RATES[0]), (select(), RATES[1]))
            p2_read = fence()
            V.wait(*p2_read)
            dtmp.close()
            dn.close()
            p3 = ExitStack()
            qs, ks, vs, zc = [sb(f"{n}{l}", [128, 4, T], stack=p3) for n in ("qs", "ks", "vs", "zc")]
            acc = sb(f"acc{l}", [128, 8, T], stack=p3)
            yh, yl = [sb(f"{n}{l}", [128, 4, T], F32R, stack=p3) for n in ("yh", "yl")]
            cdg = sb(f"cdg{l}", [128, 128], stack=p3)
            pw = sb(f"pw{l}", [128, 4, 128], stack=p3)
            m8 = sb(f"m8{l}", [128, 16], stack=p3)
            st2 = sb(f"stat{l}", [128, 8], stack=p3)
            Lx = [Slot(sb(f"Lx{l}{i}", [128, T], stack=p3)) for i in range(3)]
            Px = [Slot(sb(f"Px{l}{i}", [128, 4, 128], stack=p3)) for i in range(3)]
            gt = [Slot(sb(f"gt{l}{i}", [128, T], stack=p3)) for i in range(3)]
            s_pw = sem(f"s_pw{l}")
            S.wait(*p2_read, *[(s_gd[i], n_gd[i]) for i in range(4)])
            S.dma(pw[:], poolw[l], s_pw)
            S.dma(cdg[:], cd_d[:, 384:512], s_pw)
            S.dma(qs[:], qk_d[:, 0:4, :], s_pw)
            S.dma(ks[:], qk_d[:, 4:8, :], s_pw)
            t_pw = (s_pw, 64)
            yt = {}
            order = [8 * n + m for n in (1, 0, 2) for m in range(8)]
            gq = {"n": 0}

            def gate_loads(upto):
                while gq["n"] < min(upto, 24):
                    j = gq["n"]
                    g = gt[j % 3]
                    S.dma(g.ap[:], gates_d[order[j]], s_gl[j % 3], *g.free)
                    n_gl[j % 3] += 16
                    g.tok = (s_gl[j % 3], n_gl[j % 3])
                    gq["n"] += 1

            gate_loads(3)

            def vtok():
                for b in range(4):
                    PE.wait(*bank[b].free)
                for j in range(4):
                    i = take(("v", l, j))
                    for b in range(4):
                        s = slice(128 * b, 128 * b + 128)
                        for kk in range(2):
                            k = 2 * j + kk
                            w = slice(512 * kk, 512 * kk + 512)
                            PE.mm(bank[b].ap[:], hh[:, k, s], wh[i][:, w], k == 0, False)
                            PE.mm(bank[b].ap[:], hl[:, k, s], wh[i][:, w], False, False)
                            t = PE.mm(bank[b].ap[:], hh[:, k, s], wl[i][:, w], False, k == 7, signal=kk == 1)
                        if j == 3:
                            A.wait(*p2_read)
                            yt[("v", b)] = A.cp(vs[:, b, :], bank[b].ap[:], t)
                            bank[b].free = (yt[("v", b)],)
                    done(i, t)
                    yield

            def pool():
                zs = {}

                def gate_of(g, t):
                    z, = tmps(1)
                    V.wait(*z.free)
                    tz = silu2(z.ap[:], bank[0].ap[:], t)
                    bank[0].free = (tz,)
                    zs[g] = (z, tz)
                    yield

                def pooled(g, t):
                    z, tz = zs[g]
                    p0, p1 = pads(2)
                    tu = A.cp(p0.ap[:, 16:16 + T], bank[1].ap[:], t, *p0.free)
                    bank[1].free = (tu,)
                    u, = tmps(1)
                    t0 = V.cp(u.ap[:], p0.ap[:, 16:16 + T], tu, *u.free)
                    tz0 = V.set(p0.ap[:, 0:16], 0.0, *p0.free)
                    tz1 = V.set(p1.ap[:, 0:16], 0.0, *p1.free)
                    a, b_ = p0, p1
                    tt_ = tz0
                    for n in range(g + 1):
                        s = 2 ** n
                        tt_ = V.tt(b_.ap[:, 16:16 + T], a.ap[:, 16:16 + T], a.ap[:, 16 - s:16 - s + T], ALU.add, tt_, t0, tz1, tu)
                        a, b_ = b_, a
                    win = 2 ** (g + 1)
                    cnt = C("count").rearrange("p (g n) -> p g n", g=4)
                    th = V.tt(m8[:], a.ap[:, 16:32], cnt[:, g, :], ALU.mult, tt_, *yt.get("m8", ()))
                    th = V.tt(m8[:], m8[:], u.ap[:, 0:16], ALU.subtract, th)
                    tp = V.stt(u.ap[:], a.ap[:, 16:16 + T], 1.0 / win, u.ap[:], ALU.mult, ALU.subtract, th)
                    tp = V.cp(u.ap[:, 0:16], m8[:], tp)
                    yt["m8"] = (tp,)
                    p0.free = (tp,)
                    p1.free = (tp,)
                    yield
                    yield
                    tm = PE.mm(bank[2].ap[:], pw[:, g, :], u.ap[:], True, True, tp, t_pw, *bank[2].free, signal=True)
                    u.free = (tm,)
                    ty = V.stt(z.ap[:], bank[2].ap[:], K(f"pscale{l}", g), z.ap[:], ALU.mult, ALU.mult, tm, tz)
                    bank[2].free = (ty,)
                    ty = V.ts(z.ap[:], z.ap[:], 0.5, ALU.mult, None, None, ty)
                    th, tl = pair(yh[:, g, :], yl[:, g, :], z.ap[:], ty)
                    z.free = (th, tl)
                    yt[("B", g)] = (th, tl)

                def gated(c, t):
                    z, = tmps(1)
                    t = silu2(z.ap[:], bank[c % 2].ap[:], t, *z.free)
                    bank[c % 2].free = (t,)
                    yt[("A", c)] = V.tt(yA[:, c, :], yA[:, c, :], z.ap[:], ALU.mult, t, small[("yA", c)])
                    z.free = (yt[("A", c)],)
                    yield

                def jobs():
                    for g in range(4):
                        yield project(("p", l, 2568 + 128 * g), 0), lambda t, g=g: gate_of(g, t)
                        yield project(("p", l, 2056 + 128 * g), 1), lambda t, g=g: pooled(g, t)
                    for c in range(4):
                        yield project(("p", l, 1536 + 128 * c), c % 2), lambda t, c=c: gated(c, t)

                yield from lagged(jobs())
                for p in pad:
                    V.wait(*p.free)
                    p.free = (V.set(p.ap[:, 0:3], 0.0),)

            def zproj():
                for c in range(4):
                    t = yield from project(("p", l, 4616 + 128 * c), c % 3)
                    yt[("zc", c)] = silu2(zc[:, c, :], bank[c % 3].ap[:], t)
                    bank[c % 3].free = (yt[("zc", c)],)
                    yield

            def parts(src, toks):
                t_pe = PE.last()
                out = []
                for c in range(4):
                    A.wait(t_pe, *toks)
                    out += pair(yh[:, c, :], yl[:, c, :], src[:, c, :], toks[-1])
                return out

            def merge(n, ytoks):
                t_h = PE.last()
                for mp in range(4):
                    ib = take(("br", l, n, mp))
                    for j in range(2):
                        m = 2 * mp + j
                        b = bank[m % 4]
                        PE.wait(*b.free)
                        for k in range(4):
                            PE.wait(*ytoks[2 * k:2 * k + 2])
                            w = slice(512 * j + 128 * k, 512 * j + 128 * k + 128)
                            tb = prod3(b.ap[:], ib, w, yh[:, k, :], yl[:, k, :], k == 0, k == 3)
                        if j == 1:
                            done(ib, tb)
                        i = order.index(8 * n + m)
                        gate_loads(i + 1)
                        g = gt[i % 3]
                        if n == 1:
                            ta = V.stt(acc[:, m, :], g.ap[:], 1.0, b.ap[:], ALU.add, ALU.mult, g.tok, tb)
                            b.free = (ta,)
                        else:
                            ta = V.stt(g.ap[:], g.ap[:], 1.0, b.ap[:], ALU.add, ALU.mult, g.tok, tb)
                            b.free = (ta,)
                            ta = V.tt(acc[:, m, :], acc[:, m, :], g.ap[:], ALU.add, ta, yt[("acc", m)])
                        g.free = (ta,)
                        gate_loads(i + 4)
                        yt[("acc", m)] = ta
                        if n == 2:
                            halve(acc, m, ta, t_h)
                        yield

            def sparse():
                u = [(b, h) for b in range(4) for h in range(4)]
                while ("zc", 3) not in yt:
                    yield
                t_sc, t_p = {}, {}
                for n in range(len(u) + 4):
                    if n >= 4:
                        b, h = u[n - 4]
                        ob, P = bank[7], Px[(n - 4) % 3]
                        PE.wait(t_p[n - 4], *(ob.free if h == 0 else ()), *[yt[("v", i)] for i in range(b + 1)])
                        for i in range(b + 1):
                            t = PE.mm(ob.ap[:, 128 * h:128 * h + 128], vs[:, i, 128 * h:128 * h + 128], P.ap[:, i, :], i == 0, i == b, signal=i == b, share=True)
                        P.free = (t,)
                        if h == 3:
                            q = slice(128 * b, 128 * b + 128)
                            t = V.stt(zc[:, :, q], zc[:, :, q], 0.5, ob.ap[:].rearrange("p (h t) -> p h t", h=4), ALU.mult, ALU.mult, t, *[yt[("zc", c)] for c in range(4)])
                            ob.free = (t,)
                            yt[("C", b)] = t
                    if 2 <= n <= len(u) + 1:
                        b, h = u[n - 2]
                        bk, L, P = bank[4 + (n - 2) % 3], Lx[(n - 2) % 3], Px[(n - 2) % 3]
                        for i in range(b + 1):
                            t = PE.tr(bk.ap[:, 128 * i:128 * i + 128], L.ap[:, 128 * i:128 * i + 128], ident, *((t_sc[n - 2], *bk.free) if i == 0 else ()), signal=i == b)
                        L.free = (t,)
                        t_p[n - 2] = A.cp(P.ap[:, 0:b + 1, :].rearrange("p a b -> p (a b)"), bk.ap[:, 0:128 * (b + 1)], t, *P.free)
                        bk.free = (t_p[n - 2],)
                    if n < len(u):
                        b, h = u[n]
                        nk = 128 * (b + 1)
                        bk, L = bank[4 + n % 3], Lx[n % 3]
                        t = PE.mm(bk.ap[:, 0:nk], qs[:, h, 128 * b:128 * b + 128], ks[:, h, 0:nk], True, True, *bk.free, t_pw, signal=True)
                        mx, sm = st2[:, 2 * (n % 3):2 * (n % 3) + 1], st2[:, 2 * (n % 3) + 1:2 * (n % 3) + 2]
                        o = (0, 0, 256, 640)[b]
                        bias, t_b = (cdg[:], t_pw) if b == 0 else (bias3[:, o:o + nk], sa[("sel", b)])
                        t = V.addred(L.ap[:, 0:nk], bk.ap[:, 0:nk], bias, -(128.0 ** -0.5), 3.0e38, ALU.min, mx, t, t_b, *L.free)
                        bk.free = (t,)
                        t = A.act(L.ap[:, 0:nk], L.ap[:, 0:nk], ACT.Exp, -1.0, mx, t, acc=sm)
                        tr = V.rec(sm, sm, t)
                        t_sc[n] = V.ts(L.ap[:, 0:nk], L.ap[:, 0:nk], sm, ALU.mult, None, None, tr, t)
                    yield

            def front():
                yield from vtok()
                yield from zproj()
                yield from pool()
                yield from merge(1, sum([yt[("B", g)] for g in range(4)], ()))
                yield from merge(0, parts(yA, [yt[("A", c)] for c in range(4)]))

            weave(front(), (sparse(), RATES[2]))
            for _ in merge(2, parts(zc, [yt[("C", b)] for b in range(4)])):
                pass
            last = fence()
            p3.close()
            lay.close()
            xstack = ExitStack()
            xt = sb(f"xt{l}", [128, 8, T], stack=xstack)
            S.wait(*last)
            if l > 0:
                S.wait((s_sc, scn[0]))
            xn[0] += 16
            S.dma(xt[:], x_src, s_x)
            t_x = (s_x, xn[0])
            x_toks = []
            for m in range(8):
                for _ in project(("o", l, m), m % 4):
                    pass
                t = PE.last()
                tx = V.tt(xt[:, m, :], xt[:, m, :], bank[m % 4].ap[:], ALU.add, t, t_x)
                bank[m % 4].free = (tx,)
                x_toks.append(tx)
                square(xt, m, tx)
            S.dma(scratch, xt[:], s_sc, x_toks[-1])
            scn[0] += 16
            x_src = scratch

        S.dma(tabs[:, 0:bpack.n], tabB, s_tab, PE.last(), V.last(), A.last())

        def TB(name):
            a, b = bpack.at[name]
            return tabs[:, a:b]

        CP = 8.0
        lc = colx[:, 8:48]
        lam = col[:, names["lam"][0]:names["lam"][1]]
        t = A.act(lc[:, 0:8], lam, ACT.Abs, 1.0, None, t_lam)
        t = A.act(lc[:, 0:8], lc[:, 0:8], ACT.Exp, -1.0, None, t)
        t = A.act(lc[:, 0:8], lc[:, 0:8], ACT.Ln, 1.0, 1.0, t)
        t1 = V.ts(lc[:, 8:16], lam, -1.0, ALU.mult, 0.0, ALU.max, t_lam)
        t = V.tt(lc[:, 8:16], lc[:, 8:16], lc[:, 0:8], ALU.add, t, t1)
        t = V.ts(lc[:, 8:16], lc[:, 8:16], CP, ALU.mult, 0.5, ALU.mult, t)
        t = V.ts(lc[:, 0:8], lc[:, 8:16], -1.0, ALU.mult, None, None, t)
        t1 = V.ts(lc[:, 16:24], col[:, names["ba"][0]:names["ba"][1]], 0.5, ALU.mult, None, None, t_lam)
        t2 = V.ts(lc[:, 24:32], col[:, names["bx"][0]:names["bx"][1]], 0.5, ALU.mult, None, None, t_lam)
        t_lc = (t, t1, t2)
        norm_into_h(xt, "nrmA")
        ahead(st["used"] + AHEAD)
        last = fence() + [(s_sc, scn[0])]
        V.wait(*last)
        A.wait(*last)
        xstack.close()

        b2, comp = ExitStack(), ExitStack()
        q2 = sb("q2", [128, 4, T], stack=b2)
        kz = sb("kz", [128, 4, T], stack=b2)
        vt = sb("vt", [128, 4, 280], stack=b2)
        gs = sb("gs", [128, 4, 24], stack=b2)
        kcz = sb("kcz", [128, 2, 31], stack=b2)
        vcm = sb("vcm", [31, 2, 64], stack=b2)
        onT = sb("onT", [128, 4, T], stack=b2)
        lw = [Slot(sb(f"lw{i}", [128, 2, 128], stack=b2)) for i in range(2)]
        s_lr = [sem(f"s_lr{i}") for i in range(2)]
        cau = sb("cau", [128, 512], stack=b2)
        oh, ol = [sb(n, [128, 8, T], F32R, stack=b2) for n in ("oh", "ol")]
        lt = [Slot(sb(f"lt{i}", [128, T], stack=b2)) for i in range(4)]
        kc, kg, ph, zt = (sb("kc", [128, T], stack=comp), sb("kg", [128, 2, T], stack=comp),
                          sb("ph", [128, 8, 256], stack=comp), sb("zt", [128, 16, 62], stack=comp))
        vc = sb("vc", [128, T], stack=comp)
        p2 = sb("p2", [128, 2, 2, 64], stack=comp)
        ge = [sb(f"ge{i}", [62, 256], stack=comp) for i in range(3)]
        hid = sb("hid", [128, 2, 62], stack=comp)
        ctile = [Slot(sb(f"ctile{i}", [128, 32], stack=comp)) for i in range(4)]
        cno = [0]

        def ctiles(k):
            cno[0] += k
            return [ctile[(cno[0] - k + i) % 4] for i in range(k)]

        s_lw = sem("s_lw")
        S.wait(*last)
        for c in range(2):
            S.dma(lw[c].ap[:], lruw[:, :, c, :], s_lr[c])
        s_ph = sem("s_ph")
        S.dma(ph[:], phi1[0, :, 0:8, :], s_ph)
        S.dma(p2[:], phi2, s_lw)
        S.dma(cau[:], cd_d, s_lw)
        y2 = {}

        t_kz = V.set(kz[:].rearrange("p a b -> p (a b)"), 0.0, *last)
        t_kcz = V.set(kcz[:].rearrange("p a b -> p (a b)"), 0.0, *last)

        def headnorm(x, t, wcol, b, width=T, take_tiles=None):
            a, = (take_tiles or tmps)(1)
            t1 = A.act(a.ap[:, 0:width], x, ACT.Square, 0.125, None, t, *a.free)
            yield
            tm = PE.mm(bank[b].ap[:, 0:width], blk, a.ap[:, 0:width], True, True, t1, *bank[b].free, signal=True)
            tr = rnorm(a.ap[:, 0:width], bank[b].ap[:, 0:width], tm)
            bank[b].free = (tr,)
            yield
            tq = V.stt(x, x, wcol, a.ap[:, 0:width], ALU.mult, ALU.mult, tr, t)
            a.free = (tq,)
            yield
            return tq

        def proj2():
            V.wait((s_tab, 32))
            def query(c, t):
                x = lt[c]
                t = A.cp(x.ap[:], bank[c % 3].ap[:], t, *x.free)
                bank[c % 3].free = (t,)
                t = yield from headnorm(x.ap[:], t, K("qn2"), 3)
                t = rope(q2[:, c, :], x.ap[:], TB("r16"), TB("cos"), TB("sin"), 3, t)
                x.free = (t,)
                y2[("q", c)] = t

            def plain(j, dst, t):
                t = A.cp(dst[:], bank[j].ap[:], t)
                bank[j].free = (t,)
                y2[("c", j)] = t
                yield

            def key(j, t):
                x, r = lt[2 * j:2 * j + 2]
                t = A.cp(x.ap[:], bank[j].ap[:], t, *x.free)
                bank[j].free = (t,)
                t = yield from headnorm(x.ap[:], t, K("kn2", 1 + j), 3)
                V.wait(*r.free)
                t = rope(r.ap[:], x.ap[:], TB("r16"), TB("cos"), TB("sin"), 3, t)
                x.free = (t,)
                y2[("k", j)] = [V.cp(kz[64 * g:64 * g + 64, 2 * j + g, :], r.ap[64 * g:64 * g + 64, :], t, t_kz) for g in range(2)]
                r.free = tuple(y2[("k", j)])

            def jobs():
                for c in range(4):
                    yield project(("q2", c), c % 3), lambda t, c=c: query(c, t)
                for j, (at, dst) in enumerate(((512, kc), (640, vc))):
                    yield project(("c2", at), j), lambda t, j=j, dst=dst: plain(j, dst, t)
                for j, at in enumerate((768, 1024)):
                    yield project(("c2", at), j), lambda t, j=j: key(j, t)

            yield from lagged(jobs())
            for b in range(4):
                PE.wait(*bank[b].free)
            for j in range(3):
                i = take(("v2", j))
                k0, k1 = 3 * j, min(8, 3 * j + 3)
                for b in range(4):
                    s = slice(128 * b, 128 * b + 128)
                    o = bank[b].ap[:, 0:280]
                    for k in range(k0, k1):
                        w = slice(280 * (k - k0), 280 * (k - k0) + 280)
                        PE.mm(o, hh[:, k, s], wh[i][:, w], k == 0, False)
                        PE.mm(o, hl[:, k, s], wh[i][:, w], False, False)
                        t = PE.mm(o, hh[:, k, s], wl[i][:, w], False, k == 7, signal=k == k1 - 1)
                    if j == 2:
                        t1 = A.cp(vt[:, b, :], o, t)
                        bank[b].free = (t1,)
                        t2 = A.act(gs[:, b, :], vt[:, b, 256:280], ACT.Tanh, 0.5, None, t1)
                        y2[("v", b)] = V.ts(gs[:, b, :], gs[:, b, :], 1.0, ALU.add, 0.5, ALU.mult, t2)
                        y2[("vt", b)] = t1
                done(i, t)
                yield

        def compress():
            s_kg = sem("s_kg")
            n_ph, n_kg = 16, 0
            t_ph = t_z = t_h = None
            for j, src in enumerate((kc, vc)):
                S.wait(y2[("c", j)], t_z)
                for g in range(2):
                    r = slice(64 * g, 64 * g + 64)
                    S.dma(kg[0:64, g, :], src[r, :], s_kg)
                    S.dma(kg[64:128, g, 0:T - 1], src[r, 1:T], s_kg)
                n_kg += 64
                yield
                yield
                pos = col[:, names[("posk", "posv")[j]][0]:names[("posk", "posv")[j]][1]]
                V.wait((s_kg, n_kg), t_h)
                for g in range(2):
                    for f in range(2):
                        view = kg[:, g, 16 * f:16 * f + 496].rearrange("p (n m) -> p m n", m=16)[:, 0:16:2, :]
                        t_z = V.tt(zt[:, 8 * f:8 * f + 8, 31 * g:31 * g + 31], view,
                                   pos[:, 8 * f:8 * f + 8].unsqueeze(2).broadcast_to([128, 8, 31]), ALU.add)
                b = bank[4]
                for f in range(2):
                    PE.wait(t_z, (s_ph, n_ph), *(b.free if f == 0 else ()))
                    for k in range(8):
                        t_ph = PE.mm(b.ap[0:62, 0:256], zt[:, 8 * f + k, :], ph[:, k, :], f == 0 and k == 0, f == 1 and k == 7, signal=k == 7)
                    jn, fn = (j, 1) if f == 0 else (j + 1, 0)
                    if jn < 2:
                        S.dma(ph[:], phi1[jn, :, 8 * fn:8 * fn + 8, :], s_ph, t_ph)
                        n_ph += 16
                    yield
                    yield
                t_h = t_ph
                t = A.cp(ge[0][:], b.ap[0:62, 0:256], t_ph)
                b.free = (t,)
                t1 = A.act(ge[1][:], ge[0][:], ACT.Square, 1.0, None, t)
                t1 = V.ts(ge[1][:], ge[1][:], 0.044715, ALU.mult, 1.0, ALU.add, t1)
                t1 = V.tt(ge[1][:], ge[1][:], ge[0][:], ALU.mult, t1, t)
                t1 = A.act(ge[1][:], ge[1][:], ACT.Tanh, 0.7978845608028654, None, t1)
                t1 = V.stt(ge[2][:], ge[1][:], 1.0, ge[0][:], ALU.add, ALU.mult, t1)
                yield
                b = bank[5]
                for f in range(2):
                    t = PE.tr(b.ap[:, 62 * f:62 * f + 62], ge[2][:, 128 * f:128 * f + 128], ident[0:62, 0:62], *((t1, *b.free) if f == 0 else ()), signal=f == 1)
                t = A.cp(hid[:].rearrange("p a b -> p (a b)"), b.ap[:, 0:124], t)
                b.free = (t,)
                yield
                PE.wait(t, (s_lw, 32), *bank[4].free)
                b = bank[4]
                if j == 0:
                    for g in range(2):
                        for f in range(2):
                            t = PE.mm(b.ap[64 * g:64 * g + 64, 0:31], p2[:, 0, f, :], hid[:, f, 31 * g:31 * g + 31], f == 0, f == 1, signal=f == 1)
                    x, r = ctiles(2)
                    t = A.act(x.ap[:, 0:31], b.ap[:, 0:31], ACT.Copy, 0.5, None, t, *x.free)
                    b.free = (t,)
                    t = yield from headnorm(x.ap[:, 0:31], t, K("kn2", 0), 5, 31, ctiles)
                    V.wait(*r.free)
                    t = rope(r.ap[:, 0:31], x.ap[:, 0:31], TB("r16"), TB("cosC"), TB("sinC"), 5, t, 31, ctiles)
                    x.free = (t,)
                    y2["kcz"] = [V.cp(kcz[64 * g:64 * g + 64, g, :], r.ap[64 * g:64 * g + 64, 0:31], t, t_kcz) for g in range(2)]
                    r.free = tuple(y2["kcz"])
                else:
                    for g in range(2):
                        for f in range(2):
                            t = PE.mm(b.ap[0:31, 64 * g:64 * g + 64], hid[:, f, 31 * g:31 * g + 31], p2[:, 1, f, :], f == 0, f == 1, signal=f == 1)
                    t = A.act(vcm[:].rearrange("p a b -> p (a b)"), b.ap[0:31, 0:128], ACT.Copy, 0.5, None, t)
                    b.free = (t,)
                    y2["vcm"] = t
                yield

        def nsa():
            cb = cau
            for _ in range(2):
                yield
            V.wait(*comp_read)
            A.wait(*comp_read)
            L0, t_c = {}, {}

            def compressed(b):
                qsl = slice(128 * b, 128 * b + 128)
                bk = bank[4]
                PE.wait(*bk.free, *y2["kcz"], *[y2[("q", c)] for c in range(4)])
                for h in range(8):
                    t = PE.mm(bk.ap[:, 31 * h:31 * h + 31], q2[:, h % 4, qsl], kcz[:, h // 4, :], True, True, signal=h == 7)
                s3 = sC[:, 0:248].rearrange("p (h n) -> p h n", h=8)
                mask = TB("maskC").rearrange("p (b n) -> p b n", b=4)[:, b, :].unsqueeze(1).broadcast_to([128, 8, 31])
                t = V.tt(s3, bk.ap[:, 0:248].rearrange("p (h n) -> p h n", h=8), mask, ALU.add, t, *L0.get("sC", ()))
                bk.free = (t,)
                mx, sm = stc[:, 0:8], stc[:, 8:16]
                t1 = V.do(lambda e, mx=mx, s3=s3: e.tensor_reduce(mx, s3, AXX, ALU.max), (t,))
                t = V.tt(s3, s3, mx.unsqueeze(2).broadcast_to([128, 8, 31]), ALU.subtract, t1)
                t = A.act(sC[:, 0:248], sC[:, 0:248], ACT.Exp, 0.125, None, t)
                yield
                t1 = V.do(lambda e, sm=sm, s3=s3: e.tensor_reduce(sm, s3, AXX, ALU.add), (t,))
                t1 = V.rec(sm, sm, t1)
                t1 = V.tt(sm, sm, gs[:, b, 0:8], ALU.mult, t1, y2[("v", b)])
                t1 = V.ts(sm, sm, TB("validC")[:, b:b + 1], ALU.mult, None, None, t1)
                t = V.tt(s3, s3, sm.unsqueeze(2).broadcast_to([128, 8, 31]), ALU.mult, t1, t)
                yield
                for f in range(2):
                    bk = bank[4 + f]
                    for h in range(4):
                        c0 = 31 * (4 * f + h)
                        t2 = PE.tr(bk.ap[0:31, 128 * h:128 * h + 128], sC[:, c0:c0 + 31], ident, *((t, *bk.free) if h == 0 else ()), signal=h == 3)
                    t_c[b] = A.cp(pC[:, 4 * f:4 * f + 4, :].rearrange("p a b -> p (a b)"), bk.ap[0:31, :], t2, *L0.get("pC", ()))
                    bk.free = (t_c[b],)
                L0["sC"] = (t2,)

            ob, b6 = bank[7], bank[6]
            u = [(b, h, j) for b in range(4) for h in range(8) for j in range(2)]
            t_sc, t_p = {}, {}
            comp_b = compressed(0)
            next(comp_b)
            yield
            next(comp_b)
            yield
            for n in range(len(u) + 5):
                if n >= 4 and n - 4 < len(u):
                    b, h, j = u[n - 4]
                    g, P = h // 4, Pn2[(n - 4) % 3]
                    o = ob.ap[:, 64 * h:64 * h + 64]
                    if j == 0:
                        PE.mm(o, pC[:, h, :], vcm[:, g, :], True, False, t_c[b], y2["vcm"], *(ob.free if h == 0 else ()), share=True)
                    PE.wait(t_p[n - 4], *[y2[("vt", i)] for i in range(b + 1)])
                    for i in range(b + 1):
                        t = PE.mm(o, P.ap[:, i, :], vt[:, i, 128 * j + 64 * g:128 * j + 64 * g + 64], False, j == 1 and i == b, signal=i == b, share=True)
                    P.free = (t,)
                    L0["pC"] = (t,)
                    if (h, j) == (7, 1):
                        yo, = tmps(1)
                        t_y = A.cp(yo.ap[:], ob.ap[:], t, *yo.free)
                        ob.free = (t_y,)
                if n >= 19 and (n - 19) % 16 == 1:
                    b = (n - 19) // 16
                    for c in range(4):
                        t1 = PE.tr(b6.ap[:, 128 * c:128 * c + 128], yo.ap[:, 128 * c:128 * c + 128], ident, *((t_y, *b6.free) if c == 0 else ()), signal=c == 3)
                    yo.free = (t1,)
                    y2[("o", b)] = A.cp(onT[:, :, 128 * b:128 * b + 128], b6.ap[:].rearrange("p (c t) -> p c t", c=4), t1)
                    b6.free = (y2[("o", b)],)
                if n % 16 == 3 and n < len(u):
                    next(comp_b, None)
                if n % 16 == 12 and n < 48:
                    comp_b = compressed(n // 16 + 1)
                    next(comp_b)
                if n % 16 == 14 and n < 48:
                    next(comp_b)
                if 2 <= n <= len(u) + 1:
                    b = u[n - 2][0]
                    bk, L, P = bank[4 + (n - 2) % 3], Ln2[(n - 2) % 3], Pn2[(n - 2) % 3]
                    for i in range(b + 1):
                        t = PE.tr(bk.ap[:, 128 * i:128 * i + 128], L.ap[:, 128 * i:128 * i + 128], ident, *((t_sc[n - 2], *bk.free) if i == 0 else ()), signal=i == b)
                    L.free = (t,)
                    t_p[n - 2] = A.cp(P.ap[:, 0:b + 1, :].rearrange("p a b -> p (a b)"), bk.ap[:, 0:128 * (b + 1)], t, *P.free)
                    bk.free = (t_p[n - 2],)
                if n < len(u):
                    b, h, j = u[n]
                    nk = 128 * (b + 1)
                    bk, L = bank[4 + n % 3], Ln2[n % 3]
                    m, w = stc[:, 16 + 2 * (n % 3):17 + 2 * (n % 3)], stc[:, 17 + 2 * (n % 3):18 + 2 * (n % 3)]
                    t = PE.mm(bk.ap[:, 0:nk], q2[:, h % 4, 128 * b:128 * b + 128], kz[:, 2 * j + h // 4, 0:nk], True, True, *bk.free, *y2[("k", j)], signal=True)
                    t = V.addred(L.ap[:, 0:nk], bk.ap[:, 0:nk], cb[:, 384 - 128 * b:512], -0.125, 3.0e38, ALU.min, m, t, (s_lw, 32), *L.free)
                    bk.free = (t,)
                    t = A.act(L.ap[:, 0:nk], L.ap[:, 0:nk], ACT.Exp, -1.0, m, t, acc=w)
                    t1 = V.rec(w, w, t)
                    t1 = V.tt(w, w, gs[:, b, 8 * (j + 1) + h:8 * (j + 1) + h + 1], ALU.mult, t1)
                    t_sc[n] = V.ts(L.ap[:, 0:nk], L.ap[:, 0:nk], w, ALU.mult, None, None, t1, t)
                yield

        def lru():
            xcs = [lt[0], Slot(nacc)]
            gy = Slot(nr)
            rr, ii, aa = lt[1:]
            for s in xcs + [gy, rr, ii, aa]:
                V.wait(*s.free)
                A.wait(*s.free)
                s.free = ()

            def recurrence(c, xc, t, t_xc, gelu):
                g1, g2, t6, t7 = gelu
                t7 = A.act(g2.ap[:], g2.ap[:], ACT.Tanh, 0.7978845608028654, None, t7)
                t7 = V.stt(gy.ap[:], g2.ap[:], 1.0, g1.ap[:], ALU.add, ALU.mult, t7, t6, *gy.free)
                g1.free = g2.free = (t7,)
                y2[("gy", c)] = (t7,)
                t1 = A.act(rr.ap[:], bank[2].ap[:], ACT.Tanh, 0.5, lc[:, 16 + c:17 + c], t, *t_lc, *rr.free)
                bank[2].free = (t1,)
                t2 = A.act(ii.ap[:], bank[3].ap[:], ACT.Tanh, 0.5, lc[:, 24 + c:25 + c], t, *ii.free)
                bank[3].free = (t2,)
                t2 = V.stt(ii.ap[:], ii.ap[:], 1.0, xc.ap[:], ALU.add, ALU.mult, t2, t_xc)
                t3 = A.act(aa.ap[:], rr.ap[:], ACT.Exp, lc[:, c:c + 1], lc[:, c:c + 1], t1, *aa.free)
                yield
                t4 = A.act(rr.ap[:], rr.ap[:], ACT.Tanh, lc[:, 8 + c:9 + c], lc[:, 8 + c:9 + c], t1, t3)
                t5 = A.act(xc.ap[:], aa.ap[:], ACT.Square, 1.0, None, t3, t2, t)
                t5 = V.stt(rr.ap[:], xc.ap[:], 1.0, rr.ap[:], ALU.add, ALU.mult, t5, t4)
                t5 = V.ts(rr.ap[:], rr.ap[:], 1e-18, ALU.max, None, None, t5)
                yield
                t5 = A.act(rr.ap[:], rr.ap[:], ACT.Ln, 1.0, None, t5)
                t5 = A.act(rr.ap[:], rr.ap[:], ACT.Exp, 0.5, None, t5)
                t5 = V.stt(ii.ap[:], ii.ap[:], 0.5, rr.ap[:], ALU.mult, ALU.mult, t5, t2)
                rr.free = (t5,)
                t8 = V.scan(xc.ap[:], aa.ap[:], ii.ap[:], 0.0, t5, t3)
                aa.free = ii.free = (t8,)
                t8 = V.stt(xc.ap[:], xc.ap[:], 0.5, gy.ap[:], ALU.mult, ALU.mult, t8, *y2[("gy", c)])
                gy.free = (t8,)
                th = G.cp(oh[:, c, :], xc.ap[:], t8)
                tl = G.tt(ol[:, c, :], xc.ap[:], oh[:, c, :].bitcast(F32), ALU.subtract, t8, th)
                xc.free = (th, tl)
                y2[("lru", c)] = (th, tl)
                yield

            def step(gen):
                next(gen, None)

            prev = iter(())
            for c in range(8):
                p = project(("c2", 1304 + 128 * c), 0)
                next(p)
                step(prev)
                yield
                for _ in p:
                    pass
                xc = xcs[c % 2]
                V.wait(*xc.free)
                A.wait(*xc.free)
                t_xc = conv(bank[0], PE.last(), "conv2", c, xc.ap[:], bias=K("convb", c))
                p = project(("c2", 2328 + 128 * c), 1)
                yield
                next(p)
                step(prev)
                yield
                for _ in p:
                    pass
                g1, g2 = tmps(2)
                t6 = A.cp(g1.ap[:], bank[1].ap[:], PE.last(), *g1.free)
                bank[1].free = (t6,)
                w = lw[c % 2]
                PE.mm(bank[2].ap[:], w.ap[:, 0, :], xc.ap[:], True, True, t_xc, (s_lr[c % 2], 16 * (c // 2 + 1)), *bank[2].free)
                t = PE.mm(bank[3].ap[:], w.ap[:, 1, :], xc.ap[:], True, True, *bank[3].free, signal=True)
                if c + 2 < 8:
                    S.dma(w.ap[:], lruw[:, :, c + 2, :], s_lr[c % 2], t)
                t7 = A.act(g2.ap[:], g1.ap[:], ACT.Square, 1.0, None, t6, *g2.free)
                t7 = V.ts(g2.ap[:], g2.ap[:], 0.044715, ALU.mult, 1.0, ALU.add, t7)
                t7 = V.tt(g2.ap[:], g2.ap[:], g1.ap[:], ALU.mult, t7, t6)
                step(prev)
                prev = recurrence(c, xc, t, t_xc, (g1, g2, t6, t7))
                yield
            for _ in prev:
                yield

        def merge2():
            for m in range(8):
                t = yield from project(("c2", 4376 + 128 * m), m % 2)
                g, = tmps(1)
                tg = A.act(g.ap[:], bank[m % 2].ap[:], ACT.Tanh, 0.5, None, t, *g.free)
                bank[m % 2].free = (tg,)
                pb = 2 + m % 2
                t = yield from project(("lup", m), pb, oh, ol, [y2[("lru", c)] for c in range(8)])
                y2[("acc", m)] = V.stt(acc[:, m, :], g.ap[:], 1.0, bank[pb].ap[:], ALU.add, ALU.mult, tg, t)
                g.free = bank[pb].free = (y2[("acc", m)],)
                yield

        def merge3():
            out = []
            for c in range(4):
                out += pair(yh2[:, c, :], yl2[:, c, :], onT[:, c, :], y2[("o", 3)])
            for m in range(8):
                if m % 2 == 0:
                    ib = take(("nup", m // 2))
                    for j in range(2):
                        PE.wait(*bank[j].free)
                        for k in range(4):
                            PE.wait(*out[2 * k:2 * k + 2])
                            w = slice(512 * j + 128 * k, 512 * j + 128 * k + 128)
                            t = prod3(bank[j].ap[:], ib, w, yh2[:, k, :], yl2[:, k, :], k == 0, k == 3)
                        y2[("pb", j)] = t
                    done(ib, t)
                if m < 6:
                    g, tg = kept[m]
                else:
                    gb = 2 + m % 2
                    t = yield from project(("c2", 3352 + 128 * m), gb)
                    g, = tmps(1)
                    tg = A.act(g.ap[:], bank[gb].ap[:], ACT.Tanh, 0.5, None, t, *g.free)
                    bank[gb].free = (tg,)
                pb = bank[m % 2]
                ta = V.stt(g.ap[:], g.ap[:], 1.0, pb.ap[:], ALU.add, ALU.mult, tg, y2[("pb", m % 2)])
                pb.free = (ta,)
                ta = V.tt(acc[:, m, :], acc[:, m, :], g.ap[:], ALU.add, ta, y2[("acc", m)])
                g.free = (ta,)
                y2[("acc", m)] = ta

        for _ in proj2():
            pass
        weave(lru(), (compress(), RATES[4]))
        comp_read = fence()
        comp.close()
        m3 = ExitStack()
        acc = sb("acc_2", [128, 8, T], stack=m3)
        Ln2 = [Slot(sb(f"Ln{i}", [128, T], stack=m3)) for i in range(3)]
        Pn2 = [Slot(sb(f"Pn{i}", [128, 4, 128], stack=m3)) for i in range(2)]
        Pn2.append(Slot(tabs[:, bpack.n:bpack.n + T].rearrange("p (a b) -> p a b", a=4)))
        sC = sb("sC", [128, 256], stack=m3)
        pC = sb("pC", [31, 8, 128], stack=m3)
        stc = sb("stc", [128, 32], stack=m3)
        yh2, yl2 = oh[:, 0:4, :], ol[:, 0:4, :]

        kept = []
        V.wait(comp_read[0])

        def mains():
            yield from merge2()
            for m, g in enumerate(lt + [Slot(nacc), Slot(nr)]):
                t = yield from project(("c2", 3352 + 128 * m), m % 2)
                t = A.act(g.ap[:], bank[m % 2].ap[:], ACT.Tanh, 0.5, None, t, *g.free, *(y2[("lru", 7)] + y2[("gy", 7)]), V.last())
                bank[m % 2].free = (t,)
                kept.append((g, t))
                yield

        weave(mains(), (nsa(), RATES[3]))
        t_pe = PE.last()
        A.wait(t_pe)
        V.wait(t_pe)
        for _ in merge3():
            pass
        t_h = PE.last()
        for m in range(8):
            halve(acc, m, y2[("acc", m)], t_h)
        last = fence()
        m3.close()
        b2.close()
        xt = sb("xt_2", [128, 8, T])
        S.wait(*last)
        xn[0] += 16
        S.dma(xt[:], x_src, s_x)
        x_toks = []
        for m in range(8):
            for _ in project(("o2", m), m % 4):
                pass
            tx = V.tt(xt[:, m, :], xt[:, m, :], bank[m % 4].ap[:], ALU.add, PE.last(), (s_x, xn[0]))
            bank[m % 4].free = (tx,)
            x_toks.append(tx)
            square(xt, m, tx)
        norm_into_h(xt, "nrmB")
        fh, fl = sb("fh", [128, 16, T], F32R), sb("fl", [128, 16, T], F32R)
        s_o = sem("s_out")
        for half in range(2):
            ft = []
            t_f2 = PE.last()
            for j in range(16):
                for _ in project(("f1", 16 * half + j), j % 4):
                    pass
                r, = tmps(1)
                t = A.act(r.ap[:], bank[j % 4].ap[:], ACT.Relu, 1.0, None, PE.last(), *r.free)
                bank[j % 4].free = (t,)
                t = V.tt(r.ap[:], r.ap[:], r.ap[:], ALU.mult, t)
                th = A.cp(fh[:, j, :], r.ap[:], t, t_f2 if half else None)
                tl = V.tt(fl[:, j, :], r.ap[:], fh[:, j, :].bitcast(F32), ALU.subtract, t, th, t_f2 if half else None)
                r.free = (th, tl)
                ft += [th, tl]
            PE.wait(*ft)
            for m in range(8):
                b = bank[m % 4]
                PE.wait(*b.free)
                for jj in range(2):
                    i = take(("f2", 2 * half + jj, m))
                    for k in range(8):
                        t = prod3(b.ap[:], i, slice(128 * k, 128 * k + 128), fh[:, 8 * jj + k, :], fl[:, 8 * jj + k, :],
                                  jj == 0 and k == 0, jj == 1 and k == 7, signal=k == 7)
                    done(i, t)
                tx = V.tt(xt[:, m, :], xt[:, m, :], b.ap[:], ALU.add, t, x_toks[m])
                b.free = (tx,)
                x_toks[m] = tx
                if half == 1:
                    A.dma(x_out[:, m, :], xt[:, m, :], s_o, tx)
        A.wait((s_o, 16 * 8))
        block = ctx.enter_context(nc.Block())

        @block.sync
        def _(e):
            S.play(e)

        @block.tensor
        def _(e):
            PE.play(e)

        @block.vector
        def _(e):
            V.play(e)

        @block.scalar
        def _(e):
            A.play(e)

        @block.gpsimd
        def _(e):
            G.play(e)


def layouts(I):
    x = np.ascontiguousarray(I["x"][0].reshape(T, 8, 128).transpose(2, 1, 0))
    cpack, apack, bpack = constants(), tables_a(), tables_b()
    return {
        "x": x, "units": pack_units(I), "consts": cpack.array(), "tabA": apack.array(), "tabB": bpack.array(),
        "cols": pack_columns(I), "poolw": np.ascontiguousarray(I["pool_w"].transpose(0, 2, 1, 3)),
        "lruw": np.ascontiguousarray(np.stack([I["lru_wa_2"][0], I["lru_wx_2"][0]]).transpose(2, 0, 1, 3)),
        "phi1": np.ascontiguousarray(np.stack([I["phi_k_w1_2"][0], I["phi_v_w1_2"][0]]).reshape(2, 16, 128, 256).transpose(0, 2, 1, 3)),
        "phi2": np.ascontiguousarray(np.stack([I["phi_k_w2_2"][0], I["phi_v_w2_2"][0]]).reshape(2, 2, 128, 64).transpose(2, 0, 1, 3)),
    }, cpack, apack, bpack


def make(nc, arrays, packs):
    ap = {n: nc.dram_tensor(n, list(a.shape), F32, kind="ExternalInput").ap() for n, a in arrays.items()}
    out = nc.dram_tensor("out", [128, 8, T], F32, kind="ExternalOutput").ap()
    build(nc, ap["units"], ap["consts"], ap["tabA"], ap["tabB"], ap["cols"], ap["poolw"], ap["lruw"], ap["phi1"],
          ap["phi2"], ap["x"], out, *packs)


def kernel(**inputs):
    from concourse import bacc
    from concourse.bass_utils import run_bass_kernel_spmd

    arrays, *packs = layouts({k: np.asarray(v) for k, v in inputs.items()})
    nc = bacc.Bacc("TRN2", target_bir_lowering=False, num_devices=1)
    make(nc, arrays, packs)
    r = run_bass_kernel_spmd(nc, [arrays], core_ids=[0])
    y = np.asarray(r.results[0]["out"])
    return np.ascontiguousarray(y.transpose(2, 1, 0).reshape(1, T, D))
```
